# Optimizing a Trainium2 kernel written in Bass

```python
import jax, jax.numpy as jnp
from jax import lax
import numpy as np
import math
import jax
import jax.numpy as jnp

D_MODEL = 1024
BATCH = 1
SEQ = 256
DEPTH = 1

HEAD_DIM = 64
N_SWA_HEADS = 8
N_SWA_KV = 2
WINDOW = 128
BLOCK = 128
N_DSA_HEADS = 4
N_IDX_HEADS = 4
IDX_DIM = 64
TOPK_MAX = 256
N_MEM_HEADS = 4
MEM_LEN = 256
N_BRANCH = 3
D_FF = 4 * D_MODEL
ROPE_THETA = 10000.0
EPS = 1e-6

SWA_WIDTH = N_SWA_HEADS * HEAD_DIM
SWA_KV_WIDTH = N_SWA_KV * HEAD_DIM
DSA_WIDTH = N_DSA_HEADS * HEAD_DIM
MEM_WIDTH = N_MEM_HEADS * HEAD_DIM
IN_SPLITS = (SWA_WIDTH, SWA_KV_WIDTH, SWA_KV_WIDTH,
             DSA_WIDTH, HEAD_DIM, HEAD_DIM,
             N_IDX_HEADS * IDX_DIM, IDX_DIM, N_IDX_HEADS,
             MEM_WIDTH, N_BRANCH * D_MODEL)
D_IN = sum(IN_SPLITS)


def rmsnorm(x, g):
    xf = x.astype(jnp.float32)
    y = xf * lax.rsqrt(jnp.mean(xf * xf, axis=-1, keepdims=True) + EPS)
    return (y * g.astype(jnp.float32)).astype(x.dtype)

def rope(x, pos):
    half = x.shape[-1] // 2
    inv_freq = jnp.power(ROPE_THETA, -jnp.arange(half, dtype=jnp.float32) / half)
    ang = pos.astype(jnp.float32)[..., None] * inv_freq
    cos = jnp.cos(ang)[:, :, None, :].astype(x.dtype)
    sin = jnp.sin(ang)[:, :, None, :].astype(x.dtype)
    x1, x2 = x[..., :half], x[..., half:]
    return jnp.concatenate([x1 * cos - x2 * sin, x2 * cos + x1 * sin], axis=-1)

def sliding_window_attention(q, k, v, sinks):
    B, S, Hq, D = q.shape
    Hkv = k.shape[2]
    G = Hq // Hkv
    nb = S // BLOCK
    qb = q.reshape(B, nb, BLOCK, Hkv, G, D)

    def with_prev(t):
        tb = t.reshape(B, nb, BLOCK, Hkv, D)
        prev = jnp.concatenate([jnp.zeros_like(tb[:, :1]), tb[:, :-1]], axis=1)
        return jnp.concatenate([prev, tb], axis=2)

    kw, vw = with_prev(k), with_prev(v)
    scores = jnp.einsum("bnqkgd,bnskd->bnkgqs", qb, kw).astype(jnp.float32) * (D ** -0.5)
    qi = jnp.arange(BLOCK)[:, None]
    sj = jnp.arange(2 * BLOCK)[None, :]
    dist = qi + BLOCK - sj
    blk = jnp.arange(nb)[:, None, None]
    valid = (dist >= 0) & (dist < WINDOW) & ((blk > 0) | (sj >= BLOCK))
    scores = jnp.where(valid[None, :, None, None], scores, -jnp.inf)
    sink = jnp.broadcast_to(
        sinks.reshape(Hkv, G)[None, None, :, :, None, None].astype(jnp.float32),
        scores.shape[:-1] + (1,))
    probs = jax.nn.softmax(jnp.concatenate([scores, sink], axis=-1), axis=-1)[..., :-1]
    out = jnp.einsum("bnkgqs,bnskd->bnqkgd", probs.astype(vw.dtype), vw)
    return out.reshape(B, S, Hq * D)

def dsa_attention(q, k, v, q_idx, k_idx, w_idx):
    B, S = q.shape[:2]
    nb = S // BLOCK
    top_k = min(TOPK_MAX, S // 4)
    key_pos = jnp.arange(S)
    gather = jax.vmap(lambda t, i: t[i])

    def to_blocks(t):
        return jnp.moveaxis(t.reshape((B, nb, BLOCK) + t.shape[2:]), 1, 0)

    def block_fn(args):
        qb, qib, wb, blk = args
        qpos = blk * BLOCK + jnp.arange(BLOCK)
        rel = jax.nn.relu(jnp.einsum("bqhd,bsd->bqhs", qib, k_idx).astype(jnp.float32))
        iscore = jnp.einsum("bqhs,bqh->bqs", rel, wb.astype(jnp.float32))
        iscore = jnp.where(key_pos[None, None, :] <= qpos[None, :, None], iscore, -jnp.inf)
        _, sel = lax.top_k(iscore, top_k)
        kg = gather(k, sel)
        vg = gather(v, sel)
        s = jnp.einsum("bqhd,bqkd->bhqk", qb, kg).astype(jnp.float32) * (HEAD_DIM ** -0.5)
        s = jnp.where((sel <= qpos[None, :, None])[:, None], s, -jnp.inf)
        p = jax.nn.softmax(s, axis=-1)
        return jnp.einsum("bhqk,bqkd->bqhd", p.astype(vg.dtype), vg)

    out = lax.map(block_fn, (to_blocks(q), to_blocks(q_idx), to_blocks(w_idx), jnp.arange(nb)))
    return jnp.moveaxis(out, 0, 1).reshape(B, S, -1)

def memory_cross_attention(q, mem_k, mem_v):
    B, S = q.shape[:2]
    s = jnp.einsum("bqhd,bmhd->bhqm", q, mem_k).astype(jnp.float32) * (HEAD_DIM ** -0.5)
    p = jax.nn.softmax(s, axis=-1)
    return jnp.einsum("bhqm,bmhd->bqhd", p.astype(mem_v.dtype), mem_v).reshape(B, S, -1)

def first_inputs(seed: int = 0) -> dict:
    key = jax.random.key(seed)
    ks = jax.random.split(key, 20)
    f32 = jnp.float32

    def nrm(k, shape, scale):
        return jax.random.normal(k, shape, f32) * scale

    def gain(k, shape):
        return 1.0 + 0.02 * jax.random.normal(k, shape, f32)

    return {
        "x": nrm(ks[0], (BATCH, SEQ, D_MODEL), 1.0),
        "mem": nrm(ks[1], (BATCH, MEM_LEN, D_MODEL), 1.0),
        "positions": jnp.broadcast_to(jnp.arange(SEQ, dtype=jnp.int32)[None], (BATCH, SEQ)),
        "g_mix": gain(ks[2], (DEPTH, D_MODEL)),
        "w_in": nrm(ks[3], (DEPTH, D_MODEL, D_IN), D_MODEL ** -0.5),
        "b_gate": nrm(ks[4], (DEPTH, N_BRANCH * D_MODEL), 0.01),
        "sinks": nrm(ks[5], (DEPTH, N_SWA_HEADS), 0.5),
        "g_mem": gain(ks[6], (DEPTH, D_MODEL)),
        "w_mem_kv": nrm(ks[7], (DEPTH, D_MODEL, 2 * MEM_WIDTH), D_MODEL ** -0.5),
        "w_proj_swa": nrm(ks[8], (DEPTH, SWA_WIDTH, D_MODEL), SWA_WIDTH ** -0.5),
        "w_proj_dsa": nrm(ks[9], (DEPTH, DSA_WIDTH, D_MODEL), DSA_WIDTH ** -0.5),
        "w_proj_mem": nrm(ks[10], (DEPTH, MEM_WIDTH, D_MODEL), MEM_WIDTH ** -0.5),
        "w_out": nrm(ks[11], (DEPTH, D_MODEL, D_MODEL), D_MODEL ** -0.5),
        "g_mlp": gain(ks[12], (DEPTH, D_MODEL)),
        "w_mlp_in": nrm(ks[13], (DEPTH, D_MODEL, D_FF), D_MODEL ** -0.5),
        "w_mlp_out": nrm(ks[14], (DEPTH, D_FF, D_MODEL), D_FF ** -0.5),
        "g_final": gain(ks[15], (D_MODEL,)),
    }

def first_block(x, mem, positions, g_mix, w_in, b_gate, sinks, g_mem, w_mem_kv,
              w_proj_swa, w_proj_dsa, w_proj_mem, w_out, g_mlp, w_mlp_in, w_mlp_out,
              g_final):
    B, S, _ = x.shape
    M = mem.shape[1]
    split_points = np.cumsum(IN_SPLITS)[:-1].tolist()
    idx_scale = (N_IDX_HEADS ** -0.5) * (IDX_DIM ** -0.5)
    for l in range(DEPTH):
        h = rmsnorm(x, g_mix[l])
        proj = jnp.einsum("bsd,de->bse", h, w_in[l])
        (q_s, k_s, v_s, q_d, k_d, v_d, q_i, k_i, w_i, q_m, gate_logits) = jnp.split(
            proj, split_points, axis=-1)

        q_s = rope(q_s.reshape(B, S, N_SWA_HEADS, HEAD_DIM), positions)
        k_s = rope(k_s.reshape(B, S, N_SWA_KV, HEAD_DIM), positions)
        v_s = v_s.reshape(B, S, N_SWA_KV, HEAD_DIM)
        o_swa = sliding_window_attention(q_s, k_s, v_s, sinks[l])

        q_d = rope(q_d.reshape(B, S, N_DSA_HEADS, HEAD_DIM), positions)
        k_d = rope(k_d[:, :, None, :], positions)[:, :, 0]
        q_i = rope(q_i.reshape(B, S, N_IDX_HEADS, IDX_DIM), positions)
        k_i = rope(k_i[:, :, None, :], positions)[:, :, 0]
        o_dsa = dsa_attention(q_d, k_d, v_d, q_i, k_i, w_i * idx_scale)

        m = rmsnorm(mem, g_mem[l])
        mkv = jnp.einsum("bmd,de->bme", m, w_mem_kv[l]).reshape(B, M, 2, N_MEM_HEADS, HEAD_DIM)
        o_mem = memory_cross_attention(q_m.reshape(B, S, N_MEM_HEADS, HEAD_DIM),
                                       mkv[:, :, 0], mkv[:, :, 1])

        gates = jax.nn.sigmoid(gate_logits + b_gate[l]).reshape(B, S, N_BRANCH, D_MODEL)
        merged = (gates[:, :, 0] * jnp.einsum("bse,ed->bsd", o_swa, w_proj_swa[l])
                  + gates[:, :, 1] * jnp.einsum("bse,ed->bsd", o_dsa, w_proj_dsa[l])
                  + gates[:, :, 2] * jnp.einsum("bse,ed->bsd", o_mem, w_proj_mem[l]))
        x = x + jnp.einsum("bsd,de->bse", merged, w_out[l])

        h = rmsnorm(x, g_mlp[l])
        hid = jnp.square(jax.nn.relu(jnp.einsum("bsd,df->bsf", h, w_mlp_in[l])))
        x = x + jnp.einsum("bsf,fd->bsd", hid, w_mlp_out[l])
    return rmsnorm(x, g_final)


DEPTH_2 = 2

N_A_LAYERS = DEPTH_2 // 2
N_B_LAYERS = DEPTH_2 - N_A_LAYERS
DN_ALPHA = (2.0 * DEPTH_2) ** 0.25
DN_BETA = (8.0 * DEPTH_2) ** -0.25
LN_EPS = 1e-5
FFN_DIM = int(math.ceil(8 * D_MODEL / 3 / 256)) * 256
SGU_HIDDEN = 4 * D_MODEL
SGU_HALF = SGU_HIDDEN // 2
SGU_GROUPS = 8
SGU_GROUP_DIM = SGU_HALF // SGU_GROUPS
SGU_CHUNK = 128
N_HEADS = 16
N_KV_GROUPS = 4
HEADS_PER_GROUP = N_HEADS // N_KV_GROUPS
HEAD_DIM_2 = D_MODEL // N_HEADS
CMP_LEN = 32
CMP_STRIDE = 16
PHI_HIDDEN = 256
SEL_LEN = 64
SEL_TOP_N = 8
N_LOCAL_BLOCKS = 2
WINDOW_2 = 512
NSA_Q_BLOCK = 32
N_KV_SLOTS = 6
REL_BUCKETS = 32
REL_MAX_DIST = 128
NEG = -1e30


def layer_norm(x, g, b):
    xf = x.astype(jnp.float32)
    mu = jnp.mean(xf, axis=-1, keepdims=True)
    var = jnp.mean(jnp.square(xf - mu), axis=-1, keepdims=True)
    y = (xf - mu) * lax.rsqrt(var + LN_EPS)
    return (y * g.astype(jnp.float32) + b.astype(jnp.float32)).astype(x.dtype)

def post_norm(x, sub, g, b):
    return layer_norm(DN_ALPHA * x + sub, g, b)

def swiglu(x, w1, w3, w2):
    return (jax.nn.silu(x @ w1) * (x @ w3)) @ w2

def rel_bucket(dist):
    n = jnp.maximum(dist, 0)
    max_exact = REL_BUCKETS // 2
    nf = jnp.maximum(n, 1).astype(jnp.float32)
    large = max_exact + (jnp.log(nf / max_exact) / math.log(REL_MAX_DIST / max_exact)
                         * (REL_BUCKETS - max_exact)).astype(jnp.int32)
    return jnp.where(n < max_exact, n, jnp.minimum(large, REL_BUCKETS - 1))

def chunked_sgu_mixer(x, w_in, ln_g, ln_b, w_s, b_s, w_out):
    B, S, _ = x.shape
    z = jax.nn.gelu(x @ w_in, approximate=False)
    u, v = jnp.split(z, 2, axis=-1)
    v = layer_norm(v, ln_g, ln_b)
    n_chunks = S // SGU_CHUNK
    v = v.reshape(B, n_chunks, SGU_CHUNK, SGU_GROUPS, SGU_GROUP_DIM)
    causal = jnp.tril(jnp.ones((SGU_CHUNK, SGU_CHUNK), dtype=bool))
    w = jnp.where(causal[None], w_s, jnp.zeros_like(w_s))
    mixed = jnp.einsum('gts,bnsgc->bntgc', w, v) + b_s.T[None, None, :, :, None]
    return (u * mixed.reshape(B, S, SGU_HALF)) @ w_out

def compress(kv, pe, w1, b1, w2):
    B, S, G, Dh = kv.shape
    n_sub = CMP_LEN // CMP_STRIDE
    n_chunks = S // CMP_STRIDE
    n_cmp = n_chunks - n_sub + 1
    chunks = kv.reshape(B, n_chunks, CMP_STRIDE, G, Dh)
    blocks = jnp.concatenate([chunks[:, i:i + n_cmp] for i in range(n_sub)], axis=2)
    blocks = blocks + pe[None, None, :, None, :]
    flat = blocks.transpose(0, 1, 3, 2, 4).reshape(B, n_cmp, G, CMP_LEN * Dh)
    return jax.nn.gelu(flat @ w1 + b1, approximate=False) @ w2

def nsa_shared_kv(h, kv_w, cmp_pe, cmp_w1, cmp_b1, cmp_w2):
    B, S, _ = h.shape
    kv = (h @ kv_w).reshape(B, S, N_KV_SLOTS, N_KV_GROUPS, HEAD_DIM_2)
    k_cmp = compress(kv[:, :, 0], cmp_pe[0], cmp_w1[0], cmp_b1[0], cmp_w2[0])
    v_cmp = compress(kv[:, :, 1], cmp_pe[1], cmp_w1[1], cmp_b1[1], cmp_w2[1])
    n_sel = S // SEL_LEN
    k_sel = kv[:, :, 2].reshape(B, n_sel, SEL_LEN, N_KV_GROUPS, HEAD_DIM_2).transpose(0, 3, 1, 2, 4)
    v_sel = kv[:, :, 3].reshape(B, n_sel, SEL_LEN, N_KV_GROUPS, HEAD_DIM_2).transpose(0, 3, 1, 2, 4)
    pad = ((0, 0), (WINDOW_2, 0), (0, 0), (0, 0))
    k_win = jnp.pad(kv[:, :, 4], pad)
    v_win = jnp.pad(kv[:, :, 5], pad)
    return (k_cmp, v_cmp, k_sel, v_sel, k_win, v_win)

def masked_softmax(s, mask):
    p = jax.nn.softmax(jnp.where(mask, s, NEG), axis=-1)
    return jnp.where(mask, p, 0.0)

def cmp_to_sel_overlap(n_cmp, n_sel):
    i = np.arange(n_cmp)[:, None]
    j = np.arange(n_sel)[None, :]
    ov = (i * CMP_STRIDE < (j + 1) * SEL_LEN) & (i * CMP_STRIDE + CMP_LEN > j * SEL_LEN)
    return ov.astype(np.float32)

def nsa_mixer(h, shared, w_qg, w_o, rel_table):
    k_cmp, v_cmp, k_sel, v_sel, k_win, v_win = shared
    B, S, _ = h.shape
    G, HG, Dh, QB = N_KV_GROUPS, HEADS_PER_GROUP, HEAD_DIM_2, NSA_Q_BLOCK
    qg = h @ w_qg
    q = qg[..., :N_HEADS * Dh].reshape(B, S, G, HG, Dh) * (Dh ** -0.5)
    gates = jax.nn.sigmoid(qg[..., N_HEADS * Dh:]).reshape(B, S, G, HG, 3)
    n_qb = S // QB
    n_cmp = k_cmp.shape[1]
    n_sel = k_sel.shape[2]
    n_top = min(SEL_TOP_N, n_sel)
    overlap = jnp.asarray(cmp_to_sel_overlap(n_cmp, n_sel))
    cmp_end = jnp.arange(n_cmp, dtype=jnp.int32) * CMP_STRIDE + (CMP_LEN - 1)
    sel_ids = jnp.arange(n_sel, dtype=jnp.int32)
    b_idx = jnp.arange(B)[:, None, None]
    g_idx = jnp.arange(G)[None, :, None]
    g_idx4 = jnp.arange(G)[None, :, None, None]
    tbl_g = rel_table.reshape(REL_BUCKETS, G, HG)

    def head_bias(dist):
        return rel_table[rel_bucket(dist)].reshape(dist.shape + (G, HG)).transpose(2, 3, 0, 1).astype(jnp.float32)

    def block(args):
        q_b, g_b, q0 = args
        t = q0 + jnp.arange(QB, dtype=jnp.int32)
        dist_c = t[:, None] - cmp_end[None, :]
        mask_c = dist_c >= 0
        s_c = jnp.einsum('bqghd,bngd->bghqn', q_b, k_cmp).astype(jnp.float32) + head_bias(dist_c)
        p_c = masked_softmax(s_c, mask_c)
        o_c = jnp.einsum('bghqn,bngd->bqghd', p_c.astype(v_cmp.dtype), v_cmp)
        imp = jnp.einsum('bghqn,nj->bgqj', p_c, overlap)
        cur = t // SEL_LEN
        valid = sel_ids[None, :] <= cur[:, None]
        forced = valid & ((sel_ids[None, :] == 0) | (sel_ids[None, :] > cur[:, None] - N_LOCAL_BLOCKS))
        imp = jnp.where(forced, -NEG, jnp.where(valid, imp, NEG))
        _, idx = lax.top_k(imp, n_top)
        flat = idx.reshape(B, G, QB * n_top)
        k_g = k_sel[b_idx, g_idx, flat].reshape(B, G, QB, n_top * SEL_LEN, Dh)
        v_g = v_sel[b_idx, g_idx, flat].reshape(B, G, QB, n_top * SEL_LEN, Dh)
        pos = (idx[..., None] * SEL_LEN + jnp.arange(SEL_LEN, dtype=jnp.int32)).reshape(B, G, QB, n_top * SEL_LEN)
        dist_s = t[None, None, :, None] - pos
        mask_s = (dist_s >= 0)[:, :, None]
        bias_s = tbl_g[rel_bucket(dist_s), g_idx4].transpose(0, 1, 4, 2, 3).astype(jnp.float32)
        s_s = jnp.einsum('bqghd,bgqkd->bghqk', q_b, k_g).astype(jnp.float32) + bias_s
        p_s = masked_softmax(s_s, mask_s)
        o_s = jnp.einsum('bghqk,bgqkd->bqghd', p_s.astype(v_g.dtype), v_g)
        k_w = lax.dynamic_slice_in_dim(k_win, q0, WINDOW_2 + QB, axis=1)
        v_w = lax.dynamic_slice_in_dim(v_win, q0, WINDOW_2 + QB, axis=1)
        pos_w = q0 - WINDOW_2 + jnp.arange(WINDOW_2 + QB, dtype=jnp.int32)
        dist_w = t[:, None] - pos_w[None, :]
        mask_w = (dist_w >= 0) & (dist_w < WINDOW_2) & (pos_w[None, :] >= 0)
        s_w = jnp.einsum('bqghd,bkgd->bghqk', q_b, k_w).astype(jnp.float32) + head_bias(dist_w)
        p_w = masked_softmax(s_w, mask_w)
        o_w = jnp.einsum('bghqk,bkgd->bqghd', p_w.astype(v_w.dtype), v_w)
        return g_b[..., 0:1] * o_c + g_b[..., 1:2] * o_s + g_b[..., 2:3] * o_w

    q_blocks = q.reshape(B, n_qb, QB, G, HG, Dh).swapaxes(0, 1)
    g_blocks = gates.reshape(B, n_qb, QB, G, HG, 3).swapaxes(0, 1)
    starts = jnp.arange(n_qb, dtype=jnp.int32) * QB
    out = lax.map(block, (q_blocks, g_blocks, starts))
    out = out.swapaxes(0, 1).reshape(B, S, N_HEADS * Dh)
    return out @ w_o

def second_inputs(seed: int = 0) -> dict:
    key = jax.random.key(seed)
    ks = jax.random.split(key, 24)
    f32 = jnp.float32

    def nrm(k, shape, scale):
        return jax.random.normal(k, shape, f32) * scale

    kv_scale = jnp.array([1.0, DN_BETA, 1.0, DN_BETA, 1.0, DN_BETA], f32)[None, :, None]
    kv_w = (nrm(ks[13], (D_MODEL, N_KV_SLOTS, N_KV_GROUPS * HEAD_DIM_2), D_MODEL ** -0.5) * kv_scale)
    return {
        'x': nrm(ks[0], (BATCH, SEQ, D_MODEL), 1.0),
        'rel_table': nrm(ks[1], (REL_BUCKETS, N_HEADS), 0.5),
        'ln_g': 1.0 + nrm(ks[2], (DEPTH_2, 3, D_MODEL), 0.05),
        'ln_b': nrm(ks[3], (DEPTH_2, 3, D_MODEL), 0.02),
        'ffn_w1': nrm(ks[4], (DEPTH_2, 2, D_MODEL, FFN_DIM), D_MODEL ** -0.5),
        'ffn_w3': nrm(ks[5], (DEPTH_2, 2, D_MODEL, FFN_DIM), D_MODEL ** -0.5),
        'ffn_w2': nrm(ks[6], (DEPTH_2, 2, FFN_DIM, D_MODEL), DN_BETA * FFN_DIM ** -0.5),
        'sgu_w_in': nrm(ks[7], (N_A_LAYERS, D_MODEL, SGU_HIDDEN), D_MODEL ** -0.5),
        'sgu_ln_g': 1.0 + nrm(ks[8], (N_A_LAYERS, SGU_HALF), 0.05),
        'sgu_ln_b': nrm(ks[9], (N_A_LAYERS, SGU_HALF), 0.02),
        'sgu_w_s': nrm(ks[10], (N_A_LAYERS, SGU_GROUPS, SGU_CHUNK, SGU_CHUNK), 0.05),
        'sgu_b_s': 1.0 + nrm(ks[11], (N_A_LAYERS, SGU_GROUPS, SGU_CHUNK), 0.05),
        'sgu_w_out': nrm(ks[12], (N_A_LAYERS, SGU_HALF, D_MODEL), DN_BETA * SGU_HALF ** -0.5),
        'kv_w': kv_w.reshape(D_MODEL, N_KV_SLOTS * N_KV_GROUPS * HEAD_DIM_2),
        'cmp_pe': nrm(ks[14], (2, CMP_LEN, HEAD_DIM_2), 0.5),
        'cmp_w1': nrm(ks[15], (2, CMP_LEN * HEAD_DIM_2, PHI_HIDDEN), (CMP_LEN * HEAD_DIM_2) ** -0.5),
        'cmp_b1': nrm(ks[16], (2, PHI_HIDDEN), 0.02),
        'cmp_w2': nrm(ks[17], (2, PHI_HIDDEN, HEAD_DIM_2), PHI_HIDDEN ** -0.5),
        'nsa_w_qg': nrm(ks[18], (N_B_LAYERS, D_MODEL, N_HEADS * HEAD_DIM_2 + 3 * N_HEADS), D_MODEL ** -0.5),
        'nsa_w_o': nrm(ks[19], (N_B_LAYERS, N_HEADS * HEAD_DIM_2, D_MODEL), DN_BETA * (N_HEADS * HEAD_DIM_2) ** -0.5),
    }

def second_block(x, rel_table, ln_g, ln_b, ffn_w1, ffn_w3, ffn_w2, sgu_w_in, sgu_ln_g, sgu_ln_b, sgu_w_s,
              sgu_b_s, sgu_w_out, kv_w, cmp_pe, cmp_w1, cmp_b1, cmp_w2, nsa_w_qg, nsa_w_o):
    h = x
    shared = None
    for layer in range(DEPTH_2):
        if layer == N_A_LAYERS:
            shared = nsa_shared_kv(h, kv_w, cmp_pe, cmp_w1, cmp_b1, cmp_w2)
        h = post_norm(h, 0.5 * swiglu(h, ffn_w1[layer, 0], ffn_w3[layer, 0], ffn_w2[layer, 0]),
                      ln_g[layer, 0], ln_b[layer, 0])
        if layer < N_A_LAYERS:
            a = layer
            mix = chunked_sgu_mixer(h, sgu_w_in[a], sgu_ln_g[a], sgu_ln_b[a], sgu_w_s[a], sgu_b_s[a], sgu_w_out[a])
        else:
            bl = layer - N_A_LAYERS
            mix = nsa_mixer(h, shared, nsa_w_qg[bl], nsa_w_o[bl], rel_table)
        h = post_norm(h, mix, ln_g[layer, 1], ln_b[layer, 1])
        h = post_norm(h, 0.5 * swiglu(h, ffn_w1[layer, 1], ffn_w3[layer, 1], ffn_w2[layer, 1]),
                      ln_g[layer, 2], ln_b[layer, 2])
    return h


def setup_inputs(seed=0):
    out = dict(first_inputs(seed))
    for name, value in second_inputs(seed + 1).items():
        if name != "x":
            out[name + "_2"] = value
    return out


def reference(
    x, mem, positions, g_mix, w_in, b_gate, sinks, g_mem, w_mem_kv, w_proj_swa, w_proj_dsa,
    w_proj_mem, w_out, g_mlp, w_mlp_in, w_mlp_out, g_final, rel_table_2, ln_g_2, ln_b_2,
    ffn_w1_2, ffn_w3_2, ffn_w2_2, sgu_w_in_2, sgu_ln_g_2, sgu_ln_b_2, sgu_w_s_2, sgu_b_s_2,
    sgu_w_out_2, kv_w_2, cmp_pe_2, cmp_w1_2, cmp_b1_2, cmp_w2_2, nsa_w_qg_2, nsa_w_o_2,
):
    x = first_block(
        x, mem, positions, g_mix, w_in, b_gate, sinks, g_mem, w_mem_kv, w_proj_swa, w_proj_dsa,
        w_proj_mem, w_out, g_mlp, w_mlp_in, w_mlp_out, g_final,
    )
    return second_block(
        x, rel_table_2, ln_g_2, ln_b_2, ffn_w1_2, ffn_w3_2, ffn_w2_2, sgu_w_in_2, sgu_ln_g_2,
        sgu_ln_b_2, sgu_w_s_2, sgu_b_s_2, sgu_w_out_2, kv_w_2, cmp_pe_2, cmp_w1_2, cmp_b1_2,
        cmp_w2_2, nsa_w_qg_2, nsa_w_o_2,
    )


_drawn_inputs = setup_inputs


def setup_inputs(seed=0):
    import zlib

    import numpy as np

    out = dict(_drawn_inputs(seed))
    spreads = {}
    factors = {'g_mix': 3.291,
     'b_gate': 8.0,
     'sinks': 23.624,
     'g_mem': 8.0,
     'g_mlp': 3.131,
     'g_final': 2.758,
     'rel_table_2': 4.062,
     'sgu_ln_g_2': 8.0,
     'sgu_ln_b_2': 51.02,
     'sgu_b_s_2': 4.737,
     'cmp_b1_2': 22.891}
    for name, (base, spread) in spreads.items():
        noise = np.random.default_rng([zlib.crc32(name.encode()), seed]).standard_normal(out[name].shape)
        drawn = base * np.exp(spread * noise) if base else spread * noise
        out[name] = jnp.asarray(drawn.astype(out[name].dtype))
    for name, factor in factors.items():
        out[name] = (out[name] * factor).astype(out[name].dtype)
    return out
```

```python
from contextlib import ExitStack

import numpy as np

import concourse.bass as bass
from concourse import mybir

F32 = mybir.dt.float32
I32 = mybir.dt.int32
BF16 = mybir.dt.bfloat16
ACT = mybir.ActivationFunctionType
ALU = mybir.AluOpType
AX = mybir.AxisListType

P = 128
S = 256
NB = S // P
D = 1024
KT = D // P
HD = 64
UNIT = 2048
UC = UNIT // KT
SLOTS = 6
NEG = -1e30
GONE = -3e38
RMS_EPS, LN_EPS = 1e-6, 1e-5
ALPHA = (2.0 * 2) ** 0.25

C_QS, C_KS, C_VS, C_QD, C_KD, C_VD, C_QI, C_KI, C_WI, C_QM, C_GATE = (
    0, 512, 640, 768, 1024, 1088, 1152, 1408, 1472, 1476, 1732)
N_PROJ = -(-C_GATE // UC)
N_IDX = 4
TOPK = min(256, S // 4)
T_QS, T_KS, T_QD, T_KD, T_QI, T_KI, T_QM, N_TURN = 0, 4, 5, 7, 8, 10, 11, 13
R_COLS = T_QM * P

MLP_CHUNKS = 4 * D // UC
FFN = 2816
FFN_CHUNKS = FFN // UC
SGU = 2048
GROUPS = 8
NH, NG = 16, 4
N_CMP = S // 16 - 1
CMP_KEYS = [sum(16 * n + 31 <= (b + 1) * P - 1 for n in range(N_CMP)) for b in range(NB)]
N_REL = 2 * P + P - 1
N_FFN = 4
MLP_BODY, FFN_BODY = 3, 2
V_GMIX, V_GMEM, V_GMLP, V_GFIN, V_LNG, V_LNB, V_BG, N_VEC = 0, 1, 2, 3, 4, 10, 16, 19
V_B1, V_PE, N_COLV = KT * N_VEC, KT * N_VEC + 4, KT * N_VEC + 4 + 32
K_ID, K_SWA, K_CAUSAL, K_FREQ, K_ROW, N_CONST = 0, 128, 384, 640, 672, 673


def plan_units():
    u = [("proj", i) for i in range(N_PROJ)] + [("memkv", i) for i in range(2)]
    u += [("gate", i) for i in range(12)]
    u += [("pswa", 0), ("pswa", 1), ("pdsa", 0), ("pmem", 0)]
    u += [("wout", i) for i in range(4)]
    u += [("mu", 0)]
    for c in range(1, MLP_CHUNKS):
        u += [("mu", c), ("md", c - 1)]
    u += [("md", MLP_CHUNKS - 1)]

    def ffn(f):
        out = [("w1", f, 0), ("w3", f, 0)]
        for c in range(1, FFN_CHUNKS):
            out += [("w1", f, c), ("w3", f, c), ("w2", f, c - 1)]
        return out + [("w2", f, FFN_CHUNKS - 1)]

    u += ffn(0)
    u += [("sv", i) for i in range(8)] + [("su", i) for i in range(8)] + [("so", i) for i in range(8)]
    u += ffn(1)
    u += [("kv", i) for i in range(6)] + [("cw", i) for i in range(4)]
    u += ffn(2)
    u += [("qg", 0)] + [("q", i) for i in range(4)] + [("wo", i) for i in range(4)]
    u += ffn(3)
    return u


N_BATCH = 4 + NH // 2
MIX1 = [("I",), ("S", 0), ("S", 1), ("G", 0), ("G", 1), ("G", 2), ("V", 0), ("S", 2), ("G", 3), ("G", 4),
        ("V", 1), ("S", 3), ("G", 5), ("G", 6), ("G", 7), ("V", 2), ("G", 8), ("G", 9), ("G", 10),
        ("G", 11), ("V", 3)]
MIX2 = [("S", 4), ("S", 5), ("C",)]
for _n in range(4, N_BATCH):
    MIX2 += [("V", _n)] + ([("S", _n + 2)] if _n + 2 < N_BATCH else [])


def plan_tiles():
    names = [("vec",), ("rel",)]

    def norm(n):
        return [("n", n, b, h) for b in range(NB) for h in range(2)]

    def ffn(f):
        return [("f", f, c, t) for c in range(FFN_CHUNKS) for t in range(2)]

    def mix(steps):
        out = []
        for s in steps:
            if s[0] == "G":
                out += [("g", 2 * s[1]), ("g", 2 * s[1] + 1)]
            elif s[0] == "V":
                out += [("T", s[1], p) for p in range(4)]
            elif s[0] == "C":
                out += [("cs", b, half) for b in range(NB) for half in range(2)] + [("ct", b) for b in range(NB)]
        return out

    names += norm(0) + norm(1)
    names += [("p", i, b) for i in range(N_PROJ) for b in range(NB)]
    names += [("mk", f) for f in range(2)] + [("mv", b) for b in range(NB)]
    names += [("turn", i) for i in range(-(-N_TURN // 2))]
    names += mix(MIX1)
    names += [("mg", ft, x) for ft in range(KT) for x in range(2)]
    names += norm(2)
    names += [("m", c) for c in range(MLP_CHUNKS)]
    names += norm(3) + ffn(0) + norm(4)
    names += [("sv", i, b) for i in range(8) for b in range(NB)] + [("wst", i) for i in range(2)]
    names += [("su", i) for i in range(16)] + [("mix", i) for i in range(16)]
    names += norm(5) + ffn(1) + norm(6)
    names += [("kT", s, f) for s in (0, 1) for f in range(2)] + [("kT", 2, f) for f in range(2)]
    names += [("kv", 3, b) for b in range(NB)] + [("kT", 4, f) for f in range(2)] + [("kv", 5, b) for b in range(NB)]
    names += [("ch", s) for s in range(2)] + [("ck",), ("cv",)]
    names += ffn(2) + norm(7)
    names += [("qg", b) for b in range(NB)] + [("q", i) for i in range(8)]
    names += mix(MIX2) + norm(8) + ffn(3) + norm(9)
    held, out, turn = [0] * 4, {}, 0
    for seq, name in enumerate(names):
        if name[0] == "m":
            bank = name[1] % MLP_BODY
        else:
            bank, turn = turn % 4, turn + 1
        out[name] = (bank, held[bank], seq)
        held[bank] += 1
    return out


UNITS = {name: i for i, name in enumerate(plan_units())}
TILES = plan_tiles()
ACC_DONE = {2: ("wout", 3), 3: ("md", MLP_CHUNKS - 1), 4: ("w2", 0, FFN_CHUNKS - 1), 5: ("so", 7),
            6: ("w2", 1, FFN_CHUNKS - 1), 7: ("w2", 2, FFN_CHUNKS - 1), 8: ("wo", 3),
            9: ("w2", 3, FFN_CHUNKS - 1)}
PAIRS = {}
for _s in MIX1 + MIX2:
    if _s[0] == "I":
        PAIRS.update({("I", h): len(PAIRS) + h for h in range(N_IDX)})
    if _s[0] == "S":
        PAIRS.update({(_s[1], p): len(PAIRS) + p for p in range(4)})


def two_blocks(nc, t, out):
    ctx = ExitStack()
    with ctx:
        def sb(name, shape, dt=F32):
            return ctx.enter_context(nc.sbuf_tensor(name, shape, dt))

        def sem(name):
            return ctx.enter_context(nc.semaphore(name))

        banks = [ctx.enter_context(nc.psum_tensor(f"bank{i}", [P, 512], F32)) for i in range(8)]
        acc = banks[4:8]
        score_banks = banks[4:7]
        o_bank = banks[7]

        ring = sb("ring", [P, SLOTS, UNIT])
        resid = sb("resid", [P, NB, D])
        xn = sb("xn", [P, NB, D])
        hT = sb("hT", [P, KT, S])
        prob = sb("prob", [P, 2, 8, S])
        probT = sb("probT", [P, 4, 2, 2, P])
        oT = sb("oT", [P, KT, S])
        gain_bc = sb("gain_bc", [P, D])
        bias_bc = sb("bias_bc", [P, D])
        hid = sb("hid", [P, MLP_BODY, 2, S])
        const = sb("const", [P, N_CONST])
        zeros = sb("zeros", [P, S])
        ones = sb("ones", [1, P])
        colv = sb("colv", [P, N_COLV])
        sinks = sb("sinks", [P, 8])
        eps = sb("eps", [P, 2])
        stats = sb("stats", [P, NB, 4, 6])
        mv = sb("mv", [P, NB, 2])
        msq = sb("msq", [P, NB])
        sd = sb("sd", [P, NB])
        rstd = sb("rstd", [P, NB])
        row_max = sb("row_max", [P, 2, 8])
        neg_max = sb("neg_max", [P, 2, 8])
        row_sum = sb("row_sum", [P, 2, 8])
        sink_in = sb("sink_in", [P, 2, 8])
        sink_exp = sb("sink_exp", [P, 2, 8])
        row_rcp = sb("row_rcp", [P, 2, 8])
        wsc = sb("wsc", [P, NB, N_IDX])
        best = sb("best", [P, 8])
        cmax = sb("cmax", [P, NH])
        csum = sb("csum", [P, NH])
        crcp = sb("crcp", [P, NH])
        pos_i = sb("pos_i", [P, NB], I32)
        pos_f = sb("pos_f", [P, NB])
        trig = sb("trig", [P, 2, NB, 32])
        ang = sb("ang", [P, 4, NB, 32])
        act_out = probT[:].rearrange("p a b c q -> p (a b c q)").rearrange("p (a c) -> p a c", a=4)
        prob_all = prob[:].rearrange("p a k s -> p (a k s)")
        rope_tmp = prob_all[:, 0:4 * NB * 10 * 32].rearrange("p (x b h e) -> p x b h e", x=4, b=NB, h=10)
        merge_tmp = prob_all[:, 0:6 * S].rearrange("p (y x s) -> p y x s", y=2, x=3)
        idx_tmp = prob_all[:, 2048:2048 + S]
        vec_rows = prob_all[0:N_VEC, 0:D]
        pe_rows = prob_all[0:32, D:D + P]
        b1_rows = prob_all[0:4, D + P:D + 2 * P]
        rel_rows = prob_all[0:33, 1536:1536 + NH]
        onehot = prob_all[0:33, 2048:2048 + N_REL]
        rel_out = prob_all[0:NH, 2560:2560 + N_REL]

        arena = sb("arena", [P, 19848])

        def take(at, *shape):
            n = int(np.prod(shape))
            a = arena[:, at[0]:at[0] + n]
            at[0] += n
            if len(shape) == 1:
                return a
            names = "abcd"[:len(shape)]
            return a.rearrange("p (%s) -> p %s" % (" ".join(names), " ".join(names)),
                               **{x: s for x, s in zip(names[:-1], shape[:-1])})

        at = [0]
        proj = take(at, NB, C_GATE)
        roped = take(at, NB, R_COLS)
        qkT = take(at, N_TURN, S)
        gT = take(at, 24, S)
        mT = take(at, KT, S)
        kmT = take(at, 2, S)
        vm = take(at, NB, S)
        isc = take(at, NB, S)
        maskD = take(at, NB, S)
        memt = gT[:, 0:8, :].rearrange("p a s -> p (a s)").rearrange("p (b d) -> p b d", b=NB)
        mergedT = mT
        at = [0]
        vtok = take(at, NB, SGU)
        uT = take(at, 16, S)
        ws = take(at, GROUPS, P)
        wsT = take(at, GROUPS, P)
        sgu_g = take(at, SGU)
        sgu_b = take(at, SGU)
        bs_row = take(at, D)[0:1, :]
        at = [0]
        rel = take(at, NH, S)
        ka = take(at, 4, 2, S)
        kb = take(at, 4, 2, S)
        vv = take(at, 2, NB, S)
        qT = take(at, 8, S)
        cx = take(at, 2, 16, NG, 16)
        hidc = take(at, 2, 2, NG, 32)
        kcT = take(at, NG, 16)
        vc = take(at, S)
        pc = take(at, NB, NH, 32)
        pcT = take(at, NG, S)
        sc = take(at, NH, 16)
        cw2 = take(at, 2, 2, HD)
        nsa_g = take(at, NB, 48)

        rel_dram = nc.dram_tensor("rel_scratch", (NH, P, N_REL), F32, kind="Internal")

        ident = const[:, K_ID:K_ID + P]
        mask_swa = const[:, K_SWA:K_SWA + S]
        mask_causal = const[:, K_CAUSAL:K_CAUSAL + S]
        freq = const[:, K_FREQ:K_FREQ + 32]
        row_valid = const[:, K_ROW:K_ROW + 1]

        arrived = [sem(f"arrived{i}") for i in range(SLOTS)]
        unit_used = sem("unit_used")
        tile_done = sem("tile_done")
        tile_read = [sem(f"tile_read{i}") for i in range(4)]
        x_in, mem_in, const_in, vec_in, rel_in, sink_ld, pos_in = (
            sem(n) for n in ("x_in", "mem_in", "const_in", "vec_in", "rel_in", "sink_ld", "pos_in"))
        fills = sem("fills")
        gb_in = sem("gb_in")
        sgu_in = sem("sgu_in")
        cw2_in = sem("cw2_in")
        rel_out_ready, rel_stored, rel_back = sem("rel_out_ready"), sem("rel_stored"), sem("rel_back")
        cols_ready = sem("cols_ready")
        var_ready, sd_ready, xn_ready, resid_ready = sem("var_ready"), sem("sd_ready"), sem("xn_ready"), sem("resid_ready")
        angle_ready, trig_ready = sem("angle_ready"), sem("trig_ready")
        roped_ready = sem("roped_ready")
        score_done = sem("score_done")
        score_read = [sem(f"score_read{i}") for i in range(3)]
        neg_ready, exp_ready, prob_ready = sem("neg_ready"), sem("exp_ready"), sem("prob_ready")
        pv_done, o_read = sem("pv_done"), sem("o_read")
        merged_ready = sem("merged_ready")
        act_ready, hid_ready = sem("act_ready"), sem("hid_ready")
        ws_ready, sgu_var, sgu_sd, v_ready = sem("ws_ready"), sem("sgu_var"), sem("sgu_sd"), sem("v_ready")
        k_swapped = [sem(f"k_swapped{i}") for i in range(4)]
        cx_ready = sem("cx_ready")
        hidc_ready = sem("hidc_ready")
        cscore_ready, cexp_ready, pc_ready = sem("cscore_ready"), sem("cexp_ready"), sem("pc_ready")
        out_ready, stored = sem("out_ready"), sem("stored")
        dve_step, act_step, pool_step = sem("dve_step"), sem("act_step"), sem("pool_step")

        def bank_of(name):
            return banks[TILES[name][0]]

        def tile_ready(eng, name):
            eng.wait_ge(tile_done, TILES[name][2] + 1)
            return bank_of(name)

        def tile_copied(eng, name):
            eng.wait_ge(tile_read[TILES[name][0]], TILES[name][1] + 1)

        def frees(name):
            return tile_read[TILES[name][0]]

        def slot(name):
            return UNITS[name] % SLOTS

        def up_unit(name):
            return ring[:, slot(name), :].rearrange("p (k c) -> p k c", k=KT)

        def down_unit(name):
            return ring[:, slot(name), :].rearrange("p (k c) -> p k c", k=2)

        def chained(eng, step):
            count = [0]

            def link(ins):
                ins.then_inc(step, 1)
                count[0] += 1
                eng.wait_ge(step, count[0])
            return link

        def attention(n):
            tiles = []
            if n < 2:
                for h in range(8):
                    kv, j = h // 4, h % 4
                    part = slice(64 * kv, 64 * kv + 64)
                    w = P * (n + 1)
                    tiles.append((qkT[part, T_QS + j, n * P:(n + 1) * P], qkT[part, T_KS, 0:w], w,
                                  mask_swa[:, S - w:S], 0.125, sinks[:, h:h + 1],
                                  [proj[:, k, C_VS + kv * HD:C_VS + (kv + 1) * HD] for k in range(n + 1)],
                                  64 * (h % 2), (h // 2) * P))
            elif n < 4:
                for b in range(NB):
                    for h in (0, 2, 1, 3):
                        part = slice(64 * (h % 2), 64 * (h % 2) + 64)
                        qs = slice(b * P, (b + 1) * P)
                        o = (64 * (h % 2), (h // 2) * S + b * P)
                        if n == 2:
                            tiles.append((qkT[part, T_QM + h // 2, qs], kmT[part, h // 2, :], S, zeros[:, :], 0.125,
                                          GONE, [vm[:, k, h * HD:(h + 1) * HD] for k in range(NB)], *o))
                        else:
                            w = P * (b + 1)
                            tiles.append((qkT[part, T_QD + h // 2, qs], qkT[part, T_KD, 0:w], w, maskD[:, b, 0:w],
                                          0.125, GONE,
                                          [proj[:, k, C_VD:C_VD + HD] for k in range(b + 1)], *o))
            else:
                for h in (2 * (n - 4), 2 * (n - 4) + 1):
                    g = h // 4
                    part = slice(64 * (h % 2), 64 * (h % 2) + 64)
                    keys = ka if h % 2 == g % 2 else kb
                    for b in range(NB):
                        w = P * (b + 1)
                        for br in range(2):
                            tiles.append((qT[part, h // 2, b * P:(b + 1) * P], keys[part, 2 + br, g // 2, 0:w], w,
                                          rel[:, h, S - w:S], 1.0, GONE,
                                          [vv[:, br, k, g * HD:(g + 1) * HD] for k in range(b + 1)],
                                          64 * (h % 2), b * P))
            return tiles

        block = ctx.enter_context(nc.Block())

        @block.sync
        def _(sp):
            sp.dma_start(resid[:], t["x"][0].rearrange("(b p) d -> p b d", p=P)).then_inc(x_in, 16)
            sp.dma_start(const[:], t["consts"]).then_inc(const_in, 16)
            sp.dma_start(memt, t["mem"][0].rearrange("(b p) d -> p b d", p=P)).then_inc(mem_in, 16)

            def up(w, c0, n=UC):
                return w.rearrange("(k p) c -> p k c", p=P)[:, :, c0:c0 + n]

            def down(w, r):
                return w.rearrange("(r k p) c -> r p k c", p=P, k=2)[r]

            w_in = t["w_in"][0]
            w1 = [t["ffn_w1_2"][f // 2, f % 2].rearrange("(k p) c -> p k c", p=P) for f in range(N_FFN)]
            w3 = [t["ffn_w3_2"][f // 2, f % 2].rearrange("(k p) c -> p k c", p=P) for f in range(N_FFN)]
            w2 = [t["ffn_w2_2"][f // 2, f % 2].rearrange("(r k p) c -> r p k c", p=P, k=2) for f in range(N_FFN)]
            mu = t["w_mlp_in"][0].rearrange("(k p) c -> p k c", p=P)
            md = t["w_mlp_out"][0].rearrange("(r k p) c -> r p k c", p=P, k=2)

            def source(name):
                kind, i = name[0], name[-1]
                return {
                    "proj": lambda: up(w_in, i * UC, min(UC, C_GATE - i * UC)),
                    "memkv": lambda: up(t["w_mem_kv"][0], i * UC),
                    "gate": lambda: up(w_in, C_GATE + i * UC),
                    "pswa": lambda: down(t["w_proj_swa"][0], i),
                    "pdsa": lambda: down(t["w_proj_dsa"][0], i),
                    "pmem": lambda: down(t["w_proj_mem"][0], i),
                    "wout": lambda: down(t["w_out"][0], i),
                    "mu": lambda: up(t["w_mlp_in"][0], i * UC),
                    "md": lambda: down(t["w_mlp_out"][0], i),
                    "w1": lambda: w1[name[1]][:, :, i * UC:(i + 1) * UC],
                    "w3": lambda: w3[name[1]][:, :, i * UC:(i + 1) * UC],
                    "w2": lambda: w2[name[1]][i],
                    "sv": lambda: up(t["sgu_w_in_2"][0], SGU + i * UC),
                    "su": lambda: up(t["sgu_w_in_2"][0], i * UC),
                    "so": lambda: down(t["sgu_w_out_2"][0], i),
                    "kv": lambda: up(t["kv_w_2"], i * UC),
                    "cw": lambda: t["cmp_w1_2"][i // 2].rearrange("(h k p) c -> h p k c", h=2, p=P)[i % 2],
                    "qg": lambda: up(t["nsa_w_qg_2"][0], D, 48),
                    "q": lambda: up(t["nsa_w_qg_2"][0], i * UC),
                    "wo": lambda: down(t["nsa_w_o_2"][0], i),
                }[kind]()

            def load(name):
                u = UNITS[name]
                src = source(name)
                n = src.shape[1] * src.shape[2]
                dst = ring[:, u % SLOTS, 0:n].rearrange("p (k c) -> p k c", k=src.shape[1])
                if u >= SLOTS:
                    sp.wait_ge(unit_used, u - SLOTS + 1)
                sp.dma_start(dst, src).then_inc(arrived[u % SLOTS], 16)

            def load_loop(first, turns, sources):
                u = UNITS[first]
                with sp.Fori(0, turns) as i:
                    for k, src in enumerate(sources):
                        s = (u + k) % SLOTS
                        view = src(i)
                        dst = ring[:, s, :].rearrange("p (k c) -> p k c", k=view.shape[1])
                        used = sp.snap(i * SLOTS + (u + k - SLOTS + 1))
                        sp.wait_ge(unit_used, used)
                        sp.dma_start(dst, view).then_inc(arrived[s], 16)

            def column(w, c):
                return lambda i: w[:, :, bass.ds(sp.snap(i * (c[0] * UC) + c[1] * UC), UC)]

            def rows(w, c):
                return lambda i: w[bass.ds(sp.snap(i * c[0] + c[1]), 1)].rearrange("r p k c -> (r p) k c")

            def ffn(f):
                load(("w1", f, 0))
                load(("w3", f, 0))
                body = []
                for k in range(FFN_BODY):
                    body += [column(w1[f], (FFN_BODY, k + 1)), column(w3[f], (FFN_BODY, k + 1)),
                             rows(w2[f], (FFN_BODY, k))]
                load_loop(("w1", f, 1), (FFN_CHUNKS - 1) // FFN_BODY, body)
                load(("w2", f, FFN_CHUNKS - 1))

            def some(kind, n):
                for i in range(n):
                    load((kind, i))

            some("proj", N_PROJ)
            some("memkv", 2)
            some("gate", 12)
            some("pswa", 2)
            some("pdsa", 1)
            some("pmem", 1)
            some("wout", 4)
            load(("mu", 0))
            body = []
            for k in range(MLP_BODY):
                body += [column(mu, (MLP_BODY, k + 1)), rows(md, (MLP_BODY, k))]
            load_loop(("mu", 1), (MLP_CHUNKS - 1) // MLP_BODY, body)
            load(("md", MLP_CHUNKS - 1))
            ffn(0)
            some("sv", 8)
            some("su", 8)
            some("so", 8)
            ffn(1)
            some("kv", 6)
            some("cw", 4)
            ffn(2)
            load(("qg", 0))
            some("q", 4)
            some("wo", 4)
            ffn(3)
            for b in range(NB):
                sp.wait_ge(out_ready, b + 1)
                sp.dma_start(out[0, b * P:(b + 1) * P, :], xn[:, b, :]).then_inc(stored, 16)
            sp.wait_ge(stored, 16 * NB)

        @block.tensor
        def _(pe):
            owed = [0]

            def mm(o, lhsT, rhs, start, stop):
                ins = pe.matmul(o, lhsT, rhs, start=start, stop=stop)
                return ins

            def settle(ins):
                if owed[0]:
                    ins.then_inc(unit_used, owed[0])
                    owed[0] = 0

            def open_tile(name):
                b, held, _ = TILES[name]
                if held:
                    pe.wait_ge(tile_read[b], held)
                return banks[b]

            def have(name):
                u = UNITS[name]
                pe.wait_ge(arrived[u % SLOTS], 16 * (u // SLOTS + 1))

            def turn(o, a, n=P):
                return pe.transpose(o, a, ident[0:n, 0:n])

            def up_T(o, unit, c0, n, act, w=S):
                for k in range(KT):
                    ins = mm(o, unit[:, k, c0:c0 + n], act[:, k, 0:w], k == 0, k == KT - 1)
                    if k == 0:
                        settle(ins)
                return ins

            def up_tok(o, unit, n, act, b):
                for k in range(KT):
                    ins = mm(o, act[:, k, b * P:(b + 1) * P], unit[:, k, 0:n], k == 0, k == KT - 1)
                    if k == 0:
                        settle(ins)
                return ins

            def down_tiles(unit, act, first, last):
                for k in range(2):
                    for b in range(NB):
                        for h in range(2):
                            ins = mm(acc[b * 2 + h][:, :], act(k, b), unit[:, k, h * 512:(h + 1) * 512],
                                     first and k == 0, last and k == 1)
                            if k == 0 and b == 0 and h == 0:
                                settle(ins)
                ins.then_inc(unit_used, 1)

            def norm(n):
                for b in range(NB):
                    pe.wait_ge(xn_ready, NB * n + b + 1)
                    for h in range(2):
                        o = open_tile(("n", n, b, h))
                        for k in range(4):
                            ins = turn(o[:, k * P:(k + 1) * P], xn[:, b, (h * 4 + k) * P:(h * 4 + k + 1) * P])
                            if k == 0:
                                settle(ins)
                        ins.then_inc(tile_done, 1)

            def normed(n):
                for b in range(NB):
                    for h in range(2):
                        tile_copied(pe, ("n", n, b, h))

            pe.wait_ge(const_in, 16)
            pe.wait_ge(vec_in, 16 * 9)
            o = open_tile(("vec",))
            for k in range(KT):
                turn(o[:, k * N_VEC:(k + 1) * N_VEC], vec_rows[:, k * P:(k + 1) * P], N_VEC)
            turn(o[:, V_B1:V_B1 + 4], b1_rows, 4)
            turn(o[:, V_PE:V_PE + 32], pe_rows, 32).then_inc(tile_done, 1)
            pe.wait_ge(rel_in, 32)
            pe.wait_ge(fills, 1)
            o = open_tile(("rel",))
            mm(o[0:NH, 0:N_REL], rel_rows, onehot, True, True).then_inc(tile_done, 1)

            norm(0)
            norm(1)
            normed(0)
            for i in range(N_PROJ):
                have(("proj", i))
                n = min(UC, C_GATE - i * UC)
                unit = ring[:, slot(("proj", i)), 0:KT * n].rearrange("p (k c) -> p k c", k=KT)
                for b in range(NB):
                    o = open_tile(("p", i, b))
                    up_tok(o[:, 0:n], unit, n, hT, b).then_inc(tile_done, 1)
                owed[0] += 1
            normed(1)
            have(("memkv", 0))
            for f in range(2):
                o = open_tile(("mk", f))
                up_T(o[:, 0:S], up_unit(("memkv", 0)), f * P, P, mT).then_inc(tile_done, 1)
            owed[0] += 1
            have(("memkv", 1))
            for b in range(NB):
                o = open_tile(("mv", b))
                up_tok(o[:, 0:S], up_unit(("memkv", 1)), S, mT, b).then_inc(tile_done, 1)
            owed[0] += 1
            pe.wait_ge(roped_ready, 1)
            for i in range(-(-N_TURN // 2)):
                o = open_tile(("turn", i))
                for j in range(2 * i, min(2 * i + 2, N_TURN)):
                    for b in range(NB):
                        src = roped[:, b, j * P:(j + 1) * P] if j < T_QM else \
                            proj[:, b, C_QM + (j - T_QM) * P:C_QM + (j - T_QM + 1) * P]
                        ins = turn(o[:, ((j % 2) * NB + b) * P:((j % 2) * NB + b + 1) * P], src)
                        settle(ins)
                ins.then_inc(tile_done, 1)
            for i in range(-(-N_TURN // 2)):
                tile_copied(pe, ("turn", i))
            tile_copied(pe, ("mk", 1))
            tile_copied(pe, ("mv", 1))

            def open_pair(key):
                n = PAIRS[key]
                if n >= 3:
                    pe.wait_ge(score_read[n % 3], n // 3)
                return score_banks[n % 3]

            def index_scores():
                for h in range(N_IDX):
                    o = open_pair(("I", h))
                    part = slice(64 * (h % 2), 64 * (h % 2) + 64)
                    for b in range(NB):
                        w = P * (b + 1)
                        ins = mm(o[:, b * S:b * S + w], qkT[part, T_QI + h // 2, b * P:(b + 1) * P],
                                 qkT[part, T_KI, 0:w], True, True)
                    ins.then_inc(score_done, 1)

            def scores(n):
                tiles = attention(n)
                for p in range(4):
                    o = open_pair((n, p))
                    for a in range(2):
                        q, k, w = tiles[2 * p + a][:3]
                        ins = mm(o[:, a * S:a * S + w], q, k, True, True)
                    ins.then_inc(score_done, 1)

            def turn_probs(n, p):
                tiles = attention(n)
                o = open_tile(("T", n, p))
                pe.wait_ge(prob_ready, 4 * n + p + 1)
                for a in range(2):
                    for k in range(tiles[2 * p + a][2] // P):
                        ins = turn(o[:, (a * 2 + k) * P:(a * 2 + k + 1) * P],
                                   prob[:, n % 2, 2 * p + a, k * P:(k + 1) * P])
                        settle(ins)
                ins.then_inc(tile_done, 1)

            def values(n, p):
                tiles = attention(n)
                if p == 0 and n:
                    pe.wait_ge(o_read, n)
                tile_copied(pe, ("T", n, p))
                for a in range(2):
                    _, _, w, _, _, _, v, part, col = tiles[2 * p + a]
                    o = o_bank[part:part + 64, col:col + P]
                    if n >= 4 and a == 0:
                        h, b = 2 * (n - 4) + p // 2, p % 2
                        r = slice(32 * (h % 4), 32 * (h % 4) + 32)
                        mm(o, vc[r, (h // 4) * HD:(h // 4 + 1) * HD], pcT[r, h // 4, b * P:(b + 1) * P], True, False)
                    for k in range(w // P):
                        first = k == 0 and n < 4
                        last = k == w // P - 1 and (n < 4 or a == 1)
                        ins = mm(o, v[k], probT[:, (4 * n + p) % 4, a, k, :], first, last)
                ins.then_inc(pv_done, 1)

            def batch_values(n):
                for p in range(4):
                    turn_probs(n, p)
                    if p:
                        values(n, p - 1)
                values(n, 3)

            def gate(i):
                have(("gate", i))
                for f in range(2):
                    o = open_tile(("g", 2 * i + f))
                    up_T(o[:, 0:S], up_unit(("gate", i)), f * P, P, hT).then_inc(tile_done, 1)
                owed[0] += 1

            for s in MIX1:
                if s[0] == "I":
                    index_scores()
                elif s[0] == "S":
                    scores(s[1])
                elif s[0] == "G":
                    gate(s[1])
                else:
                    batch_values(s[1])

            pe.wait_ge(o_read, 4)
            for name in (("pswa", 0), ("pswa", 1), ("pdsa", 0), ("pmem", 0)):
                have(name)
            for ft in range(KT):
                cols = slice(ft * P, (ft + 1) * P)
                o = open_tile(("mg", ft, 0))
                for k in range(4):
                    ins = mm(o[:, 0:S], down_unit(("pswa", k // 2))[:, k % 2, cols], oT[:, k, :], k == 0, k == 3)
                    settle(ins)
                for k in range(2):
                    ins = mm(o[:, S:2 * S], down_unit(("pdsa", 0))[:, k, cols], oT[:, 6 + k, :], k == 0, k == 1)
                ins.then_inc(tile_done, 1)
                o = open_tile(("mg", ft, 1))
                for k in range(2):
                    ins = mm(o[:, 0:S], down_unit(("pmem", 0))[:, k, cols], oT[:, 4 + k, :], k == 0, k == 1)
                ins.then_inc(tile_done, 1)
            owed[0] += 4
            pe.wait_ge(merged_ready, KT)
            for i in range(4):
                have(("wout", i))
                down_tiles(down_unit(("wout", i)), lambda k, b: mergedT[:, 2 * i + k, b * P:(b + 1) * P], i == 0, i == 3)

            def arrived_in_turn(first, k, i):
                u = UNITS[first] + k
                pe.wait_ge(arrived[u % SLOTS], i * 16 + 16 * (u // SLOTS + 1))
                return ring[:, u % SLOTS, :]

            def hid_chunk(n, ring_at):
                pe.wait_ge(hid_ready, n)
                return lambda k, b: hid[:, ring_at, k, b * P:(b + 1) * P]

            def clear_acc():
                nil = zeros[:, :].bitcast(BF16)
                for a in acc:
                    settle(mm(a[:, :], nil[:, 0:P], nil[:, 0:512], True, False))

            def mlp():
                def up_chunk(o, unit):
                    for f in range(2):
                        ins = up_T(o[:, f * S:(f + 1) * S], unit, f * P, P, hT)
                    owed[0] += 1
                    ins.then_inc(tile_done, 1)

                have(("mu", 0))
                up_chunk(open_tile(("m", 0)), up_unit(("mu", 0)))
                clear_acc()
                with pe.Fori(0, (MLP_CHUNKS - 1) // MLP_BODY) as i:
                    for k in range(MLP_BODY):
                        b, held, _ = TILES[("m", k + 1)]
                        pe.wait_ge(tile_read[b], i + held)
                        w = arrived_in_turn(("mu", 1), 2 * k, i)
                        up_chunk(banks[b], w.rearrange("p (k c) -> p k c", k=KT))
                        w = arrived_in_turn(("mu", 1), 2 * k + 1, i)
                        act = hid_chunk(i * MLP_BODY + k + 1, k)
                        down_tiles(w.rearrange("p (k c) -> p k c", k=2), act, False, False)
                have(("md", MLP_CHUNKS - 1))
                down_tiles(down_unit(("md", MLP_CHUNKS - 1)),
                           hid_chunk(MLP_CHUNKS, (MLP_CHUNKS - 1) % MLP_BODY), False, True)

            def ffn(f):
                def up_chunk(w, open_bank):
                    for ft in range(2):
                        o = open_bank(ft)
                        up_T(o[:, 0:S], w[0], ft * P, P, hT)
                        if ft == 1:
                            owed[0] += 1
                        up_T(o[:, S:2 * S], w[1], ft * P, P, hT).then_inc(tile_done, 1)
                    owed[0] += 1

                have(("w1", f, 0))
                have(("w3", f, 0))
                up_chunk((up_unit(("w1", f, 0)), up_unit(("w3", f, 0))), lambda ft: open_tile(("f", f, 0, ft)))
                clear_acc()
                done = MLP_CHUNKS + f * FFN_CHUNKS
                with pe.Fori(0, (FFN_CHUNKS - 1) // FFN_BODY) as i:
                    for k in range(FFN_BODY):
                        w1 = arrived_in_turn(("w1", f, 1), 3 * k, i).rearrange("p (k c) -> p k c", k=KT)
                        w3 = arrived_in_turn(("w1", f, 1), 3 * k + 1, i).rearrange("p (k c) -> p k c", k=KT)

                        def open_bank(ft):
                            b, held, _ = TILES[("f", f, k + 1, ft)]
                            pe.wait_ge(tile_read[b], i + held)
                            return banks[b]
                        up_chunk((w1, w3), open_bank)
                        w2 = arrived_in_turn(("w1", f, 1), 3 * k + 2, i)
                        down_tiles(w2.rearrange("p (k c) -> p k c", k=2), hid_chunk(i * FFN_BODY + done + k + 1, k),
                                   False, False)
                have(("w2", f, FFN_CHUNKS - 1))
                down_tiles(down_unit(("w2", f, FFN_CHUNKS - 1)),
                           hid_chunk(done + FFN_CHUNKS, (FFN_CHUNKS - 1) % FFN_BODY), False, True)

            norm(2)
            normed(2)
            mlp()
            norm(3)
            normed(3)
            ffn(0)
            norm(4)

            normed(4)
            for i in range(8):
                have(("sv", i))
                for b in range(NB):
                    o = open_tile(("sv", i, b))
                    up_tok(o[:, 0:S], up_unit(("sv", i)), S, hT, b).then_inc(tile_done, 1)
                owed[0] += 1
            pe.wait_ge(ws_ready, 1)
            for i in range(2):
                o = open_tile(("wst", i))
                for k in range(4):
                    ins = turn(o[:, k * P:(k + 1) * P], ws[:, 4 * i + k, :])
                    settle(ins)
                ins.then_inc(tile_done, 1)
            for i in range(8):
                have(("su", i))
                for f in range(2):
                    o = open_tile(("su", 2 * i + f))
                    up_T(o[:, 0:S], up_unit(("su", i)), f * P, P, hT).then_inc(tile_done, 1)
                owed[0] += 1
            tile_copied(pe, ("wst", 0))
            tile_copied(pe, ("wst", 1))
            pe.wait_ge(v_ready, NB)
            for ft in range(16):
                g = ft // 2
                o = open_tile(("mix", ft))
                for b in range(NB):
                    ins = mm(o[:, b * P:(b + 1) * P], vtok[:, b, ft * P:(ft + 1) * P], wsT[:, g, :], True, False)
                    settle(ins)
                    ins = mm(o[:, b * P:(b + 1) * P], ones[0:1, :], bs_row[0:1, g * P:(g + 1) * P], False, True)
                ins.then_inc(tile_done, 1)
            for i in range(8):
                have(("so", i))
                for k in range(2):
                    tile_copied(pe, ("mix", 2 * i + k))
                down_tiles(down_unit(("so", i)), lambda k, b: uT[:, 2 * i + k, b * P:(b + 1) * P], i == 0, i == 7)

            norm(5)
            normed(5)
            ffn(1)
            norm(6)
            normed(6)
            for s in range(6):
                have(("kv", s))
                if s in (3, 5):
                    for b in range(NB):
                        o = open_tile(("kv", s, b))
                        up_tok(o[:, 0:S], up_unit(("kv", s)), S, hT, b).then_inc(tile_done, 1)
                else:
                    for f in range(2):
                        o = open_tile(("kT", s, f))
                        up_T(o[:, 0:S], up_unit(("kv", s)), f * P, P, hT).then_inc(tile_done, 1)
                owed[0] += 1
            for s in range(2):
                o = open_tile(("ch", s))
                pe.wait_ge(cx_ready, s + 1)
                for h in range(2):
                    have(("cw", 2 * s + h))
                for m in range(2):
                    for j in range(16):
                        ins = mm(o[:, m * HD:(m + 1) * HD], up_unit(("cw", 2 * s + j // 8))[:, j % 8, m * P:(m + 1) * P],
                                 cx[:, s, j].rearrange("p g i -> p (g i)"), j == 0, j == 15)
                        settle(ins)
                ins.then_inc(tile_done, 1)
                owed[0] += 2
            pe.wait_ge(cw2_in, 32)
            tile_copied(pe, ("ch", 0))
            o = open_tile(("ck",))
            for half in range(2):
                for m in range(2):
                    ins = mm(o[half * 64:half * 64 + 64, 0:P], cw2[:, 0, m, :],
                             hidc[:, 0, m].rearrange("p g i -> p (g i)"), m == 0, m == 1)
                    settle(ins)
            ins.then_inc(tile_done, 1)
            tile_copied(pe, ("ch", 1))
            o = open_tile(("cv",))
            for r in range(4):
                for g in range(NG):
                    for m in range(2):
                        ins = mm(o[32 * r:32 * r + 32, g * HD:(g + 1) * HD], hidc[:, 1, m, g, :], cw2[:, 1, m, :],
                                 m == 0, m == 1)
            ins.then_inc(tile_done, 1)

            ffn(2)
            norm(7)
            normed(7)
            have(("qg", 0))
            unit = ring[:, slot(("qg", 0)), 0:KT * 48].rearrange("p (k c) -> p k c", k=KT)
            for b in range(NB):
                o = open_tile(("qg", b))
                up_tok(o[:, 0:48], unit, 48, hT, b).then_inc(tile_done, 1)
            owed[0] += 1
            for i in range(4):
                have(("q", i))
                for f in range(2):
                    o = open_tile(("q", 2 * i + f))
                    up_T(o[:, 0:S], up_unit(("q", i)), f * P, P, hT).then_inc(tile_done, 1)
                owed[0] += 1
            for i in range(8):
                tile_copied(pe, ("q", i))
            for name in (("kT", 2, 1), ("kT", 4, 1), ("kv", 5, 1), ("ck",), ("cv",)):
                tile_copied(pe, name)
            for k in (2, 3):
                pe.wait_ge(k_swapped[k], 32)

            def compressed():
                for b in range(NB):
                    for half in range(2):
                        o = open_tile(("cs", b, half))
                        part = slice(64 * half, 64 * half + 64)
                        for j in range(NH // 2):
                            ins = mm(o[:, j * 16:j * 16 + CMP_KEYS[b]], qT[part, j, b * P:(b + 1) * P],
                                     kcT[part, j // 2, 0:CMP_KEYS[b]], True, True)
                            settle(ins)
                        ins.then_inc(tile_done, 1)
                for b in range(NB):
                    o = open_tile(("ct", b))
                    pe.wait_ge(pc_ready, b + 1)
                    for g in range(NG):
                        ins = turn(o[:, g * P:(g + 1) * P],
                                   pc[:, b, 4 * g:4 * g + 4, :].rearrange("p h i -> p (h i)"))
                    ins.then_inc(tile_done, 1)
                for b in range(NB):
                    tile_copied(pe, ("ct", b))

            for s in MIX2:
                if s[0] == "S":
                    scores(s[1])
                elif s[0] == "C":
                    compressed()
                else:
                    batch_values(s[1])
            pe.wait_ge(o_read, N_BATCH)
            for i in range(4):
                have(("wo", i))
                down_tiles(down_unit(("wo", i)), lambda k, b: oT[:, 2 * i + k, b * P:(b + 1) * P], i == 0, i == 3)
            norm(8)
            normed(8)
            ffn(3)

        @block.scalar
        def _(act):
            link = chained(act, act_step)
            for row, n, src in ((V_GMIX, 1, t["g_mix"]), (V_GMEM, 1, t["g_mem"]), (V_GMLP, 1, t["g_mlp"]),
                                (V_GFIN, 1, t["g_final"].rearrange("(a d) -> a d", a=1)),
                                (V_LNG, 6, t["ln_g_2"].rearrange("l n d -> (l n) d")),
                                (V_LNB, 6, t["ln_b_2"].rearrange("l n d -> (l n) d")),
                                (V_BG, 3, t["b_gate"].rearrange("a (r d) -> (a r) d", d=D))):
                act.dma_start(vec_rows[row:row + n, :], src).then_inc(vec_in, 16)
            act.dma_start(b1_rows, t["cmp_b1_2"].rearrange("s (m p) -> (s m) p", p=P)).then_inc(vec_in, 16)
            act.dma_start(pe_rows, t["cmp_pe_2"].rearrange("s (j o) d -> (s j) (o d)", o=2)).then_inc(vec_in, 16)
            act.dma_start(pos_i[:], t["positions"].rearrange("a (b p) -> p (a b)", p=P),
                          allow_slow_non_contiguous=True).then_inc(pos_in, 16)
            act.dma_start(onehot, t["onehot"]).then_inc(rel_in, 16)
            act.dma_start(rel_rows[0:32, :], t["rel_table_2"]).then_inc(rel_in, 16)
            act.dma_start(sinks[:], t["sinks"].partition_broadcast(P)).then_inc(sink_ld, 16)

            def norm(n):
                for b in range(NB):
                    act.wait_ge(var_ready, NB * n + b + 1)
                    src = msq[:, b:b + 1] if n < 4 else mv[:, b, 1:2]
                    act.activation(sd[:, b:b + 1], src, ACT.Sqrt,
                                   bias=eps[:, 0:1] if n < 4 else eps[:, 1:2]).then_inc(sd_ready, 1)
                if n == 9:
                    return
                for b in range(NB):
                    evacuate_norm(act, n, b, 0)

            def evacuate_norm(eng, n, b, h):
                o = tile_ready(eng, ("n", n, b, h))
                dst = mT if n == 1 else hT
                for k in range(4):
                    kt = 4 * h + k
                    g = colv[:, kt * N_VEC + n:kt * N_VEC + n + 1]
                    bias = colv[:, kt * N_VEC + V_LNB + n - 4:kt * N_VEC + V_LNB + n - 3] if n >= 4 else zeros[:, 0:1]
                    ins = act.activation(dst[:, kt, b * P:(b + 1) * P], o[:, k * P:(k + 1) * P], ACT.Identity,
                                         bias=bias, scale=g)
                ins.then_inc(frees(("n", n, b, h)), 1)

            def copy_tile(name, dst, cols=S, scale=None):
                o = tile_ready(act, name)
                if scale is None:
                    ins = act.activation(dst, o[:, 0:cols], ACT.Copy)
                else:
                    ins = act.activation(dst, o[:, 0:cols], ACT.Copy, scale=scale)
                ins.then_inc(frees(name), 1)

            act.wait_ge(angle_ready, 1)
            act.activation(trig[:], ang[:, 2:4], ACT.Sin).then_inc(trig_ready, 1)
            act.wait_ge(fills, 1)
            act.wait_ge(cols_ready, 1)
            norm(0)
            norm(1)
            for i in range(N_PROJ):
                n = min(UC, C_GATE - i * UC)
                for b in range(NB):
                    copy_tile(("p", i, b), proj[:, b, i * UC:i * UC + n], n)
            for f in range(2):
                copy_tile(("mk", f), kmT[:, f, :])
            for b in range(NB):
                copy_tile(("mv", b), vm[:, b, :])
            for i in range(-(-N_TURN // 2)):
                n = min(2, N_TURN - 2 * i)
                copy_tile(("turn", i), qkT[:, 2 * i:2 * i + n, :].rearrange("p a s -> p (a s)"), n * S)

            def exps(n):
                m = n % 2
                act.wait_ge(neg_ready, n + 1)
                if n < 2:
                    act.activation(sink_exp[:, m], sink_in[:, m], ACT.Exp)
                for k, tile in enumerate(attention(n)):
                    s = prob[:, m, k, 0:tile[2]]
                    ins = act.activation(s, s, ACT.Exp, bias=neg_max[:, m, k:k + 1], accum_out=row_sum[:, m, k:k + 1])
                ins.then_inc(exp_ready, 1)

            def copy_probs(n):
                tiles = attention(n)
                for p in range(4):
                    o = tile_ready(act, ("T", n, p))
                    if 4 * n + p >= 4:
                        act.wait_ge(pv_done, 4 * n + p - 3)
                    w = tiles[2 * p][2]
                    dst = probT[:, (4 * n + p) % 4].rearrange("p a k q -> p a (k q)")[:, :, 0:w]
                    src = o[:, :].rearrange("p (a s) -> p a s", a=2)[:, :, 0:w]
                    act.activation(dst, src, ACT.Copy).then_inc(frees(("T", n, p)), 1)

            def copy_out(n):
                act.wait_ge(pv_done, 4 * n + 4)
                if n < 2:
                    dst = oT[:, 0:4, n * P:(n + 1) * P]
                    src = o_bank[:, :].rearrange("p (j q) -> p j q", j=4)
                elif n < 4:
                    dst = oT[:, 4 + 2 * (n - 2):6 + 2 * (n - 2), :].rearrange("p a s -> p (a s)")
                    src = o_bank[:, :]
                else:
                    dst, src = oT[:, n - 4, :], o_bank[:, 0:S]
                act.activation(dst, src, ACT.Copy).then_inc(o_read, 1)

            def gate(i):
                for f in (2 * i, 2 * i + 1):
                    o = tile_ready(act, ("g", f))
                    row = (f % 8) * N_VEC + V_BG + f // 8
                    act.activation(gT[:, f, :], o[:, 0:S], ACT.Sigmoid,
                                   bias=colv[:, row:row + 1]).then_inc(frees(("g", f)), 1)

            act.wait_ge(sink_ld, 16)
            for s in MIX1:
                if s[0] == "S":
                    exps(s[1])
                elif s[0] == "G":
                    gate(s[1])
                elif s[0] == "V":
                    copy_probs(s[1])
                    copy_out(s[1])

            def hidden(first, turns, banks_of, func, cols):
                def one(wait, b):
                    act.wait_ge(tile_done, wait)
                    act.activation(act_out[:, b, 0:cols], banks[b][:, 0:cols], func).then_inc(act_ready, 1)
                seq = TILES[first][2]
                per = len(banks_of[0])
                for b in banks_of[0]:
                    one(seq + 1, b)
                    seq += 1
                body = [b for c in banks_of[1:] for b in c]
                with act.Fori(0, turns) as i:
                    for k, b in enumerate(body):
                        one(i * len(body) + (seq + k + 1), b)

            def ffn(f):
                names = [[TILES[("f", f, c, ft)][0] for ft in range(2)] for c in range(FFN_BODY + 1)]
                hidden(("f", f, 0, 0), (FFN_CHUNKS - 1) // FFN_BODY, names, ACT.Silu, S)

            norm(2)
            hidden(("m", 0), (MLP_CHUNKS - 1) // MLP_BODY,
                   [[TILES[("m", c)][0]] for c in range(MLP_BODY + 1)], ACT.Relu, 2 * S)
            norm(3)
            ffn(0)
            norm(4)
            for i in range(8):
                for b in range(NB):
                    o = tile_ready(act, ("sv", i, b))
                    act.activation(vtok[:, b, i * UC:(i + 1) * UC], o[:, 0:S], ACT.Gelu).then_inc(frees(("sv", i, b)), 1)
            for i in range(2):
                copy_tile(("wst", i), wsT[:, 4 * i:4 * i + 4, :].rearrange("p a s -> p (a s)"), 4 * P)
            for b in range(NB):
                act.wait_ge(sgu_var, b + 1)
                act.activation(sd[:, b:b + 1], mv[:, b, 1:2], ACT.Sqrt, bias=eps[:, 1:2]).then_inc(sgu_sd, 1)
            for i in range(16):
                o = tile_ready(act, ("su", i))
                act.activation(uT[:, i, :], o[:, 0:S], ACT.Gelu).then_inc(frees(("su", i)), 1)
            norm(5)
            ffn(1)
            norm(6)
            key_slot = {0: 0, 1: 1, 2: 2, 4: 3}
            for s in range(6):
                if s in (3, 5):
                    for b in range(NB):
                        copy_tile(("kv", s, b), vv[:, (s - 3) // 2, b, :])
                else:
                    for f in range(2):
                        copy_tile(("kT", s, f), ka[:, key_slot[s], f, :])
                    tile_copied(act, ("kT", s, 1))
                    for half in range(2):
                        act.dma_start(kb[64 * (1 - half):64 * (1 - half) + 64, key_slot[s]],
                                      ka[64 * half:64 * half + 64, key_slot[s]]).then_inc(k_swapped[key_slot[s]], 16)
            act.wait_ge(fills, 3)
            for s in range(2):
                o = tile_ready(act, ("ch", s))
                for m in range(2):
                    ins = act.activation(hidc[:, s, m, :, 0:N_CMP],
                                         o[:, m * HD:(m + 1) * HD].rearrange("p (g i) -> p g i", g=NG)[:, :, 0:N_CMP],
                                         ACT.Gelu, bias=colv[:, V_B1 + 2 * s + m:V_B1 + 2 * s + m + 1])
                ins.then_inc(frees(("ch", s)), 1)
            o = tile_ready(act, ("ck",))
            act.activation(kcT[:], o[:, 0:P].rearrange("p (g i) -> p g i", g=NG)[:, :, 0:16],
                           ACT.Copy).then_inc(frees(("ck",)), 1)
            copy_tile(("cv",), vc)
            ffn(2)
            norm(7)
            for b in range(NB):
                o = tile_ready(act, ("qg", b))
                act.activation(nsa_g[:, b, :], o[:, 0:48], ACT.Sigmoid).then_inc(frees(("qg", b)), 1)
            for i in range(8):
                copy_tile(("q", i), qT[:, i, :], scale=HD ** -0.5)
            for s in MIX2:
                if s[0] == "S":
                    exps(s[1])
                elif s[0] == "C":
                    for b in range(NB):
                        act.wait_ge(cscore_ready, b + 1)
                        act.activation(sc[:, :, 0:CMP_KEYS[b]], sc[:, :, 0:CMP_KEYS[b]], ACT.Exp).then_inc(cexp_ready, 1)
                    for b in range(NB):
                        o = tile_ready(act, ("ct", b))
                        act.activation(pcT[:, :, b * P:(b + 1) * P], o[:, :].rearrange("p (g q) -> p g q", g=NG),
                                       ACT.Copy).then_inc(frees(("ct", b)), 1)
                else:
                    copy_probs(s[1])
                    copy_out(s[1])
            norm(8)
            ffn(3)
            norm(9)

        @block.vector
        def _(dve):
            link = chained(dve, dve_step)

            dve.wait_ge(const_in, 16)
            dve.wait_ge(pos_in, 16)
            link(dve.tensor_copy(pos_f[:], pos_i[:]))
            for b in range(NB):
                ins = dve.tensor_scalar(ang[:, 0, b, :], freq, pos_f[:, b:b + 1], None, ALU.mult)
            link(ins)
            magic = 1.5 * 2.0 ** 23
            link(dve.tensor_scalar(ang[:, 1], ang[:, 0], 1.0 / (2 * np.pi), magic, ALU.mult, ALU.add))
            link(dve.tensor_scalar(ang[:, 1], ang[:, 1], magic, None, ALU.subtract))
            rest = 2 * np.pi
            for k in range(4):
                part = float(np.round(rest * 2.0 ** (5 + 8 * k)) / 2.0 ** (5 + 8 * k)) if k < 3 else float(np.float32(rest))
                rest -= part
                link(dve.scalar_tensor_tensor(out=ang[:, 0], in0=ang[:, 1], scalar=-part, in1=ang[:, 0],
                                              op0=ALU.mult, op1=ALU.add))
            pi = float(np.nextafter(np.float32(np.pi), np.float32(0)))
            link(dve.tensor_scalar(ang[:, 2], ang[:, 0], pi, -pi, ALU.min, ALU.max))
            link(dve.scalar_tensor_tensor(out=ang[:, 1], in0=ang[:, 2], scalar=-1.0, in1=ang[:, 2],
                                          op0=ALU.mult, op1=ALU.max))
            dve.tensor_scalar(ang[:, 3], ang[:, 1], -1.0, float(np.pi / 2), ALU.mult, ALU.add).then_inc(angle_ready, 1)

            o = tile_ready(dve, ("vec",))
            dve.tensor_copy(colv[:], o[:, 0:N_COLV]).then_inc(frees(("vec",)), 1)
            tile_copied(dve, ("vec",))
            dve.sem_inc(cols_ready, 1)
            o = tile_ready(dve, ("rel",))
            dve.tensor_copy(rel_out, o[0:NH, 0:N_REL]).then_inc(frees(("rel",)), 1)

            def norm(n):
                src = memt if n == 1 else resid
                if n == 0:
                    dve.wait_ge(x_in, 16)
                elif n == 1:
                    dve.wait_ge(mem_in, 16)
                else:
                    dve.wait_ge(unit_used, UNITS[ACC_DONE[n]] + 1)
                    if n >= 4:
                        dve.wait_ge(resid_ready, NB * (n - 3))
                for b in range(NB):
                    if n >= 2:
                        for h in range(2):
                            r = resid[:, b, h * 512:(h + 1) * 512]
                            ins = dve.scalar_tensor_tensor(out=r, in0=r, scalar=ALPHA if n >= 4 else 1.0,
                                                           in1=acc[2 * b + h][:, :], op0=ALU.mult, op1=ALU.add)
                        link(ins)
                    for h in range(2):
                        ins = dve.bn_stats(stats[:, b, h, :], src[:, b, h * 512:(h + 1) * 512])
                    link(ins)
                    ins = dve.bn_aggr(mv[:, b, :], stats[:, b, 0:2, :])
                    if n < 4:
                        link(ins)
                        ins = dve.scalar_tensor_tensor(out=msq[:, b:b + 1], in0=mv[:, b, 0:1], scalar=mv[:, b, 0:1],
                                                       in1=mv[:, b, 1:2], op0=ALU.mult, op1=ALU.add)
                    ins.then_inc(var_ready, 1)
                for b in range(NB):
                    dve.wait_ge(sd_ready, NB * n + b + 1)
                    link(dve.reciprocal(rstd[:, b:b + 1], sd[:, b:b + 1]))
                    if n == 1 and b == 0:
                        for bb in range(NB):
                            for h in range(2):
                                dve.wait_ge(tile_done, TILES[("n", 0, bb, h)][2] + 1)
                    if n < 4:
                        ins = dve.tensor_scalar(xn[:, b, :], src[:, b, :], rstd[:, b:b + 1], None, ALU.mult)
                    else:
                        dve.wait_ge(var_ready, NB * n + NB)
                        ins = dve.tensor_scalar(xn[:, b, :], src[:, b, :], mv[:, b, 0:1], rstd[:, b:b + 1],
                                                ALU.subtract, ALU.mult)
                    ins.then_inc(xn_ready, 1)
                if n == 9:
                    dve.wait_ge(gb_in, 16 * 13)
                    for b in range(NB):
                        dve.wait_ge(xn_ready, NB * n + b + 1)
                        link(dve.tensor_tensor(xn[:, b, :], xn[:, b, :], gain_bc[:], ALU.mult))
                        dve.tensor_tensor(xn[:, b, :], xn[:, b, :], bias_bc[:], ALU.add).then_inc(out_ready, 1)
                    return
                dst = mT if n == 1 else hT
                for b in range(NB):
                    o = tile_ready(dve, ("n", n, b, 1))
                    for k in range(4):
                        kt = 4 + k
                        g = colv[:, kt * N_VEC + n:kt * N_VEC + n + 1]
                        bias = colv[:, kt * N_VEC + V_LNB + n - 4:kt * N_VEC + V_LNB + n - 3] if n >= 4 else 0.0
                        ins = dve.tensor_scalar(dst[:, kt, b * P:(b + 1) * P], o[:, k * P:(k + 1) * P], g,
                                                bias if n >= 4 else None, ALU.mult, *([ALU.add] if n >= 4 else []))
                    ins.then_inc(frees(("n", n, b, 1)), 1)

            norm(0)
            norm(1)

            dve.wait_ge(trig_ready, 1)

            def rope(c0, nh, places):
                v = proj[:, :, c0:c0 + nh * HD].rearrange("p b (h e) -> p b h e", e=HD)
                x1, x2 = v[:, :, :, 0:32], v[:, :, :, 32:64]
                sin, cos = (trig[:, i].unsqueeze(2).to_broadcast([P, NB, nh, 32]) for i in range(2))
                tmp = [rope_tmp[:, i, :, 0:nh, :] for i in range(4)]
                dve.tensor_tensor(tmp[0], x1, cos, ALU.mult)
                dve.tensor_tensor(tmp[1], x2, sin, ALU.mult)
                dve.tensor_tensor(tmp[2], x2, cos, ALU.mult)
                link(dve.tensor_tensor(tmp[3], x1, sin, ALU.mult))
                for half, (a, b, op) in enumerate(((0, 1, ALU.subtract), (2, 3, ALU.add))):
                    for h0, n, dst in places:
                        ins = dve.tensor_tensor(dst[:, :, :, half * 32:half * 32 + 32], tmp[a][:, :, h0:h0 + n, :],
                                                tmp[b][:, :, h0:h0 + n, :], op)
                return ins

            def heads(tile, n):
                return roped[:, :, tile * P:tile * P + n * HD].rearrange("p b (h e) -> p b h e", e=HD)

            qs = roped[:, :, 0:4 * P].rearrange("p b (j v e) -> p b j v e", j=4, v=2)
            for b in range(NB):
                tile_copied(dve, ("p", (C_VS - 1) // UC, b))
            link(rope(C_QS, 10, [(0, 4, qs[:, :, :, 0, :]), (4, 4, qs[:, :, :, 1, :]), (8, 2, heads(T_KS, 2))]))
            for b in range(NB):
                tile_copied(dve, ("p", (C_VD - 1) // UC, b))
            kd = heads(T_KD, 2)
            link(rope(C_QD, 5, [(0, 4, heads(T_QD, 4)), (4, 1, kd[:, :, 0:1]), (4, 1, kd[:, :, 1:2])]))
            for b in range(NB):
                tile_copied(dve, ("p", N_PROJ - 1, b))
            ki = heads(T_KI, 2)
            rope(C_QI, 5, [(0, 4, heads(T_QI, 4)), (4, 1, ki[:, :, 0:1]), (4, 1, ki[:, :, 1:2])]).then_inc(roped_ready, 1)
            link(dve.tensor_scalar(wsc[:], proj[:, :, C_WI:C_WI + N_IDX], N_IDX ** -0.5 * HD ** -0.5, None, ALU.mult))

            def index():
                for h in range(N_IDX):
                    n = PAIRS[("I", h)]
                    dve.wait_ge(score_done, n + 1)
                    o = score_banks[n % 3]
                    for b in range(NB):
                        w = P * (b + 1)
                        s = isc[:, b, 0:w]
                        ins = dve.tensor_scalar(idx_tmp[:, 0:w] if h else s, o[:, b * S:b * S + w], 0.0,
                                                wsc[:, b, h:h + 1], ALU.max, ALU.mult)
                        if b == 1:
                            ins.then_inc(score_read[n % 3], 1)
                            dve.wait_ge(score_read[n % 3], n // 3 + 1)
                        else:
                            link(ins)
                        if h:
                            link(dve.tensor_tensor(s, s, idx_tmp[:, 0:w], ALU.add))
                for b in range(NB):
                    w = P * (b + 1)
                    link(dve.tensor_tensor(isc[:, b, 0:w], isc[:, b, 0:w], mask_causal[:, S - w:S], ALU.add))

            def select():
                for b in range(NB):
                    w = P * (b + 1)
                    s = isc[:, b, 0:w]
                    for _ in range(TOPK // 8):
                        link(dve.max(best[:], s))
                        link(dve.match_replace(s, best[:], s, GONE))
                    link(dve.tensor_scalar(maskD[:, b, 0:w], s, GONE / 2, NEG, ALU.is_ge, ALU.mult))
                    link(dve.tensor_tensor(maskD[:, b, 0:w], maskD[:, b, 0:w], mask_causal[:, S - w:S], ALU.add))

            def maxima(n):
                m = n % 2
                if n >= 2:
                    dve.wait_ge(tile_done, TILES[("T", n - 2, 3)][2] + 1)
                tiles = attention(n)
                for p in range(4):
                    pair = PAIRS[(n, p)]
                    dve.wait_ge(score_done, pair + 1)
                    o = score_banks[pair % 3]
                    for a in range(2):
                        k = 2 * p + a
                        _, _, w, addend, scale, first = tiles[k][:6]
                        ins = dve.tensor_tensor_reduce(prob[:, m, k, 0:w], o[:, a * S:a * S + w], addend, scale, first,
                                                       ALU.add, ALU.max, row_max[:, m, k:k + 1])
                    ins.then_inc(score_read[pair % 3], 1)
                dve.wait_ge(score_read[pair % 3], pair // 3 + 1)
                ins = dve.tensor_scalar(neg_max[:, m, :], row_max[:, m, :], -1.0, None, ALU.mult)
                if n < 2:
                    link(ins)
                    ins = dve.tensor_tensor(sink_in[:, m], sinks[:], neg_max[:, m, :], ALU.add)
                ins.then_inc(neg_ready, 1)

            def normalize(n):
                m = n % 2
                dve.wait_ge(exp_ready, n + 1)
                if n < 2:
                    link(dve.tensor_tensor(row_sum[:, m, :], row_sum[:, m, :], sink_exp[:, m], ALU.add))
                link(dve.reciprocal(row_rcp[:, m], row_sum[:, m, :]))
                if n >= 4:
                    h = 2 * (n - 4)
                    r = row_rcp[:, m].rearrange("p (h b r) -> p h b r", h=2, b=NB)
                    g = nsa_g[:, :, 3 * h:3 * h + 6].rearrange("p b (h r) -> p h b r", h=2)[:, :, :, 1:3]
                    for hh in range(2):
                        ins = dve.tensor_tensor(r[:, hh], r[:, hh], g[:, hh], ALU.mult)
                    link(ins)
                for k, tile in enumerate(attention(n)):
                    s = prob[:, m, k, 0:tile[2]]
                    ins = dve.tensor_scalar(s, s, row_rcp[:, m, k:k + 1], None, ALU.mult)
                    if k % 2:
                        ins.then_inc(prob_ready, 1)

            dve.wait_ge(fills, 1)
            dve.wait_ge(sink_ld, 16)
            dve.wait_ge(rel_stored, 16)
            index()
            maxima(0)
            maxima(1)
            normalize(0)
            select()
            maxima(2)
            normalize(1)
            maxima(3)
            normalize(2)
            normalize(3)

            tile_copied(dve, ("g", 23))
            dve.wait_ge(tile_done, TILES[("T", 3, 3)][2] + 1)
            for ft in range(KT):
                mt = merge_tmp[:, ft % 2]
                o = tile_ready(dve, ("mg", ft, 0))
                dve.tensor_tensor(mt[:, 0], o[:, 0:S], gT[:, ft, :], ALU.mult)
                dve.tensor_tensor(mt[:, 1], o[:, S:2 * S], gT[:, 8 + ft, :], ALU.mult).then_inc(frees(("mg", ft, 0)), 1)
                tile_copied(dve, ("mg", ft, 0))
                o = tile_ready(dve, ("mg", ft, 1))
                link(dve.tensor_tensor(mt[:, 0], mt[:, 0], mt[:, 1], ALU.add))
                dve.tensor_tensor(mt[:, 2], o[:, 0:S], gT[:, 16 + ft, :], ALU.mult).then_inc(frees(("mg", ft, 1)), 1)
                tile_copied(dve, ("mg", ft, 1))
                dve.tensor_tensor(mergedT[:, ft, :], mt[:, 0], mt[:, 2], ALU.add).then_inc(merged_ready, 1)

            def hid_free(n):
                return UNITS[n] + 1

            def mlp():
                def one(seq_wait, b, at_hid, out_sem):
                    dve.wait_ge(act_ready, seq_wait)
                    dve.tensor_tensor(hid[:, at_hid].rearrange("p f s -> p (f s)"), act_out[:, b, :], banks[b][:, :],
                                      ALU.mult).then_inc(tile_read[b], 1)
                    return b

                b, held, _ = TILES[("m", 0)]
                one(1, b, 0, None)
                dve.wait_ge(tile_read[b], held + 1)
                dve.sem_inc(hid_ready, 1)
                with dve.Fori(0, (MLP_CHUNKS - 1) // MLP_BODY) as i:
                    for k in range(MLP_BODY):
                        b, held, _ = TILES[("m", k + 1)]
                        dve.wait_ge(unit_used, i * SLOTS + (UNITS[("mu", 1)] + 2 * k + 1 - 2 * MLP_BODY + 2))
                        one(i * MLP_BODY + (k + 2), b, (k + 1) % MLP_BODY, None)
                        dve.wait_ge(tile_read[b], i + held + 1)
                        dve.sem_inc(hid_ready, 1)

            def ffn(f):
                base = MLP_CHUNKS + f * 2 * FFN_CHUNKS

                def one(seq_wait, b, at_hid, ft):
                    dve.wait_ge(act_ready, seq_wait)
                    dve.scalar_tensor_tensor(out=hid[:, at_hid, ft, :], in0=act_out[:, b, 0:S], scalar=0.5,
                                             in1=banks[b][:, S:2 * S], op0=ALU.mult,
                                             op1=ALU.mult).then_inc(tile_read[b], 1)

                for ft in range(2):
                    b, held, _ = TILES[("f", f, 0, ft)]
                    one(base + ft + 1, b, 0, ft)
                dve.wait_ge(tile_read[b], held + 1)
                dve.sem_inc(hid_ready, 1)
                with dve.Fori(0, (FFN_CHUNKS - 1) // FFN_BODY) as i:
                    for k in range(FFN_BODY):
                        dve.wait_ge(unit_used, i * SLOTS + (UNITS[("w1", f, 1)] + 3 * k + 2 - 3 * FFN_BODY + 3 - 2))
                        for ft in range(2):
                            b, held, _ = TILES[("f", f, k + 1, ft)]
                            one(i * 2 * FFN_BODY + (base + 2 * k + ft + 3), b, (k + 1) % FFN_BODY, ft)
                        dve.wait_ge(tile_read[b], i + held + 1)
                        dve.sem_inc(hid_ready, 1)

            norm(2)
            mlp()
            norm(3)
            ffn(0)
            norm(4)
            for b in range(NB):
                tile_copied(dve, ("sv", 7, b))
                for k in range(4):
                    ins = dve.bn_stats(stats[:, b, k, :], vtok[:, b, k * 512:(k + 1) * 512])
                link(ins)
                dve.bn_aggr(mv[:, b, :], stats[:, b, :, :]).then_inc(sgu_var, 1)
            dve.wait_ge(sgu_in, 16 * 4)
            for b in range(NB):
                dve.wait_ge(sgu_sd, b + 1)
                link(dve.reciprocal(rstd[:, b:b + 1], sd[:, b:b + 1]))
                link(dve.tensor_scalar(vtok[:, b, :], vtok[:, b, :], mv[:, b, 0:1], rstd[:, b:b + 1],
                                       ALU.subtract, ALU.mult))
                link(dve.tensor_tensor(vtok[:, b, :], vtok[:, b, :], sgu_g, ALU.mult))
                dve.tensor_tensor(vtok[:, b, :], vtok[:, b, :], sgu_b, ALU.add).then_inc(v_ready, 1)
            for i in range(16):
                tile_copied(dve, ("su", i))
                o = tile_ready(dve, ("mix", i))
                dve.tensor_tensor(uT[:, i, :], uT[:, i, :], o[:, 0:S], ALU.mult).then_inc(frees(("mix", i)), 1)
            norm(5)
            ffn(1)
            norm(6)
            dve.wait_ge(fills, 3)
            for s in range(2):
                tile_copied(dve, ("kT", s, 1))
                dve.wait_ge(k_swapped[s], 32)
                for g in range(NG):
                    for odd in range(2):
                        part = slice(64 * odd, 64 * odd + 64)
                        src = (ka if g % 2 == odd else kb)[part, s, g // 2, :]
                        rows = src.rearrange("p (c j o) -> p o j c", o=2, j=8)[:, odd]
                        pe_col = colv[part, V_PE + 16 * s:V_PE + 16 * s + 16].unsqueeze(2).to_broadcast([64, 16, N_CMP])
                        for half in range(2):
                            ins = dve.tensor_tensor(cx[part, s, 8 * half:8 * half + 8, g, 0:N_CMP],
                                                    rows[:, :, half:half + N_CMP], pe_col[:, 8 * half:8 * half + 8, :],
                                                    ALU.add)
                ins.then_inc(cx_ready, 1)
            ffn(2)
            norm(7)

            dve.wait_ge(rel_back, 16)
            tile_copied(dve, ("qg", 1))
            maxima(4)
            maxima(5)
            for b in range(NB):
                w = CMP_KEYS[b]
                first = (P if b == 0 else 0) + 31
                s = sc[:, :, 0:w]
                if b:
                    dve.wait_ge(pc_ready, b)
                for half in range(2):
                    o = tile_ready(dve, ("cs", b, half))
                    dve.tensor_tensor(s[:, half::2], o[:, 0:P].rearrange("p (h i) -> p h i", i=16)[:, :, 0:w],
                                      rel[:, half::2, first:first + 16 * (w - 1) + 1:16],
                                      ALU.add).then_inc(frees(("cs", b, half)), 1)
                tile_copied(dve, ("cs", b, 1))
                link(dve.tensor_reduce(cmax[:], s, AX.X, ALU.max))
                dve.tensor_tensor(s, s, cmax[:].unsqueeze(2).to_broadcast([P, NH, w]),
                                  ALU.subtract).then_inc(cscore_ready, 1)
                dve.wait_ge(cexp_ready, b + 1)
                link(dve.tensor_reduce(csum[:], s, AX.X, ALU.add))
                link(dve.reciprocal(crcp[:], csum[:]))
                link(dve.tensor_tensor(crcp[:], crcp[:], nsa_g[:, b, :].rearrange("p (h r) -> p h r", r=3)[:, :, 0], ALU.mult))
                if b == 0:
                    link(dve.tensor_scalar(crcp[:], crcp[:], row_valid, None, ALU.mult))
                dve.tensor_tensor(pc[:, b, :, 0:w], s, crcp[:].unsqueeze(2).to_broadcast([P, NH, w]),
                                  ALU.mult).then_inc(pc_ready, 1)
            normalize(4)
            for n in range(5, N_BATCH):
                if n + 1 < N_BATCH:
                    maxima(n + 1)
                normalize(n)
            norm(8)
            ffn(3)
            norm(9)

        @block.gpsimd
        def _(pool):
            link = chained(pool, pool_step)
            pool.memset(zeros[:], 0.0)
            pool.memset(ones[:], 1.0)
            pool.memset(eps[:, 0:1], RMS_EPS)
            link(pool.memset(eps[:, 1:2], LN_EPS))
            pool.memset(rel_rows[32:33, :], NEG).then_inc(fills, 1)

            def load_rows(n):
                if n == 3:
                    pool.dma_start(gain_bc[:], t["g_final"].partition_broadcast(P)).then_inc(gb_in, 16)
                else:
                    l, j = (n - 4) // 3, (n - 4) % 3
                    pool.dma_start(gain_bc[:], t["ln_g_2"][l, j].partition_broadcast(P)).then_inc(gb_in, 16)
                    pool.dma_start(bias_bc[:], t["ln_b_2"][l, j].partition_broadcast(P)).then_inc(gb_in, 16)

            def residual(n):
                pool.wait_ge(gb_in, 16 * (1 + 2 * (n - 3)))
                for b in range(NB):
                    pool.wait_ge(xn_ready, NB * n + b + 1)
                    ins = pool.tensor_tensor(resid[:, b, :], xn[:, b, :], gain_bc[:], ALU.mult)
                    if n > 3:
                        link(ins)
                        ins = pool.tensor_tensor(resid[:, b, :], resid[:, b, :], bias_bc[:], ALU.add)
                    ins.then_inc(resid_ready, 1)
                pool.wait_ge(resid_ready, NB * (n - 2))
                load_rows(n + 1)

            load_rows(3)
            tile_copied(pool, ("rel",))
            pool.dma_start(rel_dram.ap(), rel_out.unsqueeze(1).to_broadcast([NH, P, N_REL])).then_inc(rel_stored, 16)
            residual(3)
            pool.dma_start(ws, t["sgu_w_s_2"][0].rearrange("g p s -> p g s")).then_inc(sgu_in, 16)
            pool.dma_start(sgu_g, t["sgu_ln_g_2"][0].partition_broadcast(P)).then_inc(sgu_in, 16)
            pool.dma_start(sgu_b, t["sgu_ln_b_2"][0].partition_broadcast(P)).then_inc(sgu_in, 16)
            pool.dma_start(bs_row, t["sgu_b_s_2"].rearrange("a g p -> a (g p)")).then_inc(sgu_in, 16)
            pool.wait_ge(sgu_in, 16 * 4)
            pool.affine_select(out=ws, in_=ws, compare_op=ALU.is_ge, fill=0.0, base=0,
                               pattern=[[0, GROUPS], [-1, P]], channel_multiplier=1).then_inc(ws_ready, 1)
            residual(4)
            residual(5)
            pool.wait_ge(rel_stored, 16)
            pool.dma_start(rel, bass.AP(rel_dram, P - 1, [[N_REL - 1, P], [P * N_REL, NH], [1, S]])).then_inc(rel_back, 16)
            for s in range(2):
                pool.dma_start(cw2[:, s], t["cmp_w2_2"][s].rearrange("(m p) d -> p m d", p=P)).then_inc(cw2_in, 16)
            pool.memset(hidc, 0.0)
            pool.memset(pc, 0.0).then_inc(fills, 1)
            pool.memset(cx, 0.0).then_inc(fills, 1)
            residual(6)
            residual(7)
            residual(8)


NAMES = ["x", "mem", "positions", "g_mix", "w_in", "b_gate", "sinks", "g_mem", "w_mem_kv", "w_proj_swa",
         "w_proj_dsa", "w_proj_mem", "w_out", "g_mlp", "w_mlp_in", "w_mlp_out", "g_final", "rel_table_2",
         "ln_g_2", "ln_b_2", "ffn_w1_2", "ffn_w3_2", "ffn_w2_2", "sgu_w_in_2", "sgu_ln_g_2", "sgu_ln_b_2",
         "sgu_w_s_2", "sgu_b_s_2", "sgu_w_out_2", "kv_w_2", "cmp_pe_2", "cmp_w1_2", "cmp_b1_2", "cmp_w2_2",
         "nsa_w_qg_2", "nsa_w_o_2"]


def shape_constants():
    q, k = np.arange(P)[:, None], np.arange(P)[None, :]
    consts = np.zeros((P, N_CONST), np.float32)
    consts[:, K_ID:K_ID + P] = np.eye(P)
    diag = np.where(k <= q, 0.0, NEG)
    consts[:, K_SWA:K_SWA + P] = np.where(k > q, 0.0, NEG)
    consts[:, K_SWA + P:K_SWA + S] = diag
    consts[:, K_CAUSAL + P:K_CAUSAL + S] = diag
    half = np.arange(32, dtype=np.float32)
    consts[:, K_FREQ:K_FREQ + 32] = np.power(np.float32(10000.0), -half / np.float32(32))
    consts[:, K_ROW] = np.arange(P) >= 31
    dist = 2 * P - 1 - np.arange(N_REL)
    n = np.maximum(dist, 1).astype(np.float32)
    large = 16 + (np.log(n / np.float32(16)) / np.float32(np.log(128 / 16)) * np.float32(16)).astype(np.int32)
    bucket = np.where(dist < 16, np.maximum(dist, 0), np.minimum(large, 31))
    onehot = np.zeros((33, N_REL), np.float32)
    onehot[np.where(dist >= 0, bucket, 32), np.arange(N_REL)] = 1.0
    return consts, onehot


def kernel(**inputs):
    import concourse.bacc as bacc
    from concourse.bass_utils import run_bass_kernel_spmd

    nc = bacc.Bacc("TRN2", target_bir_lowering=False, num_devices=1)
    arrays, t = {}, {}
    consts, onehot = shape_constants()
    given = [(n, inputs[n]) for n in NAMES] + [("consts", consts), ("onehot", onehot)]
    for name, a in given:
        a = np.ascontiguousarray(a)
        arrays[f"in_{name}"] = a
        t[name] = nc.dram_tensor(f"in_{name}", a.shape, mybir.dt.from_np(a.dtype), kind="ExternalInput").ap()
    out = nc.dram_tensor("out_0", (1, S, D), F32, kind="ExternalOutput").ap()
    two_blocks(nc, t, out)
    r = run_bass_kernel_spmd(nc, [arrays], core_ids=[0])
    return r.results[0]["out_0"]
```

```python
from contextlib import ExitStack

import numpy as np

import concourse.bass as bass
from concourse import mybir

F32 = mybir.dt.float32
I32 = mybir.dt.int32
BF16 = mybir.dt.bfloat16
F32R = mybir.dt.float32r
ACT = mybir.ActivationFunctionType
ALU = mybir.AluOpType
AX = mybir.AxisListType

P = 128
S = 256
NB = S // P
D = 1024
KT = D // P
HD = 64
UNIT = 2048
UC = UNIT // KT
SLOTS = 3
SPLIT = 3
AHEAD = SLOTS - 1
PROBS = 3
BODY = 6
NEG = -1e30
GONE = -3e38
RMS_EPS, LN_EPS = 1e-6, 1e-5
ALPHA = (2.0 * 2) ** 0.25

C_QS, C_KS, C_VS, C_QD, C_KD, C_VD, C_QI, C_KI, C_WI, C_QM, C_GATE = (
    0, 512, 640, 768, 1024, 1088, 1152, 1408, 1472, 1476, 1732)
N_PROJ = -(-C_GATE // UC)
N_IDX = 4
TOPK = min(256, S // 4)
T_QS, T_KS, T_QD, T_KD, T_QI, T_KI, T_QM, N_TURN = 0, 4, 5, 7, 8, 10, 11, 13
R_COLS = T_QM * P

MLP_CHUNKS = 4 * D // UC
FFN = 2816
FFN_CHUNKS = FFN // UC
SGU = 2048
GROUPS = 8
NH, NG = 16, 4
N_CMP = S // 16 - 1
CMP_KEYS = [sum(16 * n + 31 <= (b + 1) * P - 1 for n in range(N_CMP)) for b in range(NB)]
N_REL = 2 * P + P - 1
N_FFN = 4
MLP_BODY, FFN_BODY = 3, 2
V_GMIX, V_GMEM, V_GMLP, V_GFIN, V_LNG, V_LNB, V_BG, N_VEC = 0, 1, 2, 3, 4, 10, 16, 19
V_B1, V_PE, N_COLV = KT * N_VEC, KT * N_VEC + 4, KT * N_VEC + 4 + 32
K_ID, K_SWA, K_CAUSAL, K_FREQ, K_ROW, N_CONST = 0, 128, 384, 640, 672, 673


def plan_units():
    u = [("proj", i) for i in range(N_PROJ)] + [("memkv", i) for i in range(2)]
    u += [("gate", i) for i in range(12)]
    u += [("pswa", 0), ("pdm", 0), ("pswa", 1), ("pdm", 1)]
    u += [("wout", i) for i in range(4)]
    u += [("mu", 0)]
    for c in range(1, MLP_CHUNKS):
        u += [("mu", c), ("md", c - 1)]
    u += [("md", MLP_CHUNKS - 1)]

    def ffn(f):
        out = [("w1", f, 0), ("w3", f, 0)]
        for c in range(1, FFN_CHUNKS):
            out += [("w1", f, c), ("w3", f, c), ("w2", f, c - 1)]
        return out + [("w2", f, FFN_CHUNKS - 1)]

    u += ffn(0)
    u += [("sv", i) for i in range(8)] + [("su", i) for i in range(8)] + [("so", i) for i in range(8)]
    u += ffn(1)
    u += [("kv", i) for i in range(6)] + [("cw", i) for i in range(4)]
    u += ffn(2)
    u += [("qg", 0)] + [("q", i) for i in range(4)] + [("wo", i) for i in range(4)]
    u += ffn(3)
    return u


N_BATCH = 4 + NH // 2
MIX1 = [("I",), ("S", 0), ("S", 1), ("G", 0), ("G", 1), ("G", 2), ("V", 0), ("S", 2), ("G", 3), ("G", 4),
        ("V", 1), ("S", 3), ("G", 5), ("G", 6), ("G", 7), ("V", 2), ("G", 8), ("G", 9), ("G", 10),
        ("G", 11), ("V", 3)]
MIX2 = [("C",), ("S", 4), ("S", 5), ("P",), ("S", 6)]
for _n in range(4, N_BATCH):
    MIX2 += [("V", _n)] + ([("S", _n + 3)] if _n + 3 < N_BATCH else [])


def plan_tiles():
    names = [("vec",), ("rel",)]

    def norm(n):
        return [("n", n, b, h) for b in range(NB) for h in range(2)]

    def ffn(f):
        return [("f", f, c, t) for c in range(FFN_CHUNKS) for t in range(2)]

    def mix(steps):
        out = []
        for s in steps:
            if s[0] == "G":
                out += [("g", 2 * s[1]), ("g", 2 * s[1] + 1)]
            elif s[0] == "V":
                out += [("T", s[1], p) for p in range(4)]
            elif s[0] == "C":
                out += [("cs", b, half) for b in range(NB) for half in range(2)]
            elif s[0] == "P":
                out += [("ct", b) for b in range(NB)]
        return out

    names += norm(0) + norm(1)
    names += [("p", i, b) for i in range(N_PROJ) for b in range(NB)]
    names += [("mk", f) for f in range(2)] + [("mv", b) for b in range(NB)]
    names += [("turn", i) for i in range(-(-N_TURN // 2))]
    names += mix(MIX1)
    names += [("mg", ft, x) for ft in range(KT) for x in range(2)]
    names += norm(2)
    names += [("m", c) for c in range(MLP_CHUNKS)]
    names += norm(3) + ffn(0) + norm(4)
    names += [("sv", i, b) for i in range(8) for b in range(NB)] + [("wst", i) for i in range(2)]
    names += [("su", i) for i in range(16)] + [("mix", i) for i in range(16)]
    names += norm(5) + ffn(1) + norm(6)
    names += [("kT", s, f) for s in (0, 1) for f in range(2)] + [("kT", 2, f) for f in range(2)]
    names += [("kv", 3, b) for b in range(NB)] + [("kT", 4, f) for f in range(2)] + [("kv", 5, b) for b in range(NB)]
    names += [("ch", s) for s in range(2)] + [("ck",), ("cv",)]
    names += ffn(2) + norm(7)
    names += [("qg", b) for b in range(NB)] + [("q", i) for i in range(8)]
    names += mix(MIX2) + norm(8) + ffn(3) + norm(9)
    held, out, turn = [0] * 4, {}, 0
    for seq, name in enumerate(names):
        if name[0] == "m":
            bank = name[1] % MLP_BODY
        else:
            bank, turn = turn % 4, turn + 1
        out[name] = (bank, held[bank], seq)
        held[bank] += 1
    return out


UNITS = {name: i for i, name in enumerate(plan_units())}
SPLITS = {name: i for i, name in enumerate(
    n for n in plan_units() if n[0] in ("mu", "md", "w1", "w3", "w2", "sv", "su", "so", "kv"))}
ORDER = plan_units()


def arrival(u):
    held = [ORDER[j][0] for j in range(u % SLOTS, u + 1, SLOTS)]
    return 16 * (len(held) + held.count("pdm"))


PLAIN_NORMS = (0, 1, 7)
TILES = plan_tiles()
ACC_DONE = {2: ("wout", 3), 3: ("md", MLP_CHUNKS - 1), 4: ("w2", 0, FFN_CHUNKS - 1), 5: ("so", 7),
            6: ("w2", 1, FFN_CHUNKS - 1), 7: ("w2", 2, FFN_CHUNKS - 1), 8: ("wo", 3),
            9: ("w2", 3, FFN_CHUNKS - 1)}
PAIRS = {}
for _s in MIX1 + MIX2:
    if _s[0] == "I":
        PAIRS.update({("I", h): len(PAIRS) + h for h in range(N_IDX)})
    if _s[0] == "S":
        PAIRS.update({(_s[1], p): len(PAIRS) + p for p in range(4)})


def two_blocks(nc, t, out):
    ctx = ExitStack()
    with ctx:
        def sb(name, shape, dt=F32):
            return ctx.enter_context(nc.sbuf_tensor(name, shape, dt))

        def sem(name):
            return ctx.enter_context(nc.semaphore(name))

        banks = [ctx.enter_context(nc.psum_tensor(f"bank{i}", [P, 512], F32)) for i in range(8)]
        acc = banks[4:8]
        score_banks = banks[4:7]
        o_bank = banks[7]

        ring = sb("ring", [P, SLOTS, UNIT])
        resid = sb("resid", [P, NB, D])
        xn = sb("xn", [P, NB, D])
        hT_hi = sb("hT_hi", [P, KT, S], F32R)
        hT_lo = sb("hT_lo", [P, KT, S], F32R)
        act_out = sb("act_out", [P, 4, 512])
        gain_bc = sb("gain_bc", [P, D])
        bias_bc = sb("bias_bc", [P, D])
        with nc.sbuf_tensor("shared_rows", [P, 3 * MLP_BODY * 512], F32) as shared_rows:
            pass
        hid = sb("hid", [P, MLP_BODY, 512])
        hid_hi = sb("hid_hi", [P, MLP_BODY, 2, S], F32R)
        hid_lo = sb("hid_lo", [P, MLP_BODY, 2, S], F32R)
        const = sb("const", [P, N_CONST])
        zeros = sb("zeros", [P, S])
        ones = sb("ones", [1, P])
        colv = sb("colv", [P, N_COLV])
        sinks = sb("sinks", [P, 8])
        eps = sb("eps", [P, 2])
        stats = sb("stats", [P, NB, 4, 6])
        mv = sb("mv", [P, NB, 2])
        msq = sb("msq", [P, NB])
        sd = sb("sd", [P, NB])
        rstd = sb("rstd", [P, NB])
        row_max = sb("row_max", [P, PROBS, 8])
        neg_max = sb("neg_max", [P, PROBS, 8])
        row_sum = sb("row_sum", [P, PROBS, 8])
        sink_in = sb("sink_in", [P, PROBS, 8])
        sink_exp = sb("sink_exp", [P, PROBS, 8])
        row_rcp = sb("row_rcp", [P, PROBS, 8])
        wsc = sb("wsc", [P, NB, N_IDX])
        best = sb("best", [P, 8])
        cmax = sb("cmax", [P, NH])
        csum = sb("csum", [P, NH])
        crcp = sb("crcp", [P, NH])
        pos_i = sb("pos_i", [P, NB], I32)
        pos_f = sb("pos_f", [P, NB])
        trig = sb("trig", [P, 2, NB, 32])
        ang = sb("ang", [P, 4, NB, 32])
        probT = act_out[:].rearrange("p a (x k q) -> p a x k q", x=2, k=2)
        hT_tmp = act_out[:].rearrange("p a (x s) -> p (a x) s", x=2)

        arena = sb("arena", [P, 14336])

        def take(at, *shape, of=None):
            n = int(np.prod(shape))
            a = (arena if of is None else of)[:, at[0]:at[0] + n]
            at[0] += n
            if len(shape) == 1:
                return a
            names = "abcd"[:len(shape)]
            return a.rearrange("p (%s) -> p %s" % (" ".join(names), " ".join(names)),
                               **{x: s for x, s in zip(names[:-1], shape[:-1])})

        with nc.sbuf_tensor("attend", [P, 2 * SPLIT * UNIT], F32) as attend:
            pass
        split = sb("split", [P, SPLIT, 2, UNIT], F32R)
        split_hi, split_lo = split[:, :, 0, :], split[:, :, 1, :]
        at = [0]
        prob = take(at, PROBS, 8, S, of=attend)
        oT = take(at, KT, S, of=attend)
        hT = take(at, KT, S, of=attend)
        shared = shared_rows[:, 0:16 * S]
        prob_all = attend[:, 0:2 * 8 * S]
        rope_tmp = prob_all[:, 0:4 * NB * 10 * 32].rearrange("p (x b h e) -> p x b h e", x=4, b=NB, h=10)
        merge_tmp = prob_all[:, 0:6 * S].rearrange("p (y x s) -> p y x s", y=2, x=3)
        idx_tmp = prob_all[:, 2048:2048 + S]
        vec_rows = prob_all[0:N_VEC, 0:D]
        pe_rows = prob_all[0:32, D:D + P]
        b1_rows = prob_all[0:4, D + P:D + 2 * P]
        rel_rows = prob_all[0:33, 1536:1536 + NH]
        onehot = prob_all[0:33, 2048:2048 + N_REL]
        rel_out = prob_all[0:NH, 2560:2560 + N_REL]

        at = [0]
        proj = take(at, NB, C_GATE)
        qkT = take(at, N_TURN, S)
        gate_rest = take(at, 8, S)
        mT = take(at, KT, S)
        kmT = take(at, 2, S)
        vm = take(at, NB, S)
        isc = take(at, NB, S)
        maskD = take(at, NB, S)
        memt = shared[:, 0:NB * D].rearrange("p (b d) -> p b d", b=NB)
        roped = shared[:, 0:NB * R_COLS].rearrange("p (b c) -> p b c", b=NB)

        def gate_tile(i):
            return shared[:, i * S:(i + 1) * S] if i < 16 else gate_rest[:, i - 16, :]

        mergedT = mT
        at = [0]
        vtok = take(at, NB, SGU)
        uT = take(at, 16, S)
        ws = uT[:, 0:4, :].rearrange("p a s -> p (a s)").rearrange("p (g s) -> p g s", g=GROUPS)
        wsT = take(at, GROUPS, P)
        sgu_g = take(at, SGU)
        sgu_b = take(at, SGU)
        bs_row = take(at, D)[0:1, :]
        at = [0]
        rel = shared.rearrange("p (h s) -> p h s", h=NH)
        ka = take(at, 4, 2, S)
        kb = take(at, 4, 2, S)
        vv = take(at, 2, NB, S)
        qT = take(at, 8, S)
        cx = take(at, 2, 16, NG, 16)
        hidc = take(at, 2, 2, NG, 32)
        kcT = take(at, NG, 16)
        vc = take(at, S)
        pc = take(at, NB, NH, 32)
        pcT = take(at, NG, S)
        sc = take(at, NB, NH, 16)
        cw2 = take(at, 2, 2, HD)
        nsa_g = take(at, NB, 48)

        rel_dram = nc.dram_tensor("rel_scratch", (NH, P, N_REL), F32, kind="Internal")

        ident = const[:, K_ID:K_ID + P]
        mask_swa = const[:, K_SWA:K_SWA + S]
        mask_causal = const[:, K_CAUSAL:K_CAUSAL + S]
        freq = const[:, K_FREQ:K_FREQ + 32]
        row_valid = const[:, K_ROW:K_ROW + 1]

        arrived = [sem(f"arrived{i}") for i in range(SLOTS)]
        half_done = sem("half_done")
        unit_used = sem("unit_used")
        hi_ready = sem("hi_ready")
        split_ready = sem("split_ready")
        hT_rounded, hT_ready = sem("hT_rounded"), sem("hT_ready")
        tile_done = sem("tile_done")
        tile_read = [sem(f"tile_read{i}") for i in range(4)]
        x_in, mem_in, const_in, vec_in, rel_in, sink_ld, pos_in = (
            sem(n) for n in ("x_in", "mem_in", "const_in", "vec_in", "rel_in", "sink_ld", "pos_in"))
        fills = sem("fills")
        gb_in = sem("gb_in")
        sgu_in = sem("sgu_in")
        cw2_in = sem("cw2_in")
        rel_out_ready, rel_stored, rel_back = sem("rel_out_ready"), sem("rel_stored"), sem("rel_back")
        cols_ready = sem("cols_ready")
        var_ready, sd_ready, xn_ready, resid_ready = sem("var_ready"), sem("sd_ready"), sem("xn_ready"), sem("resid_ready")
        angle_ready, trig_ready = sem("angle_ready"), sem("trig_ready")
        roped_ready = sem("roped_ready")
        score_done = sem("score_done")
        score_read = [sem(f"score_read{i}") for i in range(3)]
        neg_ready, exp_ready, prob_ready = sem("neg_ready"), sem("exp_ready"), sem("prob_ready")
        pv_done, o_read = sem("pv_done"), sem("o_read")
        merged_ready = sem("merged_ready")
        act_ready, hid_rounded, hid_ready = sem("act_ready"), sem("hid_rounded"), sem("hid_ready")
        ws_ready, sgu_var, sgu_sd, v_ready = sem("ws_ready"), sem("sgu_var"), sem("sgu_sd"), sem("v_ready")
        k_swapped = [sem(f"k_swapped{i}") for i in range(4)]
        cx_ready = sem("cx_ready")
        hidc_ready = sem("hidc_ready")
        cscore_ready, cexp_ready, pc_ready = sem("cscore_ready"), sem("cexp_ready"), sem("pc_ready")
        out_ready, stored = sem("out_ready"), sem("stored")
        dve_step, act_step, pool_step = sem("dve_step"), sem("act_step"), sem("pool_step")

        def bank_of(name):
            return banks[TILES[name][0]]

        def tile_ready(eng, name):
            eng.wait_ge(tile_done, TILES[name][2] + 1)
            return bank_of(name)

        def tile_copied(eng, name):
            eng.wait_ge(tile_read[TILES[name][0]], TILES[name][1] + 1)

        def frees(name):
            return tile_read[TILES[name][0]]

        def slot(name):
            return UNITS[name] % SLOTS

        def up_unit(name):
            return ring[:, slot(name), :].rearrange("p (k c) -> p k c", k=KT)

        def down_unit(name):
            return ring[:, slot(name), :].rearrange("p (k c) -> p k c", k=2)

        def parts(name, k):
            q = SPLITS[name] % SPLIT
            return [r[:, q, :].rearrange("p (k c) -> p k c", k=k) for r in (split_hi, split_lo)]

        def chained(eng, step):
            count = [0]

            def link(ins):
                ins.then_inc(step, 1)
                count[0] += 1
                eng.wait_ge(step, count[0])
            return link

        def attention(n):
            tiles = []
            if n < 2:
                for h in range(8):
                    kv, j = h // 4, h % 4
                    part = slice(64 * kv, 64 * kv + 64)
                    w = P * (n + 1)
                    tiles.append((qkT[part, T_QS + j, n * P:(n + 1) * P], qkT[part, T_KS, 0:w], w,
                                  mask_swa[:, S - w:S], 0.125, sinks[:, h:h + 1],
                                  [proj[:, k, C_VS + kv * HD:C_VS + (kv + 1) * HD] for k in range(n + 1)],
                                  64 * (h % 2), (h // 2) * P))
            elif n < 4:
                for b in range(NB):
                    for h in (0, 2, 1, 3):
                        part = slice(64 * (h % 2), 64 * (h % 2) + 64)
                        qs = slice(b * P, (b + 1) * P)
                        o = (64 * (h % 2), (h // 2) * S + b * P)
                        if n == 2:
                            tiles.append((qkT[part, T_QM + h // 2, qs], kmT[part, h // 2, :], S, zeros[:, :], 0.125,
                                          GONE, [vm[:, k, h * HD:(h + 1) * HD] for k in range(NB)], *o))
                        else:
                            w = P * (b + 1)
                            tiles.append((qkT[part, T_QD + h // 2, qs], qkT[part, T_KD, 0:w], w, maskD[:, b, 0:w],
                                          0.125, GONE,
                                          [proj[:, k, C_VD:C_VD + HD] for k in range(b + 1)], *o))
            else:
                for h in (2 * (n - 4), 2 * (n - 4) + 1):
                    g = h // 4
                    part = slice(64 * (h % 2), 64 * (h % 2) + 64)
                    keys = ka if h % 2 == g % 2 else kb
                    for b in range(NB):
                        w = P * (b + 1)
                        for br in range(2):
                            tiles.append((qT[part, h // 2, b * P:(b + 1) * P], keys[part, 2 + br, g // 2, 0:w], w,
                                          rel[:, h, S - w:S], 1.0, GONE,
                                          [vv[:, br, k, g * HD:(g + 1) * HD] for k in range(b + 1)],
                                          64 * (h % 2), b * P))
            return tiles

        block = ctx.enter_context(nc.Block())

        @block.sync
        def _(sp):
            sp.dma_start(resid[:], t["x"][0].rearrange("(b p) d -> p b d", p=P)).then_inc(x_in, 16)
            sp.dma_start(const[:], t["consts"]).then_inc(const_in, 16)
            sp.dma_start(memt, t["mem"][0].rearrange("(b p) d -> p b d", p=P)).then_inc(mem_in, 16)

            def up(w, c0, n=UC):
                return w.rearrange("(k p) c -> p k c", p=P)[:, :, c0:c0 + n]

            def down(w, r):
                return w.rearrange("(r k p) c -> r p k c", p=P, k=2)[r]

            w_in = t["w_in"][0]
            w1 = [t["ffn_w1_2"][f // 2, f % 2].rearrange("(k p) c -> p k c", p=P) for f in range(N_FFN)]
            w3 = [t["ffn_w3_2"][f // 2, f % 2].rearrange("(k p) c -> p k c", p=P) for f in range(N_FFN)]
            w2 = [t["ffn_w2_2"][f // 2, f % 2].rearrange("(r k p) c -> r p k c", p=P, k=2) for f in range(N_FFN)]
            mu = t["w_mlp_in"][0].rearrange("(k p) c -> p k c", p=P)
            md = t["w_mlp_out"][0].rearrange("(r k p) c -> r p k c", p=P, k=2)

            def source(name):
                kind, i = name[0], name[-1]
                return {
                    "proj": lambda: up(w_in, i * UC, min(UC, C_GATE - i * UC)),
                    "memkv": lambda: up(t["w_mem_kv"][0], i * UC),
                    "gate": lambda: up(w_in, C_GATE + i * UC),
                    "pswa": lambda: t["w_proj_swa"][0].rearrange("(k p) c -> p k c", p=P)[:, :, i * 512:(i + 1) * 512],
                    "wout": lambda: down(t["w_out"][0], i),
                    "mu": lambda: up(t["w_mlp_in"][0], i * UC),
                    "md": lambda: down(t["w_mlp_out"][0], i),
                    "w1": lambda: w1[name[1]][:, :, i * UC:(i + 1) * UC],
                    "w3": lambda: w3[name[1]][:, :, i * UC:(i + 1) * UC],
                    "w2": lambda: w2[name[1]][i],
                    "sv": lambda: up(t["sgu_w_in_2"][0], SGU + i * UC),
                    "su": lambda: up(t["sgu_w_in_2"][0], i * UC),
                    "so": lambda: down(t["sgu_w_out_2"][0], i),
                    "kv": lambda: up(t["kv_w_2"], i * UC),
                    "cw": lambda: t["cmp_w1_2"][i // 2].rearrange("(h k p) c -> h p k c", h=2, p=P)[i % 2],
                    "qg": lambda: up(t["nsa_w_qg_2"][0], D, 48),
                    "q": lambda: up(t["nsa_w_qg_2"][0], i * UC),
                    "wo": lambda: down(t["nsa_w_o_2"][0], i),
                }[kind]()

            def load(name):
                u = UNITS[name]
                if name[0] == "pdm":
                    sp.wait_ge(unit_used, u - SLOTS + 1)
                    for j, w in enumerate((t["w_proj_dsa"][0], t["w_proj_mem"][0])):
                        sp.dma_start(ring[:, u % SLOTS, j * D:(j + 1) * D].rearrange("p (k c) -> p k c", k=2),
                                     w.rearrange("(k p) c -> p k c", p=P)[:, :, name[1] * 512:(name[1] + 1) * 512]
                                     ).then_inc(arrived[u % SLOTS], 16)
                    return
                src = source(name)
                n = src.shape[1] * src.shape[2]
                dst = ring[:, u % SLOTS, 0:n].rearrange("p (k c) -> p k c", k=src.shape[1])
                if u >= SLOTS:
                    held = ORDER[u - SLOTS]
                    if held in SPLITS:
                        sp.wait_ge(split_ready, AHEAD + SPLITS[held] + 1)
                    else:
                        sp.wait_ge(unit_used, u - SLOTS + 1)
                sp.dma_start(dst, src).then_inc(arrived[u % SLOTS], 16)

            def load_loop(first, turns, sources):
                u, q = UNITS[first], SPLITS[first]
                plain = [n for n in ORDER[u - SLOTS:u] if n not in SPLITS]
                if plain:
                    sp.wait_ge(unit_used, UNITS[plain[-1]] + 1)
                with sp.Fori(0, turns) as i:
                    for k, src in enumerate(sources):
                        s = (u + k) % SLOTS
                        view = src(i)
                        dst = ring[:, s, :].rearrange("p (k c) -> p k c", k=view.shape[1])
                        split = sp.snap(i * BODY + (AHEAD + q + k - SLOTS + 1))
                        sp.wait_ge(split_ready, split)
                        sp.dma_start(dst, view).then_inc(arrived[s], 16)

            def column(w, c):
                return lambda i: w[:, :, bass.ds(sp.snap(i * (c[0] * UC) + c[1] * UC), UC)]

            def rows(w, c):
                return lambda i: w[bass.ds(sp.snap(i * c[0] + c[1]), 1)].rearrange("r p k c -> (r p) k c")

            def ffn(f):
                load(("w1", f, 0))
                load(("w3", f, 0))
                body = []
                for k in range(FFN_BODY):
                    body += [column(w1[f], (FFN_BODY, k + 1)), column(w3[f], (FFN_BODY, k + 1)),
                             rows(w2[f], (FFN_BODY, k))]
                load_loop(("w1", f, 1), (FFN_CHUNKS - 1) // FFN_BODY, body)
                load(("w2", f, FFN_CHUNKS - 1))

            def some(kind, n):
                for i in range(n):
                    load((kind, i))

            some("proj", N_PROJ)
            some("memkv", 2)
            some("gate", 12)
            for half in range(2):
                load(("pswa", half))
                load(("pdm", half))
            some("wout", 4)
            load(("mu", 0))
            body = []
            for k in range(MLP_BODY):
                body += [column(mu, (MLP_BODY, k + 1)), rows(md, (MLP_BODY, k))]
            load_loop(("mu", 1), (MLP_CHUNKS - 1) // MLP_BODY, body)
            load(("md", MLP_CHUNKS - 1))
            ffn(0)
            some("sv", 8)
            some("su", 8)
            some("so", 8)
            ffn(1)
            some("kv", 6)
            some("cw", 4)
            ffn(2)
            load(("qg", 0))
            some("q", 4)
            some("wo", 4)
            ffn(3)
            for b in range(NB):
                sp.wait_ge(out_ready, b + 1)
                sp.dma_start(out[0, b * P:(b + 1) * P, :], xn[:, b, :]).then_inc(stored, 16)
            sp.wait_ge(stored, 16 * NB)

        @block.tensor
        def _(pe):
            owed = [0]

            def mm(o, lhsT, rhs, start, stop):
                ins = pe.matmul(o, lhsT, rhs, start=start, stop=stop)
                return ins

            def settle(ins):
                if owed[0]:
                    ins.then_inc(unit_used, owed[0])
                    owed[0] = 0

            def open_tile(name):
                b, held, _ = TILES[name]
                if held:
                    pe.wait_ge(tile_read[b], held)
                return banks[b]

            def have(name):
                if name in SPLITS:
                    pe.wait_ge(split_ready, AHEAD + SPLITS[name] + 1)
                else:
                    u = UNITS[name]
                    pe.wait_ge(arrived[u % SLOTS], arrival(u))

            def turn(o, a, n=P):
                return pe.transpose(o, a, ident[0:n, 0:n])

            def up_T(o, unit, c0, n, act, w=S):
                for k in range(KT):
                    ins = mm(o, unit[:, k, c0:c0 + n], act[:, k, 0:w], k == 0, k == KT - 1)
                    if k == 0:
                        settle(ins)
                return ins

            def up_tok(o, unit, n, act, b):
                for k in range(KT):
                    ins = mm(o, act[:, k, b * P:(b + 1) * P], unit[:, k, 0:n], k == 0, k == KT - 1)
                    if k == 0:
                        settle(ins)
                return ins

            def passes(k, last):
                return ((0, 0, k == 0, False), (0, 1, False, False), (1, 0, False, k == last))

            def up_T_split(o, unit, c0, n, norm=None):
                for k in range(KT):
                    if norm and k % 4 == 0:
                        normed(norm, k // 4)
                    for w, a, start, stop in passes(k, KT - 1):
                        ins = mm(o, unit[w][:, k, c0:c0 + n], (hT_hi, hT_lo)[a][:, k, :], start, stop)
                        if start:
                            settle(ins)
                return ins

            def up_tok_split(o, unit, n, b, norm=None):
                for k in range(KT):
                    if norm and k % 4 == 0:
                        normed(norm, k // 4)
                    for w, a, start, stop in passes(k, KT - 1):
                        ins = mm(o, (hT_hi, hT_lo)[a][:, k, b * P:(b + 1) * P], unit[w][:, k, 0:n], start, stop)
                        if start:
                            settle(ins)
                return ins

            def down_split(unit, at_hid, last=False):
                for b in range(NB):
                    for k in range(2):
                        for w, a, _, stop in passes(k, 1):
                            for h in range(2):
                                ins = mm(acc[b * 2 + h][:, :], (hid_hi, hid_lo)[a][:, at_hid, k, b * P:(b + 1) * P],
                                         unit[w][:, k, h * 512:(h + 1) * 512], False, last and stop)
                                if k == 0 and b == 0 and h == 0:
                                    settle(ins)
                    if last and b == 0:
                        ins.then_inc(half_done, 1)
                ins.then_inc(unit_used, 1)

            def down_tiles(unit, act, first, last):
                for b in range(NB):
                    for k in range(2):
                        for h in range(2):
                            ins = mm(acc[b * 2 + h][:, :], act(k, b), unit[:, k, h * 512:(h + 1) * 512],
                                     first and k == 0, last and k == 1)
                            if k == 0 and b == 0 and h == 0:
                                settle(ins)
                    if last and b == 0:
                        ins.then_inc(half_done, 1)
                ins.then_inc(unit_used, 1)

            def norm(n):
                for b in range(NB):
                    pe.wait_ge(xn_ready, NB * n + b + 1)
                    for h in range(2):
                        o = open_tile(("n", n, b, h))
                        for k in range(4):
                            ins = turn(o[:, k * P:(k + 1) * P], xn[:, b, (h * 4 + k) * P:(h * 4 + k + 1) * P])
                            if k == 0:
                                settle(ins)
                        ins.then_inc(tile_done, 1)

            def normed(n, half=1):
                if n not in PLAIN_NORMS:
                    m = sum(j not in PLAIN_NORMS for j in range(n))
                    pe.wait_ge(hT_ready, 4 * m + 3 + half)
                    return
                for b in range(NB):
                    for h in range(2):
                        tile_copied(pe, ("n", n, b, h))

            pe.wait_ge(const_in, 16)
            pe.wait_ge(vec_in, 16 * 9)
            o = open_tile(("vec",))
            for k in range(KT):
                turn(o[:, k * N_VEC:(k + 1) * N_VEC], vec_rows[:, k * P:(k + 1) * P], N_VEC)
            turn(o[:, V_B1:V_B1 + 4], b1_rows, 4)
            turn(o[:, V_PE:V_PE + 32], pe_rows, 32).then_inc(tile_done, 1)
            pe.wait_ge(rel_in, 32)
            pe.wait_ge(fills, 1)
            o = open_tile(("rel",))
            mm(o[0:NH, 0:N_REL], rel_rows, onehot, True, True).then_inc(tile_done, 1)

            norm(0)
            norm(1)
            normed(0)
            for i in range(N_PROJ):
                have(("proj", i))
                n = min(UC, C_GATE - i * UC)
                unit = ring[:, slot(("proj", i)), 0:KT * n].rearrange("p (k c) -> p k c", k=KT)
                for b in range(NB):
                    o = open_tile(("p", i, b))
                    up_tok(o[:, 0:n], unit, n, hT, b).then_inc(tile_done, 1)
                owed[0] += 1
            normed(1)
            have(("memkv", 0))
            for f in range(2):
                o = open_tile(("mk", f))
                up_T(o[:, 0:S], up_unit(("memkv", 0)), f * P, P, mT).then_inc(tile_done, 1)
            owed[0] += 1
            have(("memkv", 1))
            for b in range(NB):
                o = open_tile(("mv", b))
                up_tok(o[:, 0:S], up_unit(("memkv", 1)), S, mT, b).then_inc(tile_done, 1)
            owed[0] += 1
            pe.wait_ge(roped_ready, 1)
            for i in range(-(-N_TURN // 2)):
                o = open_tile(("turn", i))
                for j in range(2 * i, min(2 * i + 2, N_TURN)):
                    for b in range(NB):
                        src = roped[:, b, j * P:(j + 1) * P] if j < T_QM else \
                            proj[:, b, C_QM + (j - T_QM) * P:C_QM + (j - T_QM + 1) * P]
                        ins = turn(o[:, ((j % 2) * NB + b) * P:((j % 2) * NB + b + 1) * P], src)
                        settle(ins)
                ins.then_inc(tile_done, 1)
            for i in range(-(-N_TURN // 2)):
                tile_copied(pe, ("turn", i))
            tile_copied(pe, ("mk", 1))
            tile_copied(pe, ("mv", 1))

            def open_pair(key):
                n = PAIRS[key]
                if n >= 3:
                    pe.wait_ge(score_read[n % 3], n // 3)
                return score_banks[n % 3]

            def index_scores():
                for h in range(N_IDX):
                    o = open_pair(("I", h))
                    part = slice(64 * (h % 2), 64 * (h % 2) + 64)
                    for b in range(NB):
                        w = P * (b + 1)
                        ins = mm(o[:, b * S:b * S + w], qkT[part, T_QI + h // 2, b * P:(b + 1) * P],
                                 qkT[part, T_KI, 0:w], True, True)
                    ins.then_inc(score_done, 1)

            def scores(n):
                tiles = attention(n)
                for p in range(4):
                    o = open_pair((n, p))
                    for a in range(2):
                        q, k, w = tiles[2 * p + a][:3]
                        ins = mm(o[:, a * S:a * S + w], q, k, True, True)
                    ins.then_inc(score_done, 1)

            def turn_probs(n, p):
                tiles = attention(n)
                o = open_tile(("T", n, p))
                pe.wait_ge(prob_ready, 4 * n + p + 1)
                for a in range(2):
                    for k in range(tiles[2 * p + a][2] // P):
                        ins = turn(o[:, (a * 2 + k) * P:(a * 2 + k + 1) * P],
                                   prob[:, n % PROBS, 2 * p + a, k * P:(k + 1) * P])
                        settle(ins)
                ins.then_inc(tile_done, 1)

            def values(n, p):
                tiles = attention(n)
                if p == 0 and n:
                    pe.wait_ge(o_read, n)
                tile_copied(pe, ("T", n, p))
                for a in range(2):
                    _, _, w, _, _, _, v, part, col = tiles[2 * p + a]
                    o = o_bank[part:part + 64, col:col + P]
                    if n >= 4 and a == 0:
                        h, b = 2 * (n - 4) + p // 2, p % 2
                        r = slice(32 * (h % 4), 32 * (h % 4) + 32)
                        mm(o, vc[r, (h // 4) * HD:(h // 4 + 1) * HD], pcT[r, h // 4, b * P:(b + 1) * P], True, False)
                    for k in range(w // P):
                        first = k == 0 and n < 4
                        last = k == w // P - 1 and (n < 4 or a == 1)
                        ins = mm(o, v[k], probT[:, (4 * n + p) % 4, a, k, :], first, last)
                ins.then_inc(pv_done, 1)

            def batch_values(n):
                for p in range(4):
                    turn_probs(n, p)
                    if p:
                        values(n, p - 1)
                values(n, 3)

            def gate(i):
                have(("gate", i))
                for f in range(2):
                    o = open_tile(("g", 2 * i + f))
                    up_T(o[:, 0:S], up_unit(("gate", i)), f * P, P, hT).then_inc(tile_done, 1)
                owed[0] += 1

            for s in MIX1:
                if s[0] == "I":
                    index_scores()
                elif s[0] == "S":
                    scores(s[1])
                elif s[0] == "G":
                    gate(s[1])
                else:
                    batch_values(s[1])

            pe.wait_ge(o_read, 4)
            for half in range(2):
                have(("pswa", half))
                swa, dm = (ring[:, slot((n, half)), :].rearrange("p (k c) -> p k c", k=4) for n in ("pswa", "pdm"))
                for ft in range(4 * half, 4 * half + 4):
                    cols = slice((ft % 4) * P, (ft % 4 + 1) * P)
                    o = open_tile(("mg", ft, 0))
                    for k in range(4):
                        ins = mm(o[:, 0:S], swa[:, k, cols], oT[:, k, :], k == 0, k == 3)
                        settle(ins)
                    have(("pdm", half))
                    for k in range(2):
                        ins = mm(o[:, S:2 * S], dm[:, k, cols], oT[:, 6 + k, :], k == 0, k == 1)
                    ins.then_inc(tile_done, 1)
                    o = open_tile(("mg", ft, 1))
                    for k in range(2):
                        ins = mm(o[:, 0:S], dm[:, 2 + k, cols], oT[:, 4 + k, :], k == 0, k == 1)
                    ins.then_inc(tile_done, 1)
                owed[0] += 2
            pe.wait_ge(merged_ready, KT)
            for i in range(4):
                have(("wout", i))
                down_tiles(down_unit(("wout", i)), lambda k, b: mergedT[:, 2 * i + k, b * P:(b + 1) * P], i == 0, i == 3)

            def split_in_turn(first, k, i, tiles):
                q = SPLITS[first] + k
                pe.wait_ge(split_ready, i * BODY + (AHEAD + q + 1))
                return [r[:, q % SPLIT, :].rearrange("p (k c) -> p k c", k=tiles) for r in (split_hi, split_lo)]

            def clear_acc():
                nil = zeros[:, :].bitcast(BF16)
                for a in acc:
                    settle(mm(a[:, :], nil[:, 0:P], nil[:, 0:512], True, False))

            def mlp(n):
                def up_chunk(o, unit, norm=None):
                    for f in range(2):
                        ins = up_T_split(o[:, f * S:(f + 1) * S], unit, f * P, P, None if f else norm)
                    owed[0] += 1
                    ins.then_inc(tile_done, 1)

                have(("mu", 0))
                up_chunk(open_tile(("m", 0)), parts(("mu", 0), KT), n)
                clear_acc()
                with pe.Fori(0, (MLP_CHUNKS - 1) // MLP_BODY) as i:
                    for k in range(MLP_BODY):
                        b, held, _ = TILES[("m", k + 1)]
                        pe.wait_ge(tile_read[b], i + held)
                        up_chunk(banks[b], split_in_turn(("mu", 1), 2 * k, i, KT))
                        w = split_in_turn(("mu", 1), 2 * k + 1, i, 2)
                        pe.wait_ge(hid_ready, i * MLP_BODY + (k + 1))
                        down_split(w, k)
                have(("md", MLP_CHUNKS - 1))
                pe.wait_ge(hid_ready, MLP_CHUNKS)
                down_split(parts(("md", MLP_CHUNKS - 1), 2), (MLP_CHUNKS - 1) % MLP_BODY, last=True)

            def ffn(f, n):
                def up_chunk(w1, w3, open_bank, norm=None):
                    tiles = [open_bank(ft) for ft in range(2)]
                    for ft in range(2):
                        up_T_split(tiles[ft][:, 0:S], w1, ft * P, P, None if ft else norm)
                    owed[0] += 1
                    w3 = w3()
                    for ft in range(2):
                        up_T_split(tiles[ft][:, S:2 * S], w3, ft * P, P).then_inc(tile_done, 1)
                    owed[0] += 1

                def first_w3():
                    have(("w3", f, 0))
                    return parts(("w3", f, 0), KT)

                have(("w1", f, 0))
                up_chunk(parts(("w1", f, 0), KT), first_w3, lambda ft: open_tile(("f", f, 0, ft)), n)
                clear_acc()
                done = MLP_CHUNKS + f * FFN_CHUNKS + (8 if f else 0)
                with pe.Fori(0, (FFN_CHUNKS - 1) // FFN_BODY) as i:
                    for k in range(FFN_BODY):
                        w1 = split_in_turn(("w1", f, 1), 3 * k, i, KT)

                        def w3():
                            return split_in_turn(("w1", f, 1), 3 * k + 1, i, KT)

                        def open_bank(ft):
                            b, held, _ = TILES[("f", f, k + 1, ft)]
                            pe.wait_ge(tile_read[b], i + held)
                            return banks[b]
                        up_chunk(w1, w3, open_bank)
                        w2 = split_in_turn(("w1", f, 1), 3 * k + 2, i, 2)
                        pe.wait_ge(hid_ready, i * FFN_BODY + (done + k + 1))
                        down_split(w2, k)
                have(("w2", f, FFN_CHUNKS - 1))
                pe.wait_ge(hid_ready, done + FFN_CHUNKS)
                down_split(parts(("w2", f, FFN_CHUNKS - 1), 2), (FFN_CHUNKS - 1) % FFN_BODY, last=True)

            norm(2)
            mlp(2)
            norm(3)
            ffn(0, 3)
            norm(4)

            for i in range(8):
                have(("sv", i))
                for b in range(NB):
                    o = open_tile(("sv", i, b))
                    up_tok_split(o[:, 0:S], parts(("sv", i), KT), S, b, 4 if i == 0 and b == 0 else None).then_inc(tile_done, 1)
                owed[0] += 1
            pe.wait_ge(ws_ready, 1)
            for i in range(2):
                o = open_tile(("wst", i))
                for k in range(4):
                    ins = turn(o[:, k * P:(k + 1) * P], ws[:, 4 * i + k, :])
                    settle(ins)
                ins.then_inc(tile_done, 1)
            for i in range(8):
                have(("su", i))
                for f in range(2):
                    o = open_tile(("su", 2 * i + f))
                    up_T_split(o[:, 0:S], parts(("su", i), KT), f * P, P).then_inc(tile_done, 1)
                owed[0] += 1
            tile_copied(pe, ("wst", 0))
            tile_copied(pe, ("wst", 1))
            pe.wait_ge(v_ready, NB)

            def mix(ft):
                g = ft // 2
                o = open_tile(("mix", ft))
                for b in range(NB):
                    ins = mm(o[:, b * P:(b + 1) * P], vtok[:, b, ft * P:(ft + 1) * P], wsT[:, g, :], True, False)
                    settle(ins)
                    ins = mm(o[:, b * P:(b + 1) * P], ones[0:1, :], bs_row[0:1, g * P:(g + 1) * P], False, True)
                ins.then_inc(tile_done, 1)

            for ft in range(2 * MLP_BODY):
                mix(ft)
            clear_acc()
            for i in range(8):
                have(("so", i))
                pe.wait_ge(hid_ready, MLP_CHUNKS + FFN_CHUNKS + i + 1)
                down_split(parts(("so", i), 2), i % MLP_BODY, last=i == 7)
                for ft in range(2 * (i + MLP_BODY), min(2 * (i + MLP_BODY) + 2, 16)):
                    mix(ft)
            norm(5)
            ffn(1, 5)
            norm(6)
            for s in range(6):
                have(("kv", s))
                if s in (3, 5):
                    for b in range(NB):
                        o = open_tile(("kv", s, b))
                        up_tok_split(o[:, 0:S], parts(("kv", s), KT), S, b).then_inc(tile_done, 1)
                else:
                    for f in range(2):
                        o = open_tile(("kT", s, f))
                        up_T_split(o[:, 0:S], parts(("kv", s), KT), f * P, P, 6 if s == 0 and f == 0 else None).then_inc(tile_done, 1)
                owed[0] += 1
            for s in range(2):
                o = open_tile(("ch", s))
                pe.wait_ge(cx_ready, s + 1)
                for m in range(2):
                    for j in range(16):
                        if m == 0 and j % 8 == 0:
                            have(("cw", 2 * s + j // 8))
                        ins = mm(o[:, m * HD:(m + 1) * HD], up_unit(("cw", 2 * s + j // 8))[:, j % 8, m * P:(m + 1) * P],
                                 cx[:, s, j].rearrange("p g i -> p (g i)"), j == 0, j == 15)
                        settle(ins)
                ins.then_inc(tile_done, 1)
                owed[0] += 2
            pe.wait_ge(cw2_in, 32)
            tile_copied(pe, ("ch", 0))
            o = open_tile(("ck",))
            for half in range(2):
                for m in range(2):
                    ins = mm(o[half * 64:half * 64 + 64, 0:P], cw2[:, 0, m, :],
                             hidc[:, 0, m].rearrange("p g i -> p (g i)"), m == 0, m == 1)
                    settle(ins)
            ins.then_inc(tile_done, 1)
            tile_copied(pe, ("ch", 1))
            o = open_tile(("cv",))
            for r in range(4):
                for g in range(NG):
                    for m in range(2):
                        ins = mm(o[32 * r:32 * r + 32, g * HD:(g + 1) * HD], hidc[:, 1, m, g, :], cw2[:, 1, m, :],
                                 m == 0, m == 1)
            ins.then_inc(tile_done, 1)

            ffn(2, None)
            norm(7)
            normed(7)
            have(("qg", 0))
            unit = ring[:, slot(("qg", 0)), 0:KT * 48].rearrange("p (k c) -> p k c", k=KT)
            for b in range(NB):
                o = open_tile(("qg", b))
                up_tok(o[:, 0:48], unit, 48, hT, b).then_inc(tile_done, 1)
            owed[0] += 1
            for i in range(4):
                have(("q", i))
                for f in range(2):
                    o = open_tile(("q", 2 * i + f))
                    up_T(o[:, 0:S], up_unit(("q", i)), f * P, P, hT).then_inc(tile_done, 1)
                owed[0] += 1
            for i in range(8):
                tile_copied(pe, ("q", i))
            for name in (("kT", 2, 1), ("kT", 4, 1), ("kv", 5, 1), ("ck",), ("cv",)):
                tile_copied(pe, name)
            for k in (2, 3):
                pe.wait_ge(k_swapped[k], 32)

            def compressed_scores():
                for b in range(NB):
                    for half in range(2):
                        o = open_tile(("cs", b, half))
                        part = slice(64 * half, 64 * half + 64)
                        for j in range(NH // 2):
                            ins = mm(o[:, j * 16:j * 16 + CMP_KEYS[b]], qT[part, j, b * P:(b + 1) * P],
                                     kcT[part, j // 2, 0:CMP_KEYS[b]], True, True)
                            settle(ins)
                        ins.then_inc(tile_done, 1)

            def compressed_probs():
                for b in range(NB):
                    o = open_tile(("ct", b))
                    pe.wait_ge(pc_ready, b + 1)
                    for g in range(NG):
                        ins = turn(o[:, g * P:(g + 1) * P],
                                   pc[:, b, 4 * g:4 * g + 4, :].rearrange("p h i -> p (h i)"))
                    ins.then_inc(tile_done, 1)

            for s in MIX2:
                if s[0] == "S":
                    scores(s[1])
                elif s[0] == "C":
                    compressed_scores()
                elif s[0] == "P":
                    compressed_probs()
                else:
                    if s[1] == 4:
                        for b in range(NB):
                            tile_copied(pe, ("ct", b))
                    batch_values(s[1])
            pe.wait_ge(o_read, N_BATCH)
            for i in range(4):
                have(("wo", i))
                down_tiles(down_unit(("wo", i)), lambda k, b: oT[:, 2 * i + k, b * P:(b + 1) * P], i == 0, i == 3)
            norm(8)
            ffn(3, 8)

        @block.scalar
        def _(act):
            link = chained(act, act_step)
            for row, n, src in ((V_GMIX, 1, t["g_mix"]), (V_GMEM, 1, t["g_mem"]), (V_GMLP, 1, t["g_mlp"]),
                                (V_GFIN, 1, t["g_final"].rearrange("(a d) -> a d", a=1)),
                                (V_LNG, 6, t["ln_g_2"].rearrange("l n d -> (l n) d")),
                                (V_LNB, 6, t["ln_b_2"].rearrange("l n d -> (l n) d")),
                                (V_BG, 3, t["b_gate"].rearrange("a (r d) -> (a r) d", d=D))):
                act.dma_start(vec_rows[row:row + n, :], src).then_inc(vec_in, 16)
            act.dma_start(b1_rows, t["cmp_b1_2"].rearrange("s (m p) -> (s m) p", p=P)).then_inc(vec_in, 16)
            act.dma_start(pe_rows, t["cmp_pe_2"].rearrange("s (j o) d -> (s j) (o d)", o=2)).then_inc(vec_in, 16)
            act.dma_start(pos_i[:], t["positions"].rearrange("a (b p) -> p (a b)", p=P),
                          allow_slow_non_contiguous=True).then_inc(pos_in, 16)
            act.dma_start(onehot, t["onehot"]).then_inc(rel_in, 16)
            act.dma_start(rel_rows[0:32, :], t["rel_table_2"]).then_inc(rel_in, 16)
            act.dma_start(sinks[:], t["sinks"].partition_broadcast(P)).then_inc(sink_ld, 16)

            def round_unit(name, i=None, offset=0):
                u, q = UNITS[name] + offset, SPLITS[name] + offset
                turns = 0 if i is None else i * BODY
                act.wait_ge(arrived[u % SLOTS], (0 if i is None else i * (16 * BODY // SLOTS)) + arrival(u))
                act.wait_ge(unit_used, turns + (u - SPLIT + 1))
                act.activation(split_hi[:, q % SPLIT, :], ring[:, u % SLOTS, :], ACT.Copy).then_inc(hi_ready, 1)

            def norm(n):
                for b in range(NB):
                    act.wait_ge(var_ready, NB * n + b + 1)
                    src = msq[:, b:b + 1] if n < 4 else mv[:, b, 1:2]
                    act.activation(sd[:, b:b + 1], src, ACT.Sqrt,
                                   bias=eps[:, 0:1] if n < 4 else eps[:, 1:2]).then_inc(sd_ready, 1)
                if n == 9:
                    return
                for b in range(NB):
                    name = ("n", n, b, 0)
                    o = tile_ready(act, name)
                    dst = mT if n == 1 else hT if n in PLAIN_NORMS else hT_tmp
                    for kt in range(4):
                        g = colv[:, kt * N_VEC + n:kt * N_VEC + n + 1]
                        bias = colv[:, kt * N_VEC + V_LNB + n - 4:kt * N_VEC + V_LNB + n - 3] if n >= 4 else zeros[:, 0:1]
                        ins = act.activation(dst[:, kt, b * P:(b + 1) * P], o[:, kt * P:(kt + 1) * P], ACT.Identity,
                                             bias=bias, scale=g)
                    ins.then_inc(frees(name), 1)
                    if n not in PLAIN_NORMS:
                        for h in range(2):
                            tile_copied(act, ("n", n, b, h))
                            act.activation(hT_hi[:, 4 * h:4 * h + 4, b * P:(b + 1) * P],
                                           hT_tmp[:, 4 * h:4 * h + 4, b * P:(b + 1) * P], ACT.Copy).then_inc(hT_rounded, 1)

            def copy_tile(name, dst, cols=S, scale=None):
                o = tile_ready(act, name)
                if scale is None:
                    ins = act.activation(dst, o[:, 0:cols], ACT.Copy)
                else:
                    ins = act.activation(dst, o[:, 0:cols], ACT.Copy, scale=scale)
                ins.then_inc(frees(name), 1)

            act.wait_ge(angle_ready, 1)
            act.activation(trig[:], ang[:, 2:4], ACT.Sin).then_inc(trig_ready, 1)
            act.wait_ge(fills, 1)
            act.wait_ge(cols_ready, 1)
            norm(0)
            norm(1)
            for i in range(N_PROJ):
                n = min(UC, C_GATE - i * UC)
                for b in range(NB):
                    copy_tile(("p", i, b), proj[:, b, i * UC:i * UC + n], n)
            for f in range(2):
                copy_tile(("mk", f), kmT[:, f, :])
            for b in range(NB):
                copy_tile(("mv", b), vm[:, b, :])
            for i in range(-(-N_TURN // 2)):
                n = min(2, N_TURN - 2 * i)
                copy_tile(("turn", i), qkT[:, 2 * i:2 * i + n, :].rearrange("p a s -> p (a s)"), n * S)

            def exps(n):
                m = n % PROBS
                act.wait_ge(neg_ready, n + 1)
                if n < 2:
                    act.activation(sink_exp[:, m], sink_in[:, m], ACT.Exp)
                for k, tile in enumerate(attention(n)):
                    s = prob[:, m, k, 0:tile[2]]
                    ins = act.activation(s, s, ACT.Exp, bias=neg_max[:, m, k:k + 1], accum_out=row_sum[:, m, k:k + 1])
                ins.then_inc(exp_ready, 1)

            def copy_probs(n):
                tiles = attention(n)
                for p in range(4):
                    o = tile_ready(act, ("T", n, p))
                    if 4 * n + p >= 4:
                        act.wait_ge(pv_done, 4 * n + p - 3)
                    w = tiles[2 * p][2]
                    dst = probT[:, (4 * n + p) % 4].rearrange("p a k q -> p a (k q)")[:, :, 0:w]
                    src = o[:, :].rearrange("p (a s) -> p a s", a=2)[:, :, 0:w]
                    act.activation(dst, src, ACT.Copy).then_inc(frees(("T", n, p)), 1)

            def copy_out(n):
                act.wait_ge(pv_done, 4 * n + 4)
                if n < 2:
                    dst = oT[:, 0:4, n * P:(n + 1) * P]
                    src = o_bank[:, :].rearrange("p (j q) -> p j q", j=4)
                elif n < 4:
                    dst = oT[:, 4 + 2 * (n - 2):6 + 2 * (n - 2), :].rearrange("p a s -> p (a s)")
                    src = o_bank[:, :]
                else:
                    dst, src = oT[:, n - 4, :], o_bank[:, 0:S]
                act.activation(dst, src, ACT.Copy).then_inc(o_read, 1)

            def gate(i):
                for f in (2 * i, 2 * i + 1):
                    o = tile_ready(act, ("g", f))
                    row = (f % 8) * N_VEC + V_BG + f // 8
                    act.activation(gate_tile(f), o[:, 0:S], ACT.Sigmoid,
                                   bias=colv[:, row:row + 1]).then_inc(frees(("g", f)), 1)

            act.wait_ge(sink_ld, 16)
            for s in MIX1:
                if s[0] == "S":
                    exps(s[1])
                elif s[0] == "G":
                    gate(s[1])
                elif s[0] == "V":
                    copy_probs(s[1])
                    copy_out(s[1])

            def activate(b, done, func, cols):
                act.wait_ge(tile_done, done)
                act.activation(act_out[:, b, 0:cols], banks[b][:, 0:cols], func).then_inc(act_ready, 1)

            def mlp():
                first = ("mu", 1)
                seq = TILES[("m", 0)][2] + 1
                round_unit(first)
                with act.Fori(0, (MLP_CHUNKS - 1) // MLP_BODY) as i:
                    for k in range(MLP_BODY):
                        activate(TILES[("m", k)][0], i * MLP_BODY + (seq + k), ACT.Relu, 2 * S)
                        round_unit(first, i, 2 * k + 1)
                        round_unit(first, i, 2 * k + 2)
                activate(TILES[("m", MLP_CHUNKS - 1)][0], seq + MLP_CHUNKS - 1, ACT.Relu, 2 * S)

            def ffn(f):
                first = ("w1", f, 1)
                seq = TILES[("f", f, 0, 0)][2] + 1

                def silu(k, ft, i=None):
                    done = seq + 2 * k + ft
                    activate(TILES[("f", f, k, ft)][0], done if i is None else i * 2 * FFN_BODY + done, ACT.Silu, S)

                round_unit(first)
                with act.Fori(0, (FFN_CHUNKS - 1) // FFN_BODY) as i:
                    for k in range(FFN_BODY):
                        silu(k, 0, i)
                        silu(k, 1, i)
                        for j in range(3 * k + 1, 3 * k + 4):
                            round_unit(first, i, j)
                silu(FFN_CHUNKS - 1, 0)
                silu(FFN_CHUNKS - 1, 1)

            act.wait_ge(merged_ready, KT)
            round_unit(("mu", 0))
            norm(2)
            mlp()
            round_unit(("w1", 0, 0))
            norm(3)
            round_unit(("w3", 0, 0))
            ffn(0)
            mixer = [(x, i) for x in ("sv", "su", "so") for i in range(8)]
            round_unit(mixer[0])
            norm(4)
            round_unit(mixer[1])
            round_unit(mixer[2])
            for i in range(8):
                for b in range(NB):
                    o = tile_ready(act, ("sv", i, b))
                    act.activation(vtok[:, b, i * UC:(i + 1) * UC], o[:, 0:S], ACT.Gelu).then_inc(frees(("sv", i, b)), 1)
                round_unit(mixer[i + 3])
            for i in range(2):
                copy_tile(("wst", i), wsT[:, 4 * i:4 * i + 4, :].rearrange("p a s -> p (a s)"), 4 * P)
            for i in range(8):
                for f in range(2):
                    o = tile_ready(act, ("su", 2 * i + f))
                    act.activation(uT[:, 2 * i + f, :], o[:, 0:S], ACT.Gelu).then_inc(frees(("su", 2 * i + f)), 1)
                round_unit(mixer[i + 11])
                if i == 1:
                    for b in range(NB):
                        act.wait_ge(sgu_var, b + 1)
                        act.activation(sd[:, b:b + 1], mv[:, b, 1:2], ACT.Sqrt, bias=eps[:, 1:2]).then_inc(sgu_sd, 1)
            for i in range(3, 8):
                round_unit(("so", i))
            round_unit(("w1", 1, 0))
            norm(5)
            round_unit(("w3", 1, 0))
            ffn(1)
            round_unit(("kv", 0))
            norm(6)
            round_unit(("kv", 1))
            round_unit(("kv", 2))
            key_slot = {0: 0, 1: 1, 2: 2, 4: 3}
            for s in range(6):
                if s in (3, 5):
                    for b in range(NB):
                        copy_tile(("kv", s, b), vv[:, (s - 3) // 2, b, :])
                else:
                    for f in range(2):
                        copy_tile(("kT", s, f), ka[:, key_slot[s], f, :])
                    tile_copied(act, ("kT", s, 1))
                    for half in range(2):
                        act.dma_start(kb[64 * (1 - half):64 * (1 - half) + 64, key_slot[s]],
                                      ka[64 * half:64 * half + 64, key_slot[s]]).then_inc(k_swapped[key_slot[s]], 16)
                if s + 3 < 6:
                    round_unit(("kv", s + 3))
            act.wait_ge(fills, 3)
            for s in range(2):
                o = tile_ready(act, ("ch", s))
                for m in range(2):
                    ins = act.activation(hidc[:, s, m, :, 0:N_CMP],
                                         o[:, m * HD:(m + 1) * HD].rearrange("p (g i) -> p g i", g=NG)[:, :, 0:N_CMP],
                                         ACT.Gelu, bias=colv[:, V_B1 + 2 * s + m:V_B1 + 2 * s + m + 1])
                ins.then_inc(frees(("ch", s)), 1)
                round_unit((("w1", "w3")[s], 2, 0))
            o = tile_ready(act, ("ck",))
            act.activation(kcT[:], o[:, 0:P].rearrange("p (g i) -> p g i", g=NG)[:, :, 0:16],
                           ACT.Copy).then_inc(frees(("ck",)), 1)
            copy_tile(("cv",), vc)
            ffn(2)
            norm(7)
            for b in range(NB):
                o = tile_ready(act, ("qg", b))
                act.activation(nsa_g[:, b, :], o[:, 0:48], ACT.Sigmoid).then_inc(frees(("qg", b)), 1)
            for i in range(8):
                copy_tile(("q", i), qT[:, i, :], scale=HD ** -0.5)
            for s in MIX2:
                if s[0] == "S":
                    if s[1] < 6:
                        exps(s[1])
                elif s[0] == "C":
                    for b in range(NB):
                        act.wait_ge(cscore_ready, b + 1)
                        act.activation(sc[:, b, :, 0:CMP_KEYS[b]], sc[:, b, :, 0:CMP_KEYS[b]],
                                       ACT.Exp).then_inc(cexp_ready, 1)
                elif s[0] == "P":
                    for b in range(NB):
                        o = tile_ready(act, ("ct", b))
                        act.activation(pcT[:, :, b * P:(b + 1) * P], o[:, :].rearrange("p (g q) -> p g q", g=NG),
                                       ACT.Copy).then_inc(frees(("ct", b)), 1)
                else:
                    copy_probs(s[1])
                    copy_out(s[1])
                    if s[1] + 2 < N_BATCH:
                        exps(s[1] + 2)
            act.wait_ge(o_read, N_BATCH)
            round_unit(("w1", 3, 0))
            norm(8)
            round_unit(("w3", 3, 0))
            ffn(3)
            norm(9)

        @block.vector
        def _(dve):
            link = chained(dve, dve_step)

            dve.sem_inc(split_ready, AHEAD)
            dve.wait_ge(const_in, 16)
            dve.wait_ge(pos_in, 16)
            link(dve.tensor_copy(pos_f[:], pos_i[:]))
            for b in range(NB):
                ins = dve.tensor_scalar(ang[:, 0, b, :], freq, pos_f[:, b:b + 1], None, ALU.mult)
            link(ins)
            magic = 1.5 * 2.0 ** 23
            link(dve.tensor_scalar(ang[:, 1], ang[:, 0], 1.0 / (2 * np.pi), magic, ALU.mult, ALU.add))
            link(dve.tensor_scalar(ang[:, 1], ang[:, 1], magic, None, ALU.subtract))
            rest = 2 * np.pi
            for k in range(4):
                part = float(np.round(rest * 2.0 ** (5 + 8 * k)) / 2.0 ** (5 + 8 * k)) if k < 3 else float(np.float32(rest))
                rest -= part
                link(dve.scalar_tensor_tensor(out=ang[:, 0], in0=ang[:, 1], scalar=-part, in1=ang[:, 0],
                                              op0=ALU.mult, op1=ALU.add))
            pi = float(np.nextafter(np.float32(np.pi), np.float32(0)))
            link(dve.tensor_scalar(ang[:, 2], ang[:, 0], pi, -pi, ALU.min, ALU.max))
            link(dve.scalar_tensor_tensor(out=ang[:, 1], in0=ang[:, 2], scalar=-1.0, in1=ang[:, 2],
                                          op0=ALU.mult, op1=ALU.max))
            dve.tensor_scalar(ang[:, 3], ang[:, 1], -1.0, float(np.pi / 2), ALU.mult, ALU.add).then_inc(angle_ready, 1)

            o = tile_ready(dve, ("vec",))
            dve.tensor_copy(colv[:], o[:, 0:N_COLV]).then_inc(frees(("vec",)), 1)
            tile_copied(dve, ("vec",))
            dve.sem_inc(cols_ready, 1)
            o = tile_ready(dve, ("rel",))
            dve.tensor_copy(rel_out, o[0:NH, 0:N_REL]).then_inc(frees(("rel",)), 1)

            def low_unit(name, i=None, offset=0):
                u, q = UNITS[name] + offset, SPLITS[name] + offset
                dve.wait_ge(hi_ready, (0 if i is None else i * BODY) + (q + 1))
                dve.tensor_tensor(split_lo[:, q % SPLIT, :], ring[:, u % SLOTS, :],
                                  split_hi[:, q % SPLIT, :].bitcast(F32), ALU.subtract).then_inc(split_ready, 1)

            def norm(n):
                src = memt if n == 1 else resid
                if n == 0:
                    dve.wait_ge(x_in, 16)
                elif n == 1:
                    dve.wait_ge(mem_in, 16)
                elif n >= 4:
                    dve.wait_ge(resid_ready, NB * (n - 3))
                def add(b):
                    if n < 2:
                        return
                    if b == 0:
                        dve.wait_ge(half_done, n - 1)
                    else:
                        dve.wait_ge(unit_used, UNITS[ACC_DONE[n]] + 1)
                    for h in range(2):
                        r = resid[:, b, h * 512:(h + 1) * 512]
                        ins = dve.scalar_tensor_tensor(out=r, in0=r, scalar=ALPHA if n >= 4 else 1.0,
                                                       in1=acc[2 * b + h][:, :], op0=ALU.mult, op1=ALU.add)
                    link(ins)

                def variance(b):
                    for h in range(2):
                        ins = dve.bn_stats(stats[:, b, h, :], src[:, b, h * 512:(h + 1) * 512])
                    link(ins)
                    ins = dve.bn_aggr(mv[:, b, :], stats[:, b, 0:2, :])
                    if n < 4:
                        link(ins)
                        ins = dve.scalar_tensor_tensor(out=msq[:, b:b + 1], in0=mv[:, b, 0:1], scalar=mv[:, b, 0:1],
                                                       in1=mv[:, b, 1:2], op0=ALU.mult, op1=ALU.add)
                    ins.then_inc(var_ready, 1)

                def scale(b):
                    dve.wait_ge(sd_ready, NB * n + b + 1)
                    link(dve.reciprocal(rstd[:, b:b + 1], sd[:, b:b + 1]))
                    if n == 1 and b == 0:
                        for bb in range(NB):
                            for h in range(2):
                                dve.wait_ge(tile_done, TILES[("n", 0, bb, h)][2] + 1)
                    if n < 4:
                        ins = dve.tensor_scalar(xn[:, b, :], src[:, b, :], rstd[:, b:b + 1], None, ALU.mult)
                    else:
                        ins = dve.tensor_scalar(xn[:, b, :], src[:, b, :], mv[:, b, 0:1], rstd[:, b:b + 1],
                                                ALU.subtract, ALU.mult)
                    ins.then_inc(xn_ready, 1)

                add(0)
                variance(0)
                add(1)
                scale(0)
                variance(1)
                scale(1)
                if n == 9:
                    dve.wait_ge(gb_in, 16 * 13)
                    for b in range(NB):
                        dve.wait_ge(xn_ready, NB * n + b + 1)
                        link(dve.tensor_tensor(xn[:, b, :], xn[:, b, :], gain_bc[:], ALU.mult))
                        dve.tensor_tensor(xn[:, b, :], xn[:, b, :], bias_bc[:], ALU.add).then_inc(out_ready, 1)
                    return
                dst = mT if n == 1 else hT if n in PLAIN_NORMS else hT_tmp
                m = sum(j not in PLAIN_NORMS for j in range(n))
                for b in range(NB):
                    name = ("n", n, b, 1)
                    o = tile_ready(dve, name)
                    for k in range(4):
                        kt = 4 + k
                        g = colv[:, kt * N_VEC + n:kt * N_VEC + n + 1]
                        bias = colv[:, kt * N_VEC + V_LNB + n - 4:kt * N_VEC + V_LNB + n - 3] if n >= 4 else 0.0
                        ins = dve.tensor_scalar(dst[:, kt, b * P:(b + 1) * P], o[:, k * P:(k + 1) * P], g,
                                                bias if n >= 4 else None, ALU.mult, *([ALU.add] if n >= 4 else []))
                    ins.then_inc(frees(name), 1)
                    if n not in PLAIN_NORMS:
                        tile_copied(dve, name)
                        cols = slice(b * P, (b + 1) * P)
                        for h in range(2):
                            dve.wait_ge(hT_rounded, 2 * NB * m + 2 * b + h + 1)
                            ks = slice(4 * h, 4 * h + 4)
                            dve.tensor_tensor(hT_lo[:, ks, cols], hT_tmp[:, ks, cols], hT_hi[:, ks, cols].bitcast(F32),
                                              ALU.subtract).then_inc(hT_ready, 1)

            norm(0)
            norm(1)

            dve.wait_ge(trig_ready, 1)

            def rope(c0, nh, places):
                v = proj[:, :, c0:c0 + nh * HD].rearrange("p b (h e) -> p b h e", e=HD)
                x1, x2 = v[:, :, :, 0:32], v[:, :, :, 32:64]
                sin, cos = (trig[:, i].unsqueeze(2).to_broadcast([P, NB, nh, 32]) for i in range(2))
                tmp = [rope_tmp[:, i, :, 0:nh, :] for i in range(4)]
                dve.tensor_tensor(tmp[0], x1, cos, ALU.mult)
                dve.tensor_tensor(tmp[1], x2, sin, ALU.mult)
                dve.tensor_tensor(tmp[2], x2, cos, ALU.mult)
                link(dve.tensor_tensor(tmp[3], x1, sin, ALU.mult))
                for half, (a, b, op) in enumerate(((0, 1, ALU.subtract), (2, 3, ALU.add))):
                    for h0, n, dst in places:
                        ins = dve.tensor_tensor(dst[:, :, :, half * 32:half * 32 + 32], tmp[a][:, :, h0:h0 + n, :],
                                                tmp[b][:, :, h0:h0 + n, :], op)
                return ins

            def heads(tile, n):
                return roped[:, :, tile * P:tile * P + n * HD].rearrange("p b (h e) -> p b h e", e=HD)

            qs = roped[:, :, 0:4 * P].rearrange("p b (j v e) -> p b j v e", j=4, v=2)
            for b in range(NB):
                tile_copied(dve, ("p", (C_VS - 1) // UC, b))
            link(rope(C_QS, 10, [(0, 4, qs[:, :, :, 0, :]), (4, 4, qs[:, :, :, 1, :]), (8, 2, heads(T_KS, 2))]))
            for b in range(NB):
                tile_copied(dve, ("p", (C_VD - 1) // UC, b))
            kd = heads(T_KD, 2)
            link(rope(C_QD, 5, [(0, 4, heads(T_QD, 4)), (4, 1, kd[:, :, 0:1]), (4, 1, kd[:, :, 1:2])]))
            for b in range(NB):
                tile_copied(dve, ("p", N_PROJ - 1, b))
            ki = heads(T_KI, 2)
            rope(C_QI, 5, [(0, 4, heads(T_QI, 4)), (4, 1, ki[:, :, 0:1]), (4, 1, ki[:, :, 1:2])]).then_inc(roped_ready, 1)
            link(dve.tensor_scalar(wsc[:], proj[:, :, C_WI:C_WI + N_IDX], N_IDX ** -0.5 * HD ** -0.5, None, ALU.mult))

            def index():
                for h in range(N_IDX):
                    n = PAIRS[("I", h)]
                    dve.wait_ge(score_done, n + 1)
                    o = score_banks[n % 3]
                    for b in range(NB):
                        w = P * (b + 1)
                        s = isc[:, b, 0:w]
                        ins = dve.tensor_scalar(idx_tmp[:, 0:w] if h else s, o[:, b * S:b * S + w], 0.0,
                                                wsc[:, b, h:h + 1], ALU.max, ALU.mult)
                        if b == 1:
                            ins.then_inc(score_read[n % 3], 1)
                            dve.wait_ge(score_read[n % 3], n // 3 + 1)
                        else:
                            link(ins)
                        if h:
                            link(dve.tensor_tensor(s, s, idx_tmp[:, 0:w], ALU.add))
                for b in range(NB):
                    w = P * (b + 1)
                    link(dve.tensor_tensor(isc[:, b, 0:w], isc[:, b, 0:w], mask_causal[:, S - w:S], ALU.add))

            def select():
                for b in range(NB):
                    w = P * (b + 1)
                    s = isc[:, b, 0:w]
                    for _ in range(TOPK // 8):
                        link(dve.max(best[:], s))
                        link(dve.match_replace(s, best[:], s, GONE))
                    link(dve.tensor_scalar(maskD[:, b, 0:w], s, GONE / 2, NEG, ALU.is_ge, ALU.mult))
                    link(dve.tensor_tensor(maskD[:, b, 0:w], maskD[:, b, 0:w], mask_causal[:, S - w:S], ALU.add))

            def maxima(n):
                m = n % PROBS
                if n >= PROBS:
                    dve.wait_ge(tile_done, TILES[("T", n - PROBS, 3)][2] + 1)
                tiles = attention(n)
                for p in range(4):
                    pair = PAIRS[(n, p)]
                    dve.wait_ge(score_done, pair + 1)
                    o = score_banks[pair % 3]
                    for a in range(2):
                        k = 2 * p + a
                        _, _, w, addend, scale, first = tiles[k][:6]
                        ins = dve.tensor_tensor_reduce(prob[:, m, k, 0:w], o[:, a * S:a * S + w], addend, scale, first,
                                                       ALU.add, ALU.max, row_max[:, m, k:k + 1])
                    ins.then_inc(score_read[pair % 3], 1)
                dve.wait_ge(score_read[pair % 3], pair // 3 + 1)
                ins = dve.tensor_scalar(neg_max[:, m, :], row_max[:, m, :], -1.0, None, ALU.mult)
                if n < 2:
                    link(ins)
                    ins = dve.tensor_tensor(sink_in[:, m], sinks[:], neg_max[:, m, :], ALU.add)
                ins.then_inc(neg_ready, 1)

            def normalize(n):
                m = n % PROBS
                dve.wait_ge(exp_ready, n + 1)
                if n < 2:
                    link(dve.tensor_tensor(row_sum[:, m, :], row_sum[:, m, :], sink_exp[:, m], ALU.add))
                link(dve.reciprocal(row_rcp[:, m], row_sum[:, m, :]))
                if n >= 4:
                    h = 2 * (n - 4)
                    r = row_rcp[:, m].rearrange("p (h b r) -> p h b r", h=2, b=NB)
                    g = nsa_g[:, :, 3 * h:3 * h + 6].rearrange("p b (h r) -> p h b r", h=2)[:, :, :, 1:3]
                    for hh in range(2):
                        ins = dve.tensor_tensor(r[:, hh], r[:, hh], g[:, hh], ALU.mult)
                    link(ins)
                for k, tile in enumerate(attention(n)):
                    s = prob[:, m, k, 0:tile[2]]
                    ins = dve.tensor_scalar(s, s, row_rcp[:, m, k:k + 1], None, ALU.mult)
                    if k % 2:
                        ins.then_inc(prob_ready, 1)

            dve.wait_ge(fills, 1)
            dve.wait_ge(sink_ld, 16)
            dve.wait_ge(rel_stored, 16)
            index()
            maxima(0)
            maxima(1)
            normalize(0)
            select()
            maxima(2)
            normalize(1)
            maxima(3)
            normalize(2)
            normalize(3)

            tile_copied(dve, ("g", 23))
            dve.wait_ge(tile_done, TILES[("T", 3, 3)][2] + 1)
            for ft in range(KT):
                mt = merge_tmp[:, ft % 2]
                o = tile_ready(dve, ("mg", ft, 0))
                dve.tensor_tensor(mt[:, 0], o[:, 0:S], gate_tile(ft), ALU.mult)
                dve.tensor_tensor(mt[:, 1], o[:, S:2 * S], gate_tile(8 + ft), ALU.mult).then_inc(frees(("mg", ft, 0)), 1)
                tile_copied(dve, ("mg", ft, 0))
                o = tile_ready(dve, ("mg", ft, 1))
                link(dve.tensor_tensor(mt[:, 0], mt[:, 0], mt[:, 1], ALU.add))
                dve.tensor_tensor(mt[:, 2], o[:, 0:S], gate_tile(16 + ft), ALU.mult).then_inc(frees(("mg", ft, 1)), 1)
                tile_copied(dve, ("mg", ft, 1))
                dve.tensor_tensor(mergedT[:, ft, :], mt[:, 0], mt[:, 2], ALU.add).then_inc(merged_ready, 1)

            def split_hidden(tile, at_hid):
                raw, hi, lo = (x.rearrange("p f s -> p (f s)") if len(x.shape) == 3 else x for x in at_hid)
                dve.tensor_copy(hi, raw).then_inc(hid_rounded, 1)
                dve.wait_ge(hid_rounded, tile)
                return dve.tensor_tensor(lo, raw, hi.bitcast(F32), ALU.subtract)

            def mlp():
                first = ("mu", 1)

                def hidden(c, i=None):
                    t0, t6 = (0, 0) if i is None else (i * MLP_BODY, i * BODY)
                    b, held, _ = TILES[("m", c)]
                    x = c % MLP_BODY
                    dve.wait_ge(unit_used, t6 + (UNITS[first] - 2 * MLP_BODY + 2 + 2 * c))
                    dve.wait_ge(act_ready, t0 + (c + 1))
                    dve.tensor_tensor(hid[:, x, :], act_out[:, b, :], banks[b][:, :], ALU.mult).then_inc(tile_read[b], 1)
                    dve.wait_ge(tile_read[b], (0 if i is None else i) + (held + 1))
                    split_hidden(t0 + (c + 1), (hid[:, x, :], hid_hi[:, x], hid_lo[:, x])).then_inc(hid_ready, 1)

                with dve.Fori(0, (MLP_CHUNKS - 1) // MLP_BODY) as i:
                    for k in range(MLP_BODY):
                        low_unit(first, i, 2 * k)
                        hidden(k, i)
                        low_unit(first, i, 2 * k + 1)
                low_unit(("md", MLP_CHUNKS - 1))
                hidden(MLP_CHUNKS - 1)

            def ffn(f):
                first = ("w1", f, 1)
                base = MLP_CHUNKS + f * 2 * FFN_CHUNKS

                def hidden(c, ft, i=None):
                    t4, t6 = (0, 0) if i is None else (i * 2 * FFN_BODY, i * BODY)
                    b, held, _ = TILES[("f", f, c, ft)]
                    x = c % FFN_BODY
                    if ft == 0:
                        dve.wait_ge(unit_used, t6 + (UNITS[first] - 3 * FFN_BODY + 3 + 3 * c))
                    dve.wait_ge(act_ready, t4 + (base + 2 * c + ft + 1))
                    raw = hid[:, ft, 0:S]
                    dve.scalar_tensor_tensor(out=raw, in0=act_out[:, b, 0:S], scalar=0.5, in1=banks[b][:, S:2 * S],
                                             op0=ALU.mult, op1=ALU.mult).then_inc(tile_read[b], 1)
                    dve.wait_ge(tile_read[b], (0 if i is None else i) + (held + 1))
                    ins = split_hidden(t4 + (base + (16 if f else 0) + 2 * c + ft + 1),
                                       (raw, hid_hi[:, x, ft], hid_lo[:, x, ft]))
                    if ft == 1:
                        ins.then_inc(hid_ready, 1)

                with dve.Fori(0, (FFN_CHUNKS - 1) // FFN_BODY) as i:
                    for k in range(FFN_BODY):
                        low_unit(first, i, 3 * k)
                        hidden(k, 0, i)
                        hidden(k, 1, i)
                        low_unit(first, i, 3 * k + 1)
                        low_unit(first, i, 3 * k + 2)
                low_unit(("w2", f, FFN_CHUNKS - 1))
                hidden(FFN_CHUNKS - 1, 0)
                hidden(FFN_CHUNKS - 1, 1)

            low_unit(("mu", 0))
            norm(2)
            mlp()
            low_unit(("w1", 0, 0))
            norm(3)
            low_unit(("w3", 0, 0))
            ffn(0)
            mixer = [(x, i) for x in ("sv", "su", "so") for i in range(8)]
            low_unit(mixer[0])
            norm(4)
            low_unit(mixer[1])
            low_unit(mixer[2])
            for i in range(3, 11):
                low_unit(mixer[i])
            def v_stats(b):
                tile_copied(dve, ("sv", 7, b))
                for k in range(4):
                    ins = dve.bn_stats(stats[:, b, k, :], vtok[:, b, k * 512:(k + 1) * 512])
                link(ins)
                dve.bn_aggr(mv[:, b, :], stats[:, b, :, :]).then_inc(sgu_var, 1)

            v_stats(0)
            low_unit(mixer[11])
            v_stats(1)
            low_unit(mixer[12])
            dve.wait_ge(sgu_in, 16 * 4)
            rest_units = mixer[13:19]
            for b in range(NB):
                dve.wait_ge(sgu_sd, b + 1)
                link(dve.reciprocal(rstd[:, b:b + 1], sd[:, b:b + 1]))
                link(dve.tensor_scalar(vtok[:, b, :], vtok[:, b, :], mv[:, b, 0:1], rstd[:, b:b + 1],
                                       ALU.subtract, ALU.mult))
                if rest_units:
                    low_unit(rest_units.pop(0))
                link(dve.tensor_tensor(vtok[:, b, :], vtok[:, b, :], sgu_g, ALU.mult))
                if rest_units:
                    low_unit(rest_units.pop(0))
                dve.tensor_tensor(vtok[:, b, :], vtok[:, b, :], sgu_b, ALU.add).then_inc(v_ready, 1)
            for name in rest_units:
                low_unit(name)

            def gated(i):
                if i >= MLP_BODY:
                    dve.wait_ge(unit_used, UNITS[("so", i - MLP_BODY)] + 1)
                for ft in (2 * i, 2 * i + 1):
                    tile_copied(dve, ("su", ft))
                    o = tile_ready(dve, ("mix", ft))
                    raw = hid[:, ft % 2, 0:S]
                    dve.tensor_tensor(raw, uT[:, ft, :], o[:, 0:S], ALU.mult).then_inc(frees(("mix", ft)), 1)
                    tile_copied(dve, ("mix", ft))
                    ins = split_hidden(MLP_CHUNKS + 2 * FFN_CHUNKS + ft + 1,
                                       (raw, hid_hi[:, i % MLP_BODY, ft % 2], hid_lo[:, i % MLP_BODY, ft % 2]))
                ins.then_inc(hid_ready, 1)

            for i in range(MLP_BODY):
                gated(i)
            for i in range(MLP_BODY, 8):
                gated(i)
                low_unit(("so", i))
            low_unit(("w1", 1, 0))
            norm(5)
            low_unit(("w3", 1, 0))
            ffn(1)
            low_unit(("kv", 0))
            norm(6)
            low_unit(("kv", 1))
            low_unit(("kv", 2))
            low_unit(("kv", 3))
            low_unit(("kv", 4))
            dve.wait_ge(fills, 3)
            for s in range(2):
                tile_copied(dve, ("kT", s, 1))
                dve.wait_ge(k_swapped[s], 32)
                for g in range(NG):
                    for odd in range(2):
                        part = slice(64 * odd, 64 * odd + 64)
                        src = (ka if g % 2 == odd else kb)[part, s, g // 2, :]
                        rows = src.rearrange("p (c j o) -> p o j c", o=2, j=8)[:, odd]
                        pe_col = colv[part, V_PE + 16 * s:V_PE + 16 * s + 16].unsqueeze(2).to_broadcast([64, 16, N_CMP])
                        for half in range(2):
                            ins = dve.tensor_tensor(cx[part, s, 8 * half:8 * half + 8, g, 0:N_CMP],
                                                    rows[:, :, half:half + N_CMP], pe_col[:, 8 * half:8 * half + 8, :],
                                                    ALU.add)
                ins.then_inc(cx_ready, 1)
                if s == 0:
                    low_unit(("kv", 5))
            low_unit(("w1", 2, 0))
            low_unit(("w3", 2, 0))
            ffn(2)
            norm(7)

            dve.wait_ge(rel_back, 16)
            tile_copied(dve, ("qg", 1))
            for b in range(NB):
                w = CMP_KEYS[b]
                first = (P if b == 0 else 0) + 31
                v = sc[:, b, :, 0:w]
                for half in range(2):
                    o = tile_ready(dve, ("cs", b, half))
                    dve.tensor_tensor(v[:, half::2], o[:, 0:P].rearrange("p (h i) -> p h i", i=16)[:, :, 0:w],
                                      rel[:, half::2, first:first + 16 * (w - 1) + 1:16],
                                      ALU.add).then_inc(frees(("cs", b, half)), 1)
                tile_copied(dve, ("cs", b, 1))
                link(dve.tensor_reduce(cmax[:], v, AX.X, ALU.max))
                dve.tensor_tensor(v, v, cmax[:].unsqueeze(2).to_broadcast([P, NH, w]),
                                  ALU.subtract).then_inc(cscore_ready, 1)
            maxima(4)
            for b in range(NB):
                w = CMP_KEYS[b]
                v = sc[:, b, :, 0:w]
                dve.wait_ge(cexp_ready, b + 1)
                link(dve.tensor_reduce(csum[:], v, AX.X, ALU.add))
                link(dve.reciprocal(crcp[:], csum[:]))
                link(dve.tensor_tensor(crcp[:], crcp[:], nsa_g[:, b, :].rearrange("p (h r) -> p h r", r=3)[:, :, 0], ALU.mult))
                if b == 0:
                    link(dve.tensor_scalar(crcp[:], crcp[:], row_valid, None, ALU.mult))
                dve.tensor_tensor(pc[:, b, :, 0:w], v, crcp[:].unsqueeze(2).to_broadcast([P, NH, w]),
                                  ALU.mult).then_inc(pc_ready, 1)
            maxima(5)
            normalize(4)
            for n in range(5, N_BATCH):
                if n + 1 < N_BATCH:
                    maxima(n + 1)
                normalize(n)
            low_unit(("w1", 3, 0))
            norm(8)
            low_unit(("w3", 3, 0))
            ffn(3)
            norm(9)

        @block.gpsimd
        def _(pool):
            link = chained(pool, pool_step)
            pool.memset(zeros[:], 0.0)
            pool.memset(ones[:], 1.0)
            pool.memset(eps[:, 0:1], RMS_EPS)
            link(pool.memset(eps[:, 1:2], LN_EPS))
            pool.memset(rel_rows[32:33, :], NEG).then_inc(fills, 1)

            def load_rows(n):
                if n == 3:
                    pool.dma_start(gain_bc[:], t["g_final"].partition_broadcast(P)).then_inc(gb_in, 16)
                else:
                    l, j = (n - 4) // 3, (n - 4) % 3
                    pool.dma_start(gain_bc[:], t["ln_g_2"][l, j].partition_broadcast(P)).then_inc(gb_in, 16)
                    pool.dma_start(bias_bc[:], t["ln_b_2"][l, j].partition_broadcast(P)).then_inc(gb_in, 16)

            def residual(n):
                pool.wait_ge(gb_in, 16 * (1 + 2 * (n - 3)))
                for b in range(NB):
                    pool.wait_ge(xn_ready, NB * n + b + 1)
                    ins = pool.tensor_tensor(resid[:, b, :], xn[:, b, :], gain_bc[:], ALU.mult)
                    if n > 3:
                        link(ins)
                        ins = pool.tensor_tensor(resid[:, b, :], resid[:, b, :], bias_bc[:], ALU.add)
                    ins.then_inc(resid_ready, 1)
                pool.wait_ge(resid_ready, NB * (n - 2))
                load_rows(n + 1)

            load_rows(3)
            tile_copied(pool, ("rel",))
            pool.dma_start(rel_dram.ap(), rel_out.unsqueeze(1).to_broadcast([NH, P, N_REL])).then_inc(rel_stored, 16)
            residual(3)
            pool.dma_start(ws, t["sgu_w_s_2"][0].rearrange("g p s -> p g s")).then_inc(sgu_in, 16)
            pool.dma_start(sgu_g, t["sgu_ln_g_2"][0].partition_broadcast(P)).then_inc(sgu_in, 16)
            pool.dma_start(sgu_b, t["sgu_ln_b_2"][0].partition_broadcast(P)).then_inc(sgu_in, 16)
            pool.dma_start(bs_row, t["sgu_b_s_2"].rearrange("a g p -> a (g p)")).then_inc(sgu_in, 16)
            pool.wait_ge(sgu_in, 16 * 4)
            pool.affine_select(out=ws, in_=ws, compare_op=ALU.is_ge, fill=0.0, base=0,
                               pattern=[[0, GROUPS], [-1, P]], channel_multiplier=1).then_inc(ws_ready, 1)
            residual(4)
            residual(5)
            for s in range(2):
                pool.dma_start(cw2[:, s], t["cmp_w2_2"][s].rearrange("(m p) d -> p m d", p=P)).then_inc(cw2_in, 16)
            pool.memset(hidc, 0.0)
            pool.memset(pc, 0.0).then_inc(fills, 1)
            pool.memset(cx, 0.0).then_inc(fills, 1)
            residual(6)
            residual(7)
            pool.wait_ge(rel_stored, 16)
            pool.dma_start(rel, bass.AP(rel_dram, P - 1, [[N_REL - 1, P], [P * N_REL, NH], [1, S]])).then_inc(rel_back, 16)
            residual(8)


NAMES = ["x", "mem", "positions", "g_mix", "w_in", "b_gate", "sinks", "g_mem", "w_mem_kv", "w_proj_swa",
         "w_proj_dsa", "w_proj_mem", "w_out", "g_mlp", "w_mlp_in", "w_mlp_out", "g_final", "rel_table_2",
         "ln_g_2", "ln_b_2", "ffn_w1_2", "ffn_w3_2", "ffn_w2_2", "sgu_w_in_2", "sgu_ln_g_2", "sgu_ln_b_2",
         "sgu_w_s_2", "sgu_b_s_2", "sgu_w_out_2", "kv_w_2", "cmp_pe_2", "cmp_w1_2", "cmp_b1_2", "cmp_w2_2",
         "nsa_w_qg_2", "nsa_w_o_2"]


def shape_constants():
    q, k = np.arange(P)[:, None], np.arange(P)[None, :]
    consts = np.zeros((P, N_CONST), np.float32)
    consts[:, K_ID:K_ID + P] = np.eye(P)
    diag = np.where(k <= q, 0.0, NEG)
    consts[:, K_SWA:K_SWA + P] = np.where(k > q, 0.0, NEG)
    consts[:, K_SWA + P:K_SWA + S] = diag
    consts[:, K_CAUSAL + P:K_CAUSAL + S] = diag
    half = np.arange(32, dtype=np.float32)
    consts[:, K_FREQ:K_FREQ + 32] = np.power(np.float32(10000.0), -half / np.float32(32))
    consts[:, K_ROW] = np.arange(P) >= 31
    dist = 2 * P - 1 - np.arange(N_REL)
    n = np.maximum(dist, 1).astype(np.float32)
    large = 16 + (np.log(n / np.float32(16)) / np.float32(np.log(128 / 16)) * np.float32(16)).astype(np.int32)
    bucket = np.where(dist < 16, np.maximum(dist, 0), np.minimum(large, 31))
    onehot = np.zeros((33, N_REL), np.float32)
    onehot[np.where(dist >= 0, bucket, 32), np.arange(N_REL)] = 1.0
    return consts, onehot


def kernel(**inputs):
    import concourse.bacc as bacc
    from concourse.bass_utils import run_bass_kernel_spmd

    nc = bacc.Bacc("TRN2", target_bir_lowering=False, num_devices=1)
    arrays, t = {}, {}
    consts, onehot = shape_constants()
    given = [(n, inputs[n]) for n in NAMES] + [("consts", consts), ("onehot", onehot)]
    for name, a in given:
        a = np.ascontiguousarray(a)
        arrays[f"in_{name}"] = a
        t[name] = nc.dram_tensor(f"in_{name}", a.shape, mybir.dt.from_np(a.dtype), kind="ExternalInput").ap()
    out = nc.dram_tensor("out_0", (1, S, D), F32, kind="ExternalOutput").ap()
    two_blocks(nc, t, out)
    r = run_bass_kernel_spmd(nc, [arrays], core_ids=[0])
    return r.results[0]["out_0"]
```

```python
from contextlib import ExitStack

import numpy as np

import concourse.bass as bass
from concourse import mybir

F32 = mybir.dt.float32
I32 = mybir.dt.int32
BF16 = mybir.dt.bfloat16
F32R = mybir.dt.float32r
ACT = mybir.ActivationFunctionType
ALU = mybir.AluOpType
AX = mybir.AxisListType

P = 128
S = 256
NB = S // P
D = 1024
KT = D // P
HD = 64
UNIT = 2048
UC = UNIT // KT
SLOTS = 3
SPLIT = 3
AHEAD = SLOTS - 1
WARM = (8, 8)
WARM_START = 12
PROBS = 3
BODY = 6
NEG = -1e30
GONE = -3e38
RMS_EPS, LN_EPS = 1e-6, 1e-5
ALPHA = (2.0 * 2) ** 0.25

C_QS, C_KS, C_VS, C_QD, C_KD, C_VD, C_QI, C_KI, C_WI, C_QM, C_GATE = (
    0, 512, 640, 768, 1024, 1088, 1152, 1408, 1472, 1476, 1732)
N_PROJ = -(-C_GATE // UC)
N_IDX = 4
TOPK = min(256, S // 4)
T_QS, T_KS, T_QD, T_KD, T_QI, T_KI, T_QM, N_TURN = 0, 4, 5, 7, 8, 10, 11, 13
R_COLS = T_QM * P

MLP_CHUNKS = 4 * D // UC
FFN = 2816
FFN_CHUNKS = FFN // UC
SGU = 2048
GROUPS = 8
ARENA = 14472
NH, NG = 16, 4
N_CMP = S // 16 - 1
CMP_KEYS = [sum(16 * n + 31 <= (b + 1) * P - 1 for n in range(N_CMP)) for b in range(NB)]
N_REL = 2 * P + P - 1
N_FFN = 4
MLP_BODY, FFN_BODY = 3, 2
V_GMIX, V_GMEM, V_GMLP, V_GFIN, V_LNG, V_LNB, V_BG, N_VEC = 0, 1, 2, 3, 4, 10, 16, 19
V_B1, V_PE, N_COLV = KT * N_VEC, KT * N_VEC + 4, KT * N_VEC + 4 + 32
K_ID, K_SWA, K_CAUSAL, K_FREQ, K_ROW, N_CONST = 0, 128, 384, 640, 672, 673


def plan_units():
    u = [("proj", i) for i in range(N_PROJ)] + [("memkv", i) for i in range(2)]
    u += [("gate", i) for i in range(12)]
    u += [("pswa", 0), ("pdm", 0), ("pswa", 1), ("pdm", 1)]
    u += [("wout", i) for i in range(4)]
    u += [("mu", 0)]
    for c in range(1, MLP_CHUNKS):
        u += [("mu", c), ("md", c - 1)]
    u += [("md", MLP_CHUNKS - 1)]

    def ffn(f):
        out = [("w1", f, 0), ("w3", f, 0)]
        for c in range(1, FFN_CHUNKS):
            out += [("w1", f, c), ("w3", f, c), ("w2", f, c - 1)]
        return out + [("w2", f, FFN_CHUNKS - 1)]

    u += ffn(0)
    u += [("sv", i) for i in range(8)] + [("su", i) for i in range(8)] + [("so", i) for i in range(8)]
    u += ffn(1)
    u += [("kv", i) for i in range(6)] + [("cw", i) for i in range(4)]
    u += ffn(2)
    u += [("qg", 0)] + [("q", i) for i in range(4)] + [("wo", i) for i in range(4)]
    u += ffn(3)
    return u


N_BATCH = 4 + NH // 2
MIX1 = [("I",), ("S", 0), ("S", 1), ("G", 1), ("T", 0), ("G", 2), ("V", 0), ("S", 2), ("G", 3), ("G", 4),
        ("T", 1), ("G", 5), ("V", 1), ("S", 3), ("G", 6), ("G", 7), ("T", 2), ("G", 8), ("V", 2), ("G", 9),
        ("G", 10), ("T", 3), ("G", 11), ("V", 3)]
MIX2 = [("C",), ("S", 4), ("S", 5), ("P",), ("S", 6)]
for _n in range(4, N_BATCH):
    MIX2 += [("T", _n), ("S", _n + 3), ("V", _n)] if _n + 3 < N_BATCH else [("TV", _n)]


def plan_tiles():
    names = [("vec",)]

    def norm(n):
        return [("n", n, b, h) for b in range(NB) for h in range(2)]

    def ffn(f):
        return [("f", f, c, t) for c in range(FFN_CHUNKS) for t in range(2)]

    def mix(steps):
        out = []
        for s in steps:
            if s[0] == "G":
                out += [("g", 2 * s[1]), ("g", 2 * s[1] + 1)]
            elif s[0] in ("T", "TV"):
                out += [("T", s[1], p) for p in range(4)]
            elif s[0] == "C":
                out += [("cs", b) for b in range(NB)]
            elif s[0] == "P":
                out += [("ct", b) for b in range(NB)]
        return out

    names += norm(0) + [("p", i, b) for i in range(5) for b in range(NB)] + [("rel",)] + norm(1)
    names += [("p", i, b) for i in range(5, N_PROJ) for b in range(NB)]
    names += [("mk", f) for f in range(2)] + [("mv", b) for b in range(NB)]
    names += [("g", 0), ("g", 1)] + [("turn", i) for i in range(-(-N_TURN // 2))]
    names += mix(MIX1)
    names += [("mg", ft, x) for ft in range(KT) for x in range(2)]
    names += norm(2)
    names += [("m", c) for c in range(MLP_CHUNKS)]
    names += norm(3) + ffn(0) + norm(4)
    names += [("sv", i, b) for i in range(8) for b in range(NB)] + [("wst", i) for i in range(2)]
    names += [("su", i) for i in range(16)] + [("mix", i) for i in range(16)]
    names += norm(5) + ffn(1) + norm(6)
    names += [("kT", s, f) for s in (0, 1) for f in range(2)] + [("kT", 2, f) for f in range(2)]
    names += [("kv", 3, b) for b in range(NB)] + [("kT", 4, f) for f in range(2)] + [("kv", 5, b) for b in range(NB)]
    names += [("ch", s, m) for s in range(2) for m in range(2)] + [("ck",), ("cv",)]
    names += ffn(2) + norm(7)
    names += [("qg",)] + [("q", i) for i in range(8)] + [("qt",)]
    names += mix(MIX2) + norm(8) + ffn(3) + norm(9)
    held, out, turn = [0] * 4, {}, 0
    for seq, name in enumerate(names):
        if name[0] == "m":
            bank = name[1] % MLP_BODY
        else:
            bank, turn = turn % 4, turn + 1
        out[name] = (bank, held[bank], seq)
        held[bank] += 1
    return out


UNITS = {name: i for i, name in enumerate(plan_units())}
SPLITS = {name: i for i, name in enumerate(
    n for n in plan_units() if n[0] != "cw")}
ORDER = plan_units()
GATE_0, GATES = SPLITS[("gate", 0)], 12


def split_slot(q):
    return (q - GATE_0) % 2 if GATE_0 <= q < GATE_0 + GATES else q % SPLIT


def split_free(name):
    q = SPLITS[name]
    held = [n for n in ORDER if n in SPLITS and SPLITS[n] < q and split_slot(SPLITS[n]) == split_slot(q)]
    return UNITS[held[-1]] + 1 if held else 0


def width(name):
    return KT * (3 * NH if name == ("qg", 0) else UC)


def arrival(u):
    held = [ORDER[j][0] for j in range(u % SLOTS, u + 1, SLOTS)]
    return 16 * (len(held) + held.count("pdm"))


TILES = plan_tiles()
ACC_DONE = {2: ("wout", 3), 3: ("md", MLP_CHUNKS - 1), 4: ("w2", 0, FFN_CHUNKS - 1), 5: ("so", 7),
            6: ("w2", 1, FFN_CHUNKS - 1), 7: ("w2", 2, FFN_CHUNKS - 1), 8: ("wo", 3),
            9: ("w2", 3, FFN_CHUNKS - 1)}
WO_EARLY = 2
PAIRS = {}
for _s in MIX1 + MIX2:
    if _s[0] == "I":
        PAIRS.update({("I", h): len(PAIRS) + h for h in range(N_IDX)})
    if _s[0] == "S":
        PAIRS.update({(_s[1], p): len(PAIRS) + p for p in range(4)})


def two_blocks(nc, t, out):
    ctx = ExitStack()
    with ctx:
        def sb(name, shape, dt=F32):
            return ctx.enter_context(nc.sbuf_tensor(name, shape, dt))

        def sem(name):
            return ctx.enter_context(nc.semaphore(name))

        banks = [ctx.enter_context(nc.psum_tensor(f"bank{i}", [P, 512], F32)) for i in range(8)]
        acc = banks[4:8]
        score_banks = banks[4:7]
        o_bank = banks[7]

        ring = sb("ring", [P, SLOTS, UNIT])
        resid = sb("resid", [P, NB, D])
        xn = sb("xn", [P, NB, D])
        hT_hi = sb("hT_hi", [P, KT, S], F32R)
        hT_lo = sb("hT_lo", [P, KT, S], F32R)
        act_out = sb("act_out", [P, 4, 512])
        gain_bc = sb("gain_bc", [P, D])
        bias_bc = sb("bias_bc", [P, D])
        with nc.sbuf_tensor("shared_rows", [P, 3 * MLP_BODY * 512], F32) as shared_rows:
            pass
        hid = sb("hid", [P, MLP_BODY, 512])
        hid_hi = sb("hid_hi", [P, MLP_BODY, 2, S], F32R)
        hid_lo = sb("hid_lo", [P, MLP_BODY, 2, S], F32R)
        const = sb("const", [P, N_CONST])
        zeros = sb("zeros", [P, S])
        ones = sb("ones", [1, P])
        colv = sb("colv", [P, N_COLV])
        sinks = sb("sinks", [P, 8])
        eps = sb("eps", [P, 2])
        stats = sb("stats", [P, NB, 4, 6])
        mv = sb("mv", [P, NB, 2])
        msq = sb("msq", [P, NB])
        sd = sb("sd", [P, NB])
        rstd = sb("rstd", [P, NB])
        row_max = sb("row_max", [P, PROBS, 8])
        neg_max = sb("neg_max", [P, PROBS, 8])
        row_sum = sb("row_sum", [P, PROBS, 8])
        sink_in = sb("sink_in", [P, PROBS, 8])
        sink_exp = sb("sink_exp", [P, PROBS, 8])
        row_rcp = sb("row_rcp", [P, PROBS, 8])
        wsc = sb("wsc", [P, NB, N_IDX])
        best = sb("best", [P, 8])
        cmax = sb("cmax", [P, NH])
        csum = sb("csum", [P, NH])
        crcp = sb("crcp", [P, NH])
        pos_i = sb("pos_i", [P, NB], I32)
        pos_f = sb("pos_f", [P, NB])
        trig = sb("trig", [P, 2, NB, 32])
        ang = sb("ang", [P, 4, NB, 32])
        probT = act_out[:].rearrange("p a (x k q) -> p a x k q", x=2, k=2)
        hT_tmp = act_out[:].rearrange("p a (x s) -> p (a x) s", x=2)

        with nc.sbuf_tensor("arena", [P, ARENA], F32) as arena:
            pass
        two = sb("two", [P, 2, KT, S], F32R)
        sb("arena_rest", [P, ARENA - 2 * KT * S])

        def take(at, *shape, of=None):
            n = int(np.prod(shape))
            a = (arena if of is None else of)[:, at[0]:at[0] + n]
            at[0] += n
            if len(shape) == 1:
                return a
            names = "abcd"[:len(shape)]
            return a.rearrange("p (%s) -> p %s" % (" ".join(names), " ".join(names)),
                               **{x: s for x, s in zip(names[:-1], shape[:-1])})

        with nc.sbuf_tensor("attend", [P, 2 * SPLIT * UNIT], F32) as attend:
            pass
        split = sb("split", [P, SPLIT, 2, UNIT], F32R)
        split_hi, split_lo = split[:, :, 0, :], split[:, :, 1, :]
        xn_flat = xn[:].rearrange("p b d -> p (b d)")
        third = attend[:, 2 * 2 * UNIT:3 * 2 * UNIT]
        prob = [a.rearrange("p (k s) -> p k s", k=8) for a in (third[:, 0:UNIT], third[:, UNIT:2 * UNIT], xn_flat)]
        merge_tmp = xn_flat[:, 0:6 * S].rearrange("p (y x s) -> p y x s", y=2, x=3)
        idx_tmp = xn_flat[:, 0:S]
        at = [0]
        memt = take(at, NB, D, of=shared_rows)
        vec_rows = take(at, D, of=shared_rows)[0:N_VEC]
        pe_rows = take(at, P, of=shared_rows)[0:32]
        b1_rows = take(at, P, of=shared_rows)[0:4]
        rel_rows = take(at, NH, of=shared_rows)[0:33]
        onehot = take(at, N_REL, of=shared_rows)[0:33]
        rel_out = take(at, N_REL, of=shared_rows)[0:NH]
        roped = take([0], NB, R_COLS, of=shared_rows)
        rel = take([0], NH, S, of=shared_rows)

        at = [2 * KT * S]
        proj = take(at, NB, C_GATE)
        qkT = take(at, N_TURN, S)
        rope_tmp = qkT[:].rearrange("p a s -> p (a s)")[:, 0:4 * NB * 10 * 32].rearrange(
            "p (x b h e) -> p x b h e", x=4, b=NB, h=10)
        gate_rest = take(at, 6, S)
        kmT = take(at, 2, S)
        vm = take(at, NB, S)
        isc = take(at, NB, S)
        maskD = take(at, NB, S)

        def gate_tile(i):
            return gate_rest[:, i, :] if i < 6 else shared_rows[:, (i - 6) * S:(i - 5) * S]

        both_hT = (hT_hi, hT_lo)
        both_two = (two[:, 0], two[:, 1])
        at = [0]
        vtok = take(at, NB, SGU)
        uT = take(at, 16, S)
        ws = uT[:, 0:4, :].rearrange("p a s -> p (a s)").rearrange("p (g s) -> p g s", g=GROUPS)
        wsT = take(at, GROUPS, P)
        sgu_g = take(at, SGU)
        sgu_b = take(at, SGU)
        bs_bc = take(at, GROUPS * P)
        at = [0]
        ka = take(at, 4, 2, S)
        kb = take(at, 4, 2, S)
        vv = take(at, 2, NB, S)
        qT = take(at, 8, S)
        cx = take(at, 2, 16, NG, 16)
        hidc = take(at, 2, 2, NG, 32)
        kcT = take(at, NG, 2, 16)
        vc = take(at, S)
        pc = take(at, NB, NH, 32)
        pcT = take(at, NG, S)
        sc = take(at, NB, NH, 16)
        cw2 = take(at, 2, 2, HD)
        nsa_g = take(at, NB, 3 * NH)
        nsa_gT = take(at, S)[0:3 * NH, :]

        rel_dram = nc.dram_tensor("rel_scratch", (NH, P, N_REL), F32, kind="Internal")

        ident = const[:, K_ID:K_ID + P]
        mask_swa = const[:, K_SWA:K_SWA + S]
        mask_causal = const[:, K_CAUSAL:K_CAUSAL + S]
        freq = const[:, K_FREQ:K_FREQ + 32]
        row_valid = const[:, K_ROW:K_ROW + 1]

        arrived = [sem(f"arrived{i}") for i in range(SLOTS)]
        half_done = sem("half_done")
        unit_used = sem("unit_used")
        hi_ready = sem("hi_ready")
        split_ready = sem("split_ready")
        hT_rounded, hT_ready = sem("hT_rounded"), sem("hT_ready")
        tile_done = sem("tile_done")
        tile_read = [sem(f"tile_read{i}") for i in range(4)]
        x_in = [sem(f"x_in{b}") for b in range(NB)]
        mem_in, ident_in, const_in, vec_in, rel_in, sink_ld, pos_in = (
            sem(n) for n in ("mem_in", "ident_in", "const_in", "vec_in", "rel_in", "sink_ld", "pos_in"))
        fills = sem("fills")
        gb_in = sem("gb_in")
        sgu_in = sem("sgu_in")
        cw2_in = sem("cw2_in")
        rel_out_ready, rel_stored, rel_back = sem("rel_out_ready"), sem("rel_stored"), sem("rel_back")
        cols_ready = sem("cols_ready")
        var_ready, sd_ready, xn_ready, resid_ready = sem("var_ready"), sem("sd_ready"), sem("xn_ready"), sem("resid_ready")
        angle_ready, trig_ready = sem("angle_ready"), sem("trig_ready")
        roped_ready = sem("roped_ready")
        score_done = sem("score_done")
        score_read = [sem(f"score_read{i}") for i in range(3)]
        neg_ready, exp_ready, prob_ready = sem("neg_ready"), sem("exp_ready"), sem("prob_ready")
        pv_done, o_read = sem("pv_done"), sem("o_read")
        merged_ready = sem("merged_ready")
        act_ready, hid_rounded, hid_ready = sem("act_ready"), sem("hid_rounded"), sem("hid_ready")
        ws_ready, sgu_var, sgu_sd, v_ready = sem("ws_ready"), sem("sgu_var"), sem("sgu_sd"), sem("v_ready")
        k_swapped = [sem(f"k_swapped{i}") for i in range(4)]
        cx_ready = sem("cx_ready")
        hidc_ready = sem("hidc_ready")
        cscore_ready, cexp_ready, pc_ready = sem("cscore_ready"), sem("cexp_ready"), sem("pc_ready")
        o_rounded = sem("o_rounded")
        merged_raw, merged_rounded = sem("merged_raw"), sem("merged_rounded")
        out_ready, stored = [sem(f"out_ready{b}") for b in range(NB)], sem("stored")
        dve_step, act_step, pool_step = sem("dve_step"), sem("act_step"), sem("pool_step")

        def bank_of(name):
            return banks[TILES[name][0]]

        def tile_ready(eng, name):
            eng.wait_ge(tile_done, TILES[name][2] + 1)
            return bank_of(name)

        def tile_copied(eng, name):
            eng.wait_ge(tile_read[TILES[name][0]], TILES[name][1] + 1)

        def frees(name):
            return tile_read[TILES[name][0]]

        def slot(name):
            return UNITS[name] % SLOTS

        def up_unit(name):
            return ring[:, slot(name), :].rearrange("p (k c) -> p k c", k=KT)

        def parts(name, k):
            q = split_slot(SPLITS[name])
            return [r[:, q, 0:width(name)].rearrange("p (k c) -> p k c", k=k) for r in (split_hi, split_lo)]

        def chained(eng, step):
            count = [0]

            def link(ins):
                ins.then_inc(step, 1)
                count[0] += 1
                eng.wait_ge(step, count[0])
            return link

        def attention(n):
            tiles = []
            if n < 2:
                for h in range(8):
                    kv, j = h // 4, h % 4
                    part = slice(64 * kv, 64 * kv + 64)
                    w = P * (n + 1)
                    tiles.append((qkT[part, T_QS + j, n * P:(n + 1) * P], qkT[part, T_KS, 0:w], w,
                                  mask_swa[:, S - w:S], 0.125, sinks[:, h:h + 1],
                                  [proj[:, k, C_VS + kv * HD:C_VS + (kv + 1) * HD] for k in range(n + 1)],
                                  64 * (h % 2), (h // 2) * P))
            elif n < 4:
                for b in range(NB):
                    for h in (0, 2, 1, 3):
                        part = slice(64 * (h % 2), 64 * (h % 2) + 64)
                        qs = slice(b * P, (b + 1) * P)
                        o = (64 * (h % 2), (h // 2) * S + b * P)
                        if n == 2:
                            tiles.append((qkT[part, T_QM + h // 2, qs], kmT[part, h // 2, :], S, zeros[:, :], 0.125,
                                          GONE, [vm[:, k, h * HD:(h + 1) * HD] for k in range(NB)], *o))
                        else:
                            w = P * (b + 1)
                            tiles.append((qkT[part, T_QD + h // 2, qs], qkT[part, T_KD, 0:w], w, maskD[:, b, 0:w],
                                          0.125, GONE,
                                          [proj[:, k, C_VD:C_VD + HD] for k in range(b + 1)], *o))
            else:
                for h in (2 * (n - 4), 2 * (n - 4) + 1):
                    g = h // 4
                    part = slice(64 * (h % 2), 64 * (h % 2) + 64)
                    keys = ka if h % 2 == g % 2 else kb
                    for b in range(NB):
                        w = P * (b + 1)
                        for br in range(2):
                            tiles.append((qT[part, h // 2, b * P:(b + 1) * P], keys[part, 2 + br, g // 2, 0:w], w,
                                          rel[:, h, S - w:S], 1.0, GONE,
                                          [vv[:, br, k, g * HD:(g + 1) * HD] for k in range(b + 1)],
                                          64 * (h % 2), b * P))
            return tiles

        def out_place(n, part):
            if n < 2:
                return both_two[part][:, 0:4, n * P:(n + 1) * P], o_bank[:, :].rearrange("p (j q) -> p j q", j=4)
            if n < 4:
                return (both_two[part][:, 4 + 2 * (n - 2):6 + 2 * (n - 2), :].rearrange("p a s -> p (a s)"),
                        o_bank[:, :])
            return both_hT[part][:, n - 4, :], o_bank[:, 0:S]

        block = ctx.enter_context(nc.Block())

        @block.sync
        def _(sp):
            for b in range(NB):
                sp.dma_start(resid[:, b, :], t["x"][0, b * P:(b + 1) * P, :]).then_inc(x_in[b], 16)

            def up(w, c0, n=UC):
                return w.rearrange("(k p) c -> p k c", p=P)[:, :, c0:c0 + n]

            def down(w, r):
                return w.rearrange("(r k p) c -> r p k c", p=P, k=2)[r]

            w_in = t["w_in"][0]
            w1 = [t["ffn_w1_2"][f // 2, f % 2].rearrange("(k p) c -> p k c", p=P) for f in range(N_FFN)]
            w3 = [t["ffn_w3_2"][f // 2, f % 2].rearrange("(k p) c -> p k c", p=P) for f in range(N_FFN)]
            w2 = [t["ffn_w2_2"][f // 2, f % 2].rearrange("(r k p) c -> r p k c", p=P, k=2) for f in range(N_FFN)]
            mu = t["w_mlp_in"][0].rearrange("(k p) c -> p k c", p=P)
            md = t["w_mlp_out"][0].rearrange("(r k p) c -> r p k c", p=P, k=2)

            def source(name):
                kind, i = name[0], name[-1]
                return {
                    "proj": lambda: up(w_in, i * UC),
                    "memkv": lambda: up(t["w_mem_kv"][0], i * UC),
                    "gate": lambda: up(w_in, C_GATE + i * UC),
                    "pswa": lambda: t["w_proj_swa"][0].rearrange("(k p) c -> p k c", p=P)[:, :, i * 512:(i + 1) * 512],
                    "wout": lambda: down(t["w_out"][0], i),
                    "mu": lambda: up(t["w_mlp_in"][0], i * UC),
                    "md": lambda: down(t["w_mlp_out"][0], i),
                    "w1": lambda: w1[name[1]][:, :, i * UC:(i + 1) * UC],
                    "w3": lambda: w3[name[1]][:, :, i * UC:(i + 1) * UC],
                    "w2": lambda: w2[name[1]][i],
                    "sv": lambda: up(t["sgu_w_in_2"][0], SGU + i * UC),
                    "su": lambda: up(t["sgu_w_in_2"][0], i * UC),
                    "so": lambda: down(t["sgu_w_out_2"][0], i),
                    "kv": lambda: up(t["kv_w_2"], i * UC),
                    "cw": lambda: t["cmp_w1_2"][i // 2].rearrange("(h k p) c -> h p k c", h=2, p=P)[i % 2],
                    "qg": lambda: up(t["nsa_w_qg_2"][0], D, 48),
                    "q": lambda: up(t["nsa_w_qg_2"][0], i * UC),
                    "wo": lambda: down(t["nsa_w_o_2"][0], i),
                }[kind]()

            def load(name):
                u = UNITS[name]
                if u >= SLOTS:
                    held = ORDER[u - SLOTS]
                    if held in SPLITS:
                        sp.wait_ge(split_ready, AHEAD + SPLITS[held] + 1)
                    else:
                        sp.wait_ge(unit_used, u - SLOTS + 1)
                if name[0] == "pdm":
                    for j, w in enumerate((t["w_proj_dsa"][0], t["w_proj_mem"][0])):
                        sp.dma_start(ring[:, u % SLOTS, j * D:(j + 1) * D].rearrange("p (k c) -> p k c", k=2),
                                     w.rearrange("(k p) c -> p k c", p=P)[:, :, name[1] * 512:(name[1] + 1) * 512]
                                     ).then_inc(arrived[u % SLOTS], 16)
                    return
                src = source(name)
                n = src.shape[1] * src.shape[2]
                dst = ring[:, u % SLOTS, 0:n].rearrange("p (k c) -> p k c", k=src.shape[1])
                sp.dma_start(dst, src).then_inc(arrived[u % SLOTS], 16)

            def load_loop(first, turns, sources):
                u, q = UNITS[first], SPLITS[first]
                plain = [n for n in ORDER[u - SLOTS:u] if n not in SPLITS]
                if plain:
                    sp.wait_ge(unit_used, UNITS[plain[-1]] + 1)
                with sp.Fori(0, turns) as i:
                    for k, src in enumerate(sources):
                        s = (u + k) % SLOTS
                        view = src(i)
                        dst = ring[:, s, :].rearrange("p (k c) -> p k c", k=view.shape[1])
                        split = sp.snap(i * BODY + (AHEAD + q + k - SLOTS + 1))
                        sp.wait_ge(split_ready, split)
                        sp.dma_start(dst, view).then_inc(arrived[s], 16)

            def column(w, c):
                return lambda i: w[:, :, bass.ds(sp.snap(i * (c[0] * UC) + c[1] * UC), UC)]

            def rows(w, c):
                return lambda i: w[bass.ds(sp.snap(i * c[0] + c[1]), 1)].rearrange("r p k c -> (r p) k c")

            def ffn(f):
                load(("w1", f, 0))
                load(("w3", f, 0))
                body = []
                for k in range(FFN_BODY):
                    body += [column(w1[f], (FFN_BODY, k + 1)), column(w3[f], (FFN_BODY, k + 1)),
                             rows(w2[f], (FFN_BODY, k))]
                load_loop(("w1", f, 1), (FFN_CHUNKS - 1) // FFN_BODY, body)
                load(("w2", f, FFN_CHUNKS - 1))

            def some(kind, n):
                for i in range(n):
                    load((kind, i))

            load(("proj", 0))
            sp.wait_ge(vec_in, 16 * 9)
            sp.dma_start(const[:, P:N_CONST], t["consts"][:, P:N_CONST]).then_inc(const_in, 16)
            load(("proj", 1))
            sp.dma_start(memt, t["mem"][0].rearrange("(b p) d -> p b d", p=P)).then_inc(mem_in, 16)
            for i in range(2, N_PROJ):
                load(("proj", i))
            some("memkv", 2)
            some("gate", 12)
            for half in range(2):
                load(("pswa", half))
                load(("pdm", half))
            some("wout", 4)
            load(("mu", 0))
            body = []
            for k in range(MLP_BODY):
                body += [column(mu, (MLP_BODY, k + 1)), rows(md, (MLP_BODY, k))]
            load_loop(("mu", 1), (MLP_CHUNKS - 1) // MLP_BODY, body)
            load(("md", MLP_CHUNKS - 1))
            ffn(0)
            some("sv", 8)
            some("su", 8)
            some("so", 8)
            ffn(1)
            some("kv", 6)
            some("cw", 4)
            ffn(2)
            load(("qg", 0))
            some("q", 4)
            some("wo", 4)
            ffn(3)
            sp.wait_ge(out_ready[0], 1)
            sp.dma_start(out[0, 0:P, :], xn[:, 0, :]).then_inc(stored, 16)
            for h in range(2):
                sp.wait_ge(out_ready[1], h + 1)
                sp.dma_start(out[0, P:S, h * 512:(h + 1) * 512], xn[:, 1, h * 512:(h + 1) * 512]).then_inc(stored, 16)
            sp.wait_ge(stored, 16 * 3)

        @block.tensor
        def _(pe):
            owed = [0]

            def mm(o, lhsT, rhs, start, stop):
                ins = pe.matmul(o, lhsT, rhs, start=start, stop=stop)
                return ins

            def settle(ins):
                if owed[0]:
                    ins.then_inc(unit_used, owed[0])
                    owed[0] = 0

            def open_tile(name):
                b, held, _ = TILES[name]
                if held:
                    pe.wait_ge(tile_read[b], held)
                return banks[b]

            def have(name):
                if name in SPLITS:
                    pe.wait_ge(split_ready, AHEAD + SPLITS[name] + 1)
                else:
                    u = UNITS[name]
                    pe.wait_ge(arrived[u % SLOTS], arrival(u))

            def turn(o, a, n=P):
                return pe.transpose(o, a, ident[0:n, 0:n])

            def passes(k, last):
                return ((0, 0, k == 0, False), (0, 1, False, False), (1, 0, False, k == last))

            def up_T_split(o, unit, c0, n, norm=None, act=both_hT):
                for k in range(KT):
                    if norm is not None:
                        normed(norm, NB - 1, k)
                    for w, a, start, stop in passes(k, KT - 1):
                        ins = mm(o, unit[w][:, k, c0:c0 + n], act[a][:, k, :], start, stop)
                        if start:
                            settle(ins)
                return ins

            def up_tok_split(o, unit, n, b, norm=None, act=both_hT):
                for k in range(KT):
                    if norm is not None:
                        normed(norm, b, k)
                    for w, a, start, stop in passes(k, KT - 1):
                        ins = mm(o, act[a][:, k, b * P:(b + 1) * P], unit[w][:, k, 0:n], start, stop)
                        if start:
                            settle(ins)
                return ins

            def branch(o, unit, k0, ks, cols, at):
                for k in range(ks):
                    for w, a, start, stop in passes(k, ks - 1):
                        ins = mm(o, unit[w][:, k0 + k, cols], both_two[a][:, at + k, :], start, stop)
                        settle(ins)
                return ins

            def down_split(unit, act):
                for b in range(NB):
                    for k in range(2):
                        for w, a, _, _ in passes(k, 1):
                            for h in range(2):
                                ins = mm(acc[b * 2 + h][:, :], act(a, k)[:, b * P:(b + 1) * P],
                                         unit[w][:, k, h * 512:(h + 1) * 512], False, False)
                                settle(ins)
                ins.then_inc(unit_used, 1)

            def down_last(before, last):
                units = [before]

                def add(n, b, h):
                    unit, act = units[n]
                    for k in range(2):
                        for w, a, _, stop in passes(k, 1):
                            ins = mm(acc[b * 2 + h][:, :], act(a, k)[:, b * P:(b + 1) * P],
                                     unit[w][:, k, h * 512:(h + 1) * 512], False, stop and n == 1)
                            settle(ins)
                    return ins

                add(0, 0, 0)
                add(0, 0, 1)
                units.append(last())
                add(1, 0, 0)
                add(1, 0, 1).then_inc(half_done, 1)
                add(0, 1, 0)
                add(1, 1, 0).then_inc(half_done, 1)
                add(0, 1, 1).then_inc(unit_used, 1)
                add(1, 1, 1).then_inc(unit_used, 1)

            def hidden_chunk(x):
                return lambda a, k: (hid_hi, hid_lo)[a][:, x, k, :]

            def features(i):
                return lambda a, k: both_hT[a][:, 2 * i + k, :]

            def down_all(kind):
                def unit(i):
                    have((kind, i))
                    return parts((kind, i), 2), features(i)

                for i in range(2):
                    down_split(*unit(i))
                down_last(unit(2), lambda: unit(3))

            def clear_acc():
                nil = zeros[:, :].bitcast(BF16)
                for a in acc:
                    settle(mm(a[:, :], nil[:, 0:P], nil[:, 0:512], True, False))

            def keep_warm(n):
                nil = zeros[:, :].bitcast(BF16)
                for _ in range(n):
                    settle(mm(acc[0][:, :], nil[:, 0:P], nil[:, 0:512], True, True))

            def norm(n):
                for b in range(NB):
                    pe.wait_ge(xn_ready, NB * n + b + 1)
                    for h in range(2):
                        o = open_tile(("n", n, b, h))
                        for k in range(4):
                            ins = turn(o[:, k * P:(k + 1) * P], xn[:, b, (h * 4 + k) * P:(h * 4 + k + 1) * P])
                            if k == 0:
                                settle(ins)
                        ins.then_inc(tile_done, 1)
                    if n != 1:
                        keep_warm(WARM[b])

            def normed(n, b, k):
                if k % 4 == 0:
                    pe.wait_ge(hT_ready, 4 * n + 2 * b + k // 4 + 1)

            pe.wait_ge(fills, 1)
            keep_warm(WARM_START)
            pe.wait_ge(ident_in, 16)
            pe.wait_ge(vec_in, 16 * 9)
            o = open_tile(("vec",))
            for k in range(KT):
                turn(o[:, k * N_VEC:(k + 1) * N_VEC], vec_rows[:, k * P:(k + 1) * P], N_VEC)
            turn(o[:, V_B1:V_B1 + 4], b1_rows, 4)
            turn(o[:, V_PE:V_PE + 32], pe_rows, 32).then_inc(tile_done, 1)

            norm(0)
            for i in range(N_PROJ):
                have(("proj", i))
                for b in range(NB):
                    o = open_tile(("p", i, b))
                    up_tok_split(o[:, 0:UC], parts(("proj", i), KT), UC, b, None if i else 0).then_inc(tile_done, 1)
                owed[0] += 1
                if i == 4:
                    pe.wait_ge(rel_in, 32)
                    o = open_tile(("rel",))
                    ins = mm(o[0:NH, 0:N_REL], rel_rows, onehot, True, True)
                    ins.then_inc(tile_done, 1)
                    norm(1)
            have(("memkv", 0))
            for f in range(2):
                o = open_tile(("mk", f))
                up_T_split(o[:, 0:S], parts(("memkv", 0), KT), f * P, P, None if f else 1, both_two).then_inc(tile_done, 1)
            owed[0] += 1
            have(("memkv", 1))
            for b in range(NB):
                o = open_tile(("mv", b))
                up_tok_split(o[:, 0:S], parts(("memkv", 1), KT), S, b, None, both_two).then_inc(tile_done, 1)
            owed[0] += 1
            def gate(i):
                have(("gate", i))
                for f in range(2):
                    o = open_tile(("g", 2 * i + f))
                    up_T_split(o[:, 0:S], parts(("gate", i), KT), f * P, P).then_inc(tile_done, 1)
                owed[0] += 1

            gate(0)
            pe.wait_ge(roped_ready, 1)
            for i in range(-(-N_TURN // 2)):
                o = open_tile(("turn", i))
                for j in range(2 * i, min(2 * i + 2, N_TURN)):
                    for b in range(NB):
                        src = roped[:, b, j * P:(j + 1) * P] if j < T_QM else \
                            proj[:, b, C_QM + (j - T_QM) * P:C_QM + (j - T_QM + 1) * P]
                        ins = turn(o[:, ((j % 2) * NB + b) * P:((j % 2) * NB + b + 1) * P], src)
                        settle(ins)
                ins.then_inc(tile_done, 1)
            for i in range(-(-N_TURN // 2)):
                tile_copied(pe, ("turn", i))
            tile_copied(pe, ("mk", 1))
            tile_copied(pe, ("mv", 1))

            def open_pair(key):
                n = PAIRS[key]
                if n >= 3:
                    pe.wait_ge(score_read[n % 3], n // 3)
                return score_banks[n % 3]

            def index_scores():
                for h in range(N_IDX):
                    o = open_pair(("I", h))
                    part = slice(64 * (h % 2), 64 * (h % 2) + 64)
                    for b in range(NB):
                        w = P * (b + 1)
                        ins = mm(o[:, b * S:b * S + w], qkT[part, T_QI + h // 2, b * P:(b + 1) * P],
                                 qkT[part, T_KI, 0:w], True, True)
                    ins.then_inc(score_done, 1)

            def scores(n):
                tiles = attention(n)
                for p in range(4):
                    o = open_pair((n, p))
                    for a in range(2):
                        q, k, w = tiles[2 * p + a][:3]
                        ins = mm(o[:, a * S:a * S + w], q, k, True, True)
                        if a == 0:
                            settle(ins)
                    ins.then_inc(score_done, 1)

            def turn_probs(n, p):
                tiles = attention(n)
                o = open_tile(("T", n, p))
                pe.wait_ge(prob_ready, 4 * n + p + 1)
                for a in range(2):
                    for k in range(tiles[2 * p + a][2] // P):
                        ins = turn(o[:, (a * 2 + k) * P:(a * 2 + k + 1) * P],
                                   prob[n % PROBS][:, 2 * p + a, k * P:(k + 1) * P])
                        settle(ins)
                ins.then_inc(tile_done, 1)

            def values(n, p):
                tiles = attention(n)
                if p == 0 and n:
                    pe.wait_ge(o_read, n)
                tile_copied(pe, ("T", n, p))
                for a in range(2):
                    _, _, w, _, _, _, v, part, col = tiles[2 * p + a]
                    o = o_bank[part:part + 64, col:col + P]
                    if n >= 4 and a == 0:
                        h, b = 2 * (n - 4) + p // 2, p % 2
                        r = slice(32 * (h % 4), 32 * (h % 4) + 32)
                        settle(mm(o, vc[r, (h // 4) * HD:(h // 4 + 1) * HD], pcT[r, h // 4, b * P:(b + 1) * P], True, False))
                    for k in range(w // P):
                        first = k == 0 and n < 4
                        last = k == w // P - 1 and (n < 4 or a == 1)
                        ins = mm(o, v[k], probT[:, (4 * n + p) % 4, a, k, :], first, last)
                        if a == 0:
                            settle(ins)
                ins.then_inc(pv_done, 1)

            def batch(step):
                what, n = step
                for p in range(4):
                    if "T" in what:
                        turn_probs(n, p)
                    if what == "V":
                        values(n, p)
                    elif what == "TV" and p:
                        values(n, p - 1)
                if what == "TV":
                    values(n, 3)

            for s in MIX1:
                if s[0] == "I":
                    index_scores()
                elif s[0] == "S":
                    scores(s[1])
                elif s[0] == "G":
                    gate(s[1])
                else:
                    batch(s)

            windowed = {}

            def windowed_branch(ft):
                o = windowed[ft] = open_tile(("mg", ft, 0))
                branch(o[:, 0:S], parts(("pswa", ft // 4), 4), 0, 4, slice((ft % 4) * P, (ft % 4 + 1) * P), 0)

            pe.wait_ge(o_read, 2)
            have(("pswa", 0))
            for ft in range(2):
                windowed_branch(ft)
            pe.wait_ge(o_read, 4)
            for half in range(2):
                if half:
                    have(("pswa", half))
                dm = parts(("pdm", half), 4)
                for ft in range(4 * half, 4 * half + 4):
                    cols = slice((ft % 4) * P, (ft % 4 + 1) * P)
                    if ft not in windowed:
                        windowed_branch(ft)
                    o = windowed[ft]
                    if ft % 4 == 3:
                        owed[0] += 1
                    if ft % 4 == 0:
                        have(("pdm", half))
                    branch(o[:, S:2 * S], dm, 0, 2, cols, 6).then_inc(tile_done, 1)
                    o = open_tile(("mg", ft, 1))
                    branch(o[:, 0:S], dm, 2, 2, cols, 4).then_inc(tile_done, 1)
                owed[0] += 1
            clear_acc()
            pe.wait_ge(merged_ready, KT)
            down_all("wout")

            def split_in_turn(first, k, i, tiles):
                q = SPLITS[first] + k
                pe.wait_ge(split_ready, i * BODY + (AHEAD + q + 1))
                return [r[:, q % SPLIT, :].rearrange("p (k c) -> p k c", k=tiles) for r in (split_hi, split_lo)]

            def mlp(n):
                have(("mu", 0))
                o = open_tile(("m", 0))
                for f in range(2):
                    ins = up_T_split(o[:, f * S:(f + 1) * S], parts(("mu", 0), KT), f * P, P, None if f else n)
                ins.then_inc(tile_done, 1)
                owed[0] += 1
                clear_acc()

                def chunk(k, i):
                    b, held, _ = TILES[("m", k + 1)]
                    pe.wait_ge(tile_read[b], i + held)
                    unit = split_in_turn(("mu", 1), 2 * k, i, KT)
                    for f in range(2):
                        ins = up_T_split(banks[b][:, f * S:(f + 1) * S], unit, f * P, P)
                    owed[0] += 1
                    ins.then_inc(tile_done, 1)
                    w = split_in_turn(("mu", 1), 2 * k + 1, i, 2)
                    pe.wait_ge(hid_ready, i * MLP_BODY + (k + 1))
                    return w, hidden_chunk(k)

                turns = (MLP_CHUNKS - 1) // MLP_BODY
                with pe.Fori(0, turns - 1) as i:
                    for k in range(MLP_BODY):
                        down_split(*chunk(k, i))
                for k in range(MLP_BODY - 1):
                    down_split(*chunk(k, turns - 1))
                before = chunk(MLP_BODY - 1, turns - 1)

                def last():
                    have(("md", MLP_CHUNKS - 1))
                    pe.wait_ge(hid_ready, MLP_CHUNKS)
                    return parts(("md", MLP_CHUNKS - 1), 2), hidden_chunk((MLP_CHUNKS - 1) % MLP_BODY)

                down_last(before, last)

            def ffn(f, n):
                have(("w1", f, 0))
                tiles = [open_tile(("f", f, 0, ft)) for ft in range(2)]

                def up_w3(tiles, w3):
                    for ft in range(2):
                        up_T_split(tiles[ft][:, S:2 * S], w3, ft * P, P).then_inc(tile_done, 1)
                    owed[0] += 1

                for ft in range(2):
                    up_T_split(tiles[ft][:, 0:S], parts(("w1", f, 0), KT), ft * P, P, None if ft else n)
                owed[0] += 1
                have(("w3", f, 0))
                up_w3(tiles, parts(("w3", f, 0), KT))
                clear_acc()
                done = MLP_CHUNKS + f * FFN_CHUNKS + (8 if f else 0)

                def chunk(k, i):
                    tiles = []
                    w1 = split_in_turn(("w1", f, 1), 3 * k, i, KT)
                    for ft in range(2):
                        b, held, _ = TILES[("f", f, k + 1, ft)]
                        pe.wait_ge(tile_read[b], i + held)
                        tiles.append(banks[b])
                        up_T_split(banks[b][:, 0:S], w1, ft * P, P)
                    owed[0] += 1
                    up_w3(tiles, split_in_turn(("w1", f, 1), 3 * k + 1, i, KT))
                    w2 = split_in_turn(("w1", f, 1), 3 * k + 2, i, 2)
                    pe.wait_ge(hid_ready, i * FFN_BODY + (done + k + 1))
                    return w2, hidden_chunk(k)

                turns = (FFN_CHUNKS - 1) // FFN_BODY
                with pe.Fori(0, turns - 1) as i:
                    for k in range(FFN_BODY):
                        down_split(*chunk(k, i))
                for k in range(FFN_BODY - 1):
                    down_split(*chunk(k, turns - 1))
                before = chunk(FFN_BODY - 1, turns - 1)

                def last():
                    have(("w2", f, FFN_CHUNKS - 1))
                    pe.wait_ge(hid_ready, done + FFN_CHUNKS)
                    return parts(("w2", f, FFN_CHUNKS - 1), 2), hidden_chunk((FFN_CHUNKS - 1) % FFN_BODY)

                down_last(before, last)

            norm(2)
            mlp(2)
            norm(3)
            ffn(0, 3)
            norm(4)

            for i in range(8):
                have(("sv", i))
                for b in range(NB):
                    o = open_tile(("sv", i, b))
                    up_tok_split(o[:, 0:S], parts(("sv", i), KT), S, b, None if i else 4).then_inc(tile_done, 1)
                owed[0] += 1
            pe.wait_ge(ws_ready, 1)
            for i in range(2):
                o = open_tile(("wst", i))
                for k in range(4):
                    ins = turn(o[:, k * P:(k + 1) * P], ws[:, 4 * i + k, :])
                    settle(ins)
                ins.then_inc(tile_done, 1)
            for i in range(8):
                have(("su", i))
                for f in range(2):
                    o = open_tile(("su", 2 * i + f))
                    up_T_split(o[:, 0:S], parts(("su", i), KT), f * P, P).then_inc(tile_done, 1)
                owed[0] += 1
            tile_copied(pe, ("wst", 0))
            tile_copied(pe, ("wst", 1))
            pe.wait_ge(v_ready, NB)

            def mix(ft):
                g = ft // 2
                o = open_tile(("mix", ft))
                for b in range(NB):
                    ins = mm(o[:, b * P:(b + 1) * P], vtok[:, b, ft * P:(ft + 1) * P], wsT[:, g, :], True, True)
                    settle(ins)
                ins.then_inc(tile_done, 1)

            for ft in range(2 * MLP_BODY):
                mix(ft)
            clear_acc()
            def gated_unit(i):
                have(("so", i))
                pe.wait_ge(hid_ready, MLP_CHUNKS + FFN_CHUNKS + i + 1)
                return parts(("so", i), 2), hidden_chunk(i % MLP_BODY)

            for i in range(6):
                down_split(*gated_unit(i))
                for ft in range(2 * (i + MLP_BODY), min(2 * (i + MLP_BODY) + 2, 16)):
                    mix(ft)
            down_last(gated_unit(6), lambda: gated_unit(7))

            norm(5)
            ffn(1, 5)
            norm(6)
            for s in range(6):
                have(("kv", s))
                if s in (3, 5):
                    for b in range(NB):
                        o = open_tile(("kv", s, b))
                        up_tok_split(o[:, 0:S], parts(("kv", s), KT), S, b).then_inc(tile_done, 1)
                else:
                    tiles = [open_tile(("kT", s, f)) for f in range(2)]
                    for f in range(2):
                        up_T_split(tiles[f][:, 0:S], parts(("kv", s), KT), f * P, P,
                                   6 if s == 0 and f == 0 else None).then_inc(tile_done, 1)
                owed[0] += 1
            for s in range(2):
                tiles = [open_tile(("ch", s, m)) for m in range(2)]
                pe.wait_ge(cx_ready, s + 1)
                for h in range(2):
                    have(("cw", 2 * s + h))
                    for m in range(2):
                        for j in range(8):
                            ins = mm(tiles[m][:, 0:HD], up_unit(("cw", 2 * s + h))[:, j, m * P:(m + 1) * P],
                                     cx[:, s, 8 * h + j].rearrange("p g i -> p (g i)"), h == 0 and j == 0,
                                     h == 1 and j == 7)
                            if j == 0:
                                settle(ins)
                        if h:
                            ins.then_inc(tile_done, 1)
                    owed[0] += 1
            pe.wait_ge(cw2_in, 32)
            for m in range(2):
                tile_copied(pe, ("ch", 0, m))
            o = open_tile(("ck",))
            for half in range(2):
                for m in range(2):
                    ins = mm(o[half * 64:half * 64 + 64, 0:P], cw2[:, 0, m, :],
                             hidc[:, 0, m].rearrange("p g i -> p (g i)"), m == 0, m == 1)
                    settle(ins)
            ins.then_inc(tile_done, 1)
            for m in range(2):
                tile_copied(pe, ("ch", 1, m))
            o = open_tile(("cv",))
            for r in range(4):
                for g in range(NG):
                    for m in range(2):
                        ins = mm(o[32 * r:32 * r + 32, g * HD:(g + 1) * HD], hidc[:, 1, m, g, :], cw2[:, 1, m, :],
                                 m == 0, m == 1)
            ins.then_inc(tile_done, 1)

            ffn(2, None)
            norm(7)
            have(("qg", 0))
            o = open_tile(("qg",))
            up_T_split(o[0:3 * NH, 0:S], parts(("qg", 0), KT), 0, 3 * NH, 7).then_inc(tile_done, 1)
            owed[0] += 1
            for i in range(4):
                have(("q", i))
                for f in range(2):
                    o = open_tile(("q", 2 * i + f))
                    up_T_split(o[:, 0:S], parts(("q", i), KT), f * P, P).then_inc(tile_done, 1)
                owed[0] += 1
            tile_copied(pe, ("qg",))
            o = open_tile(("qt",))
            for b in range(NB):
                ins = turn(o[:, b * 3 * NH:(b + 1) * 3 * NH], nsa_gT[:, b * P:(b + 1) * P], 3 * NH)
                settle(ins)
            ins.then_inc(tile_done, 1)
            for i in range(8):
                tile_copied(pe, ("q", i))
            for name in (("kT", 2, 1), ("kT", 4, 1), ("kv", 5, 1), ("ck",), ("cv",)):
                tile_copied(pe, name)
            for k in (2, 3):
                pe.wait_ge(k_swapped[k], 32)

            def compressed_scores():
                for b in range(NB):
                    o = open_tile(("cs", b))
                    for j in range(NH // 2):
                        ins = mm(o[:, j * 32:(j + 1) * 32], qT[:, j, b * P:(b + 1) * P],
                                 kcT[:, j // 2].rearrange("p f i -> p (f i)"), True, True)
                        settle(ins)
                        if j < NH // 2 - 1:
                            keep_warm(2)
                    ins.then_inc(tile_done, 1)

            def compressed_probs():
                for b in range(NB):
                    o = open_tile(("ct", b))
                    pe.wait_ge(pc_ready, b + 1)
                    for g in range(NG):
                        ins = turn(o[:, g * P:(g + 1) * P],
                                   pc[:, b, 4 * g:4 * g + 4, :].rearrange("p h i -> p (h i)"))
                    ins.then_inc(tile_done, 1)

            for s in MIX2:
                if s[0] == "S":
                    scores(s[1])
                elif s[0] == "C":
                    compressed_scores()
                elif s[0] == "P":
                    compressed_probs()
                else:
                    if s == ("V", 4):
                        for b in range(NB):
                            tile_copied(pe, ("ct", b))
                    batch(s)
            pe.wait_ge(o_read, N_BATCH)
            clear_acc()
            down_all("wo")
            norm(8)
            ffn(3, 8)

        @block.scalar
        def _(act):
            link = chained(act, act_step)
            act.dma_start(const[:, 0:P], t["consts"][:, 0:P]).then_inc(ident_in, 16)
            for row, n, src in ((V_GMIX, 1, t["g_mix"]), (V_GMEM, 1, t["g_mem"]), (V_GMLP, 1, t["g_mlp"]),
                                (V_GFIN, 1, t["g_final"].rearrange("(a d) -> a d", a=1)),
                                (V_LNG, 6, t["ln_g_2"].rearrange("l n d -> (l n) d")),
                                (V_LNB, 6, t["ln_b_2"].rearrange("l n d -> (l n) d")),
                                (V_BG, 3, t["b_gate"].rearrange("a (r d) -> (a r) d", d=D))):
                act.dma_start(vec_rows[row:row + n, :], src).then_inc(vec_in, 16)
            act.dma_start(b1_rows, t["cmp_b1_2"].rearrange("s (m p) -> (s m) p", p=P)).then_inc(vec_in, 16)
            act.dma_start(pe_rows, t["cmp_pe_2"].rearrange("s (j o) d -> (s j) (o d)", o=2)).then_inc(vec_in, 16)

            def round_unit(name, i=None, offset=0):
                u, q = UNITS[name] + offset, SPLITS[name] + offset
                n = width(name)
                free = split_free(name) if i is None else i * BODY + (u - SPLIT + 1)
                act.wait_ge(arrived[u % SLOTS], (0 if i is None else i * (16 * BODY // SLOTS)) + arrival(u))
                if i is not None or free:
                    act.wait_ge(unit_used, free)
                act.activation(split_hi[:, split_slot(q), 0:n], ring[:, u % SLOTS, 0:n], ACT.Copy).then_inc(hi_ready, 1)

            def deviation(n, b):
                act.wait_ge(var_ready, NB * n + b + 1)
                src = msq[:, b:b + 1] if n < 4 else mv[:, b, 1:2]
                act.activation(sd[:, b:b + 1], src, ACT.Sqrt,
                               bias=eps[:, 0:1] if n < 4 else eps[:, 1:2]).then_inc(sd_ready, 1)

            def gain(n, b, h):
                if n == 1 and b == 0:
                    act.wait_ge(hT_ready, 4)
                name = ("n", n, b, h)
                o = tile_ready(act, name)
                for k in range(4):
                    kt = 4 * h + k
                    g = colv[:, kt * N_VEC + n:kt * N_VEC + n + 1]
                    bias = colv[:, kt * N_VEC + V_LNB + n - 4:kt * N_VEC + V_LNB + n - 3] if n >= 4 else zeros[:, 0:1]
                    ins = act.activation(hT_tmp[:, kt, b * P:(b + 1) * P], o[:, k * P:(k + 1) * P], ACT.Identity,
                                         bias=bias, scale=g)
                ins.then_inc(frees(name), 1)

            def round_half(n, b, h):
                hi = both_two[0] if n == 1 else hT_hi
                tile_copied(act, ("n", n, b, h))
                act.activation(hi[:, 4 * h:4 * h + 4, b * P:(b + 1) * P], hT_tmp[:, 4 * h:4 * h + 4, b * P:(b + 1) * P],
                               ACT.Copy).then_inc(hT_rounded, 1)

            def turned(n, between=None):
                gain(n, 0, 0)
                round_half(n, 0, 0)
                if between:
                    between()
                gain(n, 0, 1)
                round_half(n, 0, 1)
                gain(n, 1, 0)
                round_half(n, 1, 0)
                round_half(n, 1, 1)

            def norm(n):
                deviation(n, 0)
                turned(n, lambda: deviation(n, 1))

            def copy_tile(name, dst, cols=S, scale=None):
                o = tile_ready(act, name)
                if scale is None:
                    ins = act.activation(dst, o[:, 0:cols], ACT.Copy)
                else:
                    ins = act.activation(dst, o[:, 0:cols], ACT.Copy, scale=scale)
                ins.then_inc(frees(name), 1)

            act.wait_ge(fills, 1)
            deviation(0, 0)
            deviation(0, 1)
            round_unit(("proj", 0))
            act.wait_ge(cols_ready, 1)
            turned(0)
            round_unit(("proj", 1))
            round_unit(("proj", 2))
            ahead = ORDER[3:]
            for i in range(N_PROJ):
                n = min(UC, C_GATE - i * UC)
                for b in range(NB):
                    copy_tile(("p", i, b), proj[:, b, i * UC:i * UC + n], n)
                if i == 1:
                    act.wait_ge(angle_ready, 1)
                    act.activation(trig[:], ang[:, 2:4], ACT.Sin).then_inc(trig_ready, 1)
                if i == 4:
                    turned(1)
                round_unit(ahead.pop(0))
                if i == 2:
                    deviation(1, 0)
                    deviation(1, 1)
            for f in range(2):
                copy_tile(("mk", f), kmT[:, f, :])
            round_unit(ahead.pop(0))
            for b in range(NB):
                copy_tile(("mv", b), vm[:, b, :])
            def gate(i):
                for f in (2 * i, 2 * i + 1):
                    o = tile_ready(act, ("g", f))
                    row = (f % 8) * N_VEC + V_BG + f // 8
                    act.activation(gate_tile(f), o[:, 0:S], ACT.Sigmoid,
                                   bias=colv[:, row:row + 1]).then_inc(frees(("g", f)), 1)

            gate(0)
            round_unit(ahead.pop(0))
            for i in range(-(-N_TURN // 2)):
                n = min(2, N_TURN - 2 * i)
                copy_tile(("turn", i), qkT[:, 2 * i:2 * i + n, :].rearrange("p a s -> p (a s)"), n * S)

            def exps(n):
                m = n % PROBS
                act.wait_ge(neg_ready, n + 1)
                if n < 2:
                    act.activation(sink_exp[:, m], sink_in[:, m], ACT.Exp)
                for k, tile in enumerate(attention(n)):
                    s = prob[m][:, k, 0:tile[2]]
                    ins = act.activation(s, s, ACT.Exp, bias=neg_max[:, m, k:k + 1], accum_out=row_sum[:, m, k:k + 1])
                ins.then_inc(exp_ready, 1)

            def copy_probs(n):
                tiles = attention(n)
                for p in range(4):
                    o = tile_ready(act, ("T", n, p))
                    if 4 * n + p >= 4:
                        act.wait_ge(pv_done, 4 * n + p - 3)
                    w = tiles[2 * p][2]
                    dst = probT[:, (4 * n + p) % 4].rearrange("p a k q -> p a (k q)")[:, :, 0:w]
                    src = o[:, :].rearrange("p (a s) -> p a s", a=2)[:, :, 0:w]
                    act.activation(dst, src, ACT.Copy).then_inc(frees(("T", n, p)), 1)

            def copy_out(n):
                act.wait_ge(pv_done, 4 * n + 4)
                dst, src = out_place(n, 0)
                act.activation(dst, src, ACT.Copy).then_inc(o_rounded, 1)

            act.wait_ge(sink_ld, 16)
            act.wait_ge(rel_stored, 16)
            for s in MIX1:
                if s[0] == "S":
                    exps(s[1])
                elif s[0] == "G":
                    gate(s[1])
                    round_unit(ahead.pop(0))
                if "T" in s[0]:
                    copy_probs(s[1])
                if "V" in s[0]:
                    copy_out(s[1])
            round_unit(("pswa", 1))

            between = {2: [("pdm", 1)], 4: [("wout", 0)], 7: [("wout", i) for i in (1, 2, 3)] + [("mu", 0)]}
            for ft in range(KT):
                act.wait_ge(merged_raw, ft + 1)
                act.activation(hT_hi[:, ft, :], merge_tmp[:, ft % 2, 2], ACT.Copy).then_inc(merged_rounded, 1)
                for name in between.get(ft, ()):
                    round_unit(name)

            def activate(b, done, func, cols):
                act.wait_ge(tile_done, done)
                act.activation(act_out[:, b, 0:cols], banks[b][:, 0:cols], func).then_inc(act_ready, 1)

            def mlp():
                first = ("mu", 1)
                seq = TILES[("m", 0)][2] + 1
                round_unit(first)
                with act.Fori(0, (MLP_CHUNKS - 1) // MLP_BODY) as i:
                    for k in range(MLP_BODY):
                        activate(TILES[("m", k)][0], i * MLP_BODY + (seq + k), ACT.Relu, 2 * S)
                        round_unit(first, i, 2 * k + 1)
                        round_unit(first, i, 2 * k + 2)
                activate(TILES[("m", MLP_CHUNKS - 1)][0], seq + MLP_CHUNKS - 1, ACT.Relu, 2 * S)

            def ffn(f):
                first = ("w1", f, 1)
                seq = TILES[("f", f, 0, 0)][2] + 1

                def silu(k, ft, i=None):
                    done = seq + 2 * k + ft
                    activate(TILES[("f", f, k, ft)][0], done if i is None else i * 2 * FFN_BODY + done, ACT.Silu, S)

                round_unit(first)
                with act.Fori(0, (FFN_CHUNKS - 1) // FFN_BODY) as i:
                    for k in range(FFN_BODY):
                        silu(k, 0, i)
                        silu(k, 1, i)
                        for j in range(3 * k + 1, 3 * k + 4):
                            round_unit(first, i, j)
                silu(FFN_CHUNKS - 1, 0)
                silu(FFN_CHUNKS - 1, 1)

            norm(2)
            mlp()
            round_unit(("w1", 0, 0))
            norm(3)
            round_unit(("w3", 0, 0))
            ffn(0)
            mixer = [(x, i) for x in ("sv", "su", "so") for i in range(8)]
            round_unit(mixer[0])
            norm(4)
            round_unit(mixer[1])
            round_unit(mixer[2])
            for i in range(8):
                for b in range(NB):
                    o = tile_ready(act, ("sv", i, b))
                    act.activation(vtok[:, b, i * UC:(i + 1) * UC], o[:, 0:S], ACT.Gelu).then_inc(frees(("sv", i, b)), 1)
                round_unit(mixer[i + 3])
            for i in range(2):
                copy_tile(("wst", i), wsT[:, 4 * i:4 * i + 4, :].rearrange("p a s -> p (a s)"), 4 * P)
            for i in range(8):
                for f in range(2):
                    o = tile_ready(act, ("su", 2 * i + f))
                    act.activation(uT[:, 2 * i + f, :], o[:, 0:S], ACT.Gelu).then_inc(frees(("su", 2 * i + f)), 1)
                round_unit(mixer[i + 11])
                if i == 1:
                    for b in range(NB):
                        act.wait_ge(sgu_var, b + 1)
                        act.activation(sd[:, b:b + 1], mv[:, b, 1:2], ACT.Sqrt, bias=eps[:, 1:2]).then_inc(sgu_sd, 1)
            for i in range(3, 8):
                round_unit(("so", i))
            round_unit(("w1", 1, 0))
            norm(5)
            round_unit(("w3", 1, 0))
            ffn(1)
            round_unit(("kv", 0))
            norm(6)
            round_unit(("kv", 1))
            round_unit(("kv", 2))
            key_slot = {0: 0, 1: 1, 2: 2, 4: 3}
            for s in range(6):
                if s in (3, 5):
                    for b in range(NB):
                        copy_tile(("kv", s, b), vv[:, (s - 3) // 2, b, :])
                else:
                    for f in range(2):
                        copy_tile(("kT", s, f), ka[:, key_slot[s], f, :])
                    tile_copied(act, ("kT", s, 1))
                    for half in range(2):
                        act.dma_start(kb[64 * (1 - half):64 * (1 - half) + 64, key_slot[s]],
                                      ka[64 * half:64 * half + 64, key_slot[s]]).then_inc(k_swapped[key_slot[s]], 16)
                if s + 3 < 6:
                    round_unit(("kv", s + 3))
            act.wait_ge(fills, 3)
            for s in range(2):
                for m in range(2):
                    o = tile_ready(act, ("ch", s, m))
                    act.activation(hidc[:, s, m, :, 0:N_CMP], o[:, 0:HD].rearrange("p (g i) -> p g i", g=NG)[:, :, 0:N_CMP],
                                   ACT.Gelu, bias=colv[:, V_B1 + 2 * s + m:V_B1 + 2 * s + m + 1]).then_inc(
                                       frees(("ch", s, m)), 1)
                round_unit((("w1", "w3")[s], 2, 0))
            o = tile_ready(act, ("ck",))
            for half in range(2):
                part = slice(64 * half, 64 * half + 64)
                ins = act.activation(kcT[part, :, half, :], o[part, 0:P].rearrange("p (g i) -> p g i", g=NG)[:, :, 0:16],
                                     ACT.Copy)
            ins.then_inc(frees(("ck",)), 1)
            copy_tile(("cv",), vc)
            ffn(2)
            round_unit(("qg", 0))
            norm(7)
            round_unit(("q", 0))
            round_unit(("q", 1))
            o = tile_ready(act, ("qg",))
            act.activation(nsa_gT, o[0:3 * NH, 0:S], ACT.Sigmoid).then_inc(frees(("qg",)), 1)
            round_unit(("q", 2))
            for i in range(8):
                copy_tile(("q", i), qT[:, i, :], scale=HD ** -0.5)
                if i == 1:
                    round_unit(("q", 3))
            copy_tile(("qt",), nsa_g.rearrange("p b c -> p (b c)"), NB * 3 * NH)
            for i in range(WO_EARLY):
                round_unit(("wo", i))
            for s in MIX2:
                if s[0] == "S":
                    if s[1] < 6:
                        exps(s[1])
                elif s[0] == "C":
                    for b in range(NB):
                        act.wait_ge(cscore_ready, b + 1)
                        act.activation(sc[:, b, :, 0:CMP_KEYS[b]], sc[:, b, :, 0:CMP_KEYS[b]],
                                       ACT.Exp).then_inc(cexp_ready, 1)
                elif s[0] == "P":
                    for b in range(NB):
                        o = tile_ready(act, ("ct", b))
                        act.activation(pcT[:, :, b * P:(b + 1) * P], o[:, :].rearrange("p (g q) -> p g q", g=NG),
                                       ACT.Copy).then_inc(frees(("ct", b)), 1)
                if "T" in s[0]:
                    copy_probs(s[1])
                    if s[1] + 3 < N_BATCH:
                        exps(s[1] + 2)
                if "V" in s[0]:
                    copy_out(s[1])
                    if s[1] == N_BATCH - 4:
                        exps(N_BATCH - 1)
            for i in range(WO_EARLY, 4):
                round_unit(("wo", i))
            round_unit(("w1", 3, 0))
            norm(8)
            round_unit(("w3", 3, 0))
            ffn(3)
            deviation(9, 0)
            deviation(9, 1)

        @block.vector
        def _(dve):
            link = chained(dve, dve_step)

            dve.sem_inc(split_ready, AHEAD)

            def angles():
                dve.wait_ge(const_in, 16)
                dve.wait_ge(pos_in, 16)
                link(dve.tensor_copy(pos_f[:], pos_i[:]))
                for b in range(NB):
                    ins = dve.tensor_scalar(ang[:, 0, b, :], freq, pos_f[:, b:b + 1], None, ALU.mult)
                link(ins)
                magic = 1.5 * 2.0 ** 23
                link(dve.tensor_scalar(ang[:, 1], ang[:, 0], 1.0 / (2 * np.pi), magic, ALU.mult, ALU.add))
                link(dve.tensor_scalar(ang[:, 1], ang[:, 1], magic, None, ALU.subtract))
                rest = 2 * np.pi
                for k in range(4):
                    part = float(np.round(rest * 2.0 ** (5 + 8 * k)) / 2.0 ** (5 + 8 * k)) if k < 3 else float(np.float32(rest))
                    rest -= part
                    link(dve.scalar_tensor_tensor(out=ang[:, 0], in0=ang[:, 1], scalar=-part, in1=ang[:, 0],
                                                  op0=ALU.mult, op1=ALU.add))
                pi = float(np.nextafter(np.float32(np.pi), np.float32(0)))
                link(dve.tensor_scalar(ang[:, 2], ang[:, 0], pi, -pi, ALU.min, ALU.max))
                link(dve.scalar_tensor_tensor(out=ang[:, 1], in0=ang[:, 2], scalar=-1.0, in1=ang[:, 2],
                                              op0=ALU.mult, op1=ALU.max))
                dve.tensor_scalar(ang[:, 3], ang[:, 1], -1.0, float(np.pi / 2), ALU.mult, ALU.add).then_inc(angle_ready, 1)

            def low_unit(name, i=None, offset=0):
                u, q = UNITS[name] + offset, SPLITS[name] + offset
                dve.wait_ge(hi_ready, (0 if i is None else i * BODY) + (q + 1))
                if i is None and q in (GATE_0 + GATES, SPLITS[("wo", WO_EARLY)]):
                    dve.wait_ge(split_ready, AHEAD + q)
                n, place = width(name), split_slot(q)
                dve.tensor_tensor(split_lo[:, place, 0:n], ring[:, u % SLOTS, 0:n],
                                  split_hi[:, place, 0:n].bitcast(F32), ALU.subtract).then_inc(split_ready, 1)

            def norm_rows(n):
                src = memt if n == 1 else resid
                if n == 1:
                    dve.wait_ge(mem_in, 16)
                elif n >= 4:
                    dve.wait_ge(resid_ready, NB * (n - 3))
                def add(b):
                    if n < 2:
                        return
                    for h in range(2):
                        if b == 0 or h == 0:
                            dve.wait_ge(half_done, 2 * (n - 2) + b + 1)
                        else:
                            dve.wait_ge(unit_used, UNITS[ACC_DONE[n]] + 1)
                        r = resid[:, b, h * 512:(h + 1) * 512]
                        ins = dve.scalar_tensor_tensor(out=r, in0=r, scalar=ALPHA if n >= 4 else 1.0,
                                                       in1=acc[2 * b + h][:, :], op0=ALU.mult, op1=ALU.add)
                        link(ins)
                        if b == 1:
                            link(statistics(b, h))

                def statistics(b, h):
                    return dve.bn_stats(stats[:, b, h, :], src[:, b, h * 512:(h + 1) * 512])

                def variance(b):
                    if n == 0:
                        dve.wait_ge(x_in[b], 16)
                    if n < 2 or b == 0:
                        statistics(b, 0)
                        link(statistics(b, 1))
                    ins = dve.bn_aggr(mv[:, b, :], stats[:, b, 0:2, :])
                    if n < 4:
                        link(ins)
                        ins = dve.scalar_tensor_tensor(out=msq[:, b:b + 1], in0=mv[:, b, 0:1], scalar=mv[:, b, 0:1],
                                                       in1=mv[:, b, 1:2], op0=ALU.mult, op1=ALU.add)
                    ins.then_inc(var_ready, 1)

                def scale(b):
                    dve.wait_ge(sd_ready, NB * n + b + 1)
                    link(dve.reciprocal(rstd[:, b:b + 1], sd[:, b:b + 1]))
                    if n == 1 and b == 0:
                        for bb in range(NB):
                            for h in range(2):
                                dve.wait_ge(tile_done, TILES[("n", 0, bb, h)][2] + 1)
                    if n < 4:
                        ins = dve.tensor_scalar(xn[:, b, :], src[:, b, :], rstd[:, b:b + 1], None, ALU.mult)
                    else:
                        ins = dve.tensor_scalar(xn[:, b, :], src[:, b, :], mv[:, b, 0:1], rstd[:, b:b + 1],
                                                ALU.subtract, ALU.mult)
                    ins.then_inc(xn_ready, 1)

                for b in range(NB):
                    add(b)
                    variance(b)
                    scale(b)

            def norm_turned(n):
                hi, lo = both_two if n == 1 else both_hT
                for b in range(NB):
                    if b == 1:
                        name = ("n", n, 1, 1)
                        o = tile_ready(dve, name)
                        for k in range(4):
                            kt = 4 + k
                            g = colv[:, kt * N_VEC + n:kt * N_VEC + n + 1]
                            bias = colv[:, kt * N_VEC + V_LNB + n - 4:kt * N_VEC + V_LNB + n - 3] if n >= 4 else 0.0
                            ins = dve.tensor_scalar(hT_tmp[:, kt, P:S], o[:, k * P:(k + 1) * P], g,
                                                    bias if n >= 4 else None, ALU.mult, *([ALU.add] if n >= 4 else []))
                        ins.then_inc(frees(name), 1)
                        tile_copied(dve, name)
                    cols = slice(b * P, (b + 1) * P)
                    for h in range(2):
                        dve.wait_ge(hT_rounded, 2 * NB * n + 2 * b + h + 1)
                        ks = slice(4 * h, 4 * h + 4)
                        dve.tensor_tensor(lo[:, ks, cols], hT_tmp[:, ks, cols], hi[:, ks, cols].bitcast(F32),
                                          ALU.subtract).then_inc(hT_ready, 1)

            def norm(n):
                norm_rows(n)
                norm_turned(n)

            norm_rows(0)
            low_unit(("proj", 0))
            o = tile_ready(dve, ("vec",))
            dve.tensor_copy(colv[:], o[:, 0:N_COLV]).then_inc(frees(("vec",)), 1)
            tile_copied(dve, ("vec",))
            dve.sem_inc(cols_ready, 1)
            norm_turned(0)
            low_unit(("proj", 1))
            low_unit(("proj", 2))
            angles()
            low_unit(("proj", 3))
            low_unit(("proj", 4))
            low_unit(("proj", 5))
            norm_rows(1)
            low_unit(("proj", 6))
            o = tile_ready(dve, ("rel",))
            dve.tensor_copy(rel_out, o[0:NH, 0:N_REL]).then_inc(frees(("rel",)), 1)
            norm_turned(1)

            dve.wait_ge(trig_ready, 1)

            def rope(c0, nh, places):
                v = proj[:, :, c0:c0 + nh * HD].rearrange("p b (h e) -> p b h e", e=HD)
                x1, x2 = v[:, :, :, 0:32], v[:, :, :, 32:64]
                sin, cos = (trig[:, i].unsqueeze(2).to_broadcast([P, NB, nh, 32]) for i in range(2))
                tmp = [rope_tmp[:, i, :, 0:nh, :] for i in range(4)]
                dve.tensor_tensor(tmp[0], x1, cos, ALU.mult)
                dve.tensor_tensor(tmp[1], x2, sin, ALU.mult)
                dve.tensor_tensor(tmp[2], x2, cos, ALU.mult)
                link(dve.tensor_tensor(tmp[3], x1, sin, ALU.mult))
                for half, (a, b, op) in enumerate(((0, 1, ALU.subtract), (2, 3, ALU.add))):
                    for h0, n, dst in places:
                        ins = dve.tensor_tensor(dst[:, :, :, half * 32:half * 32 + 32], tmp[a][:, :, h0:h0 + n, :],
                                                tmp[b][:, :, h0:h0 + n, :], op)
                return ins

            def heads(tile, n):
                return roped[:, :, tile * P:tile * P + n * HD].rearrange("p b (h e) -> p b h e", e=HD)

            qs = roped[:, :, 0:4 * P].rearrange("p b (j v e) -> p b j v e", j=4, v=2)
            for b in range(NB):
                tile_copied(dve, ("p", (C_VS - 1) // UC, b))
            link(rope(C_QS, 10, [(0, 4, qs[:, :, :, 0, :]), (4, 4, qs[:, :, :, 1, :]), (8, 2, heads(T_KS, 2))]))
            for b in range(NB):
                tile_copied(dve, ("p", (C_VD - 1) // UC, b))
            kd = heads(T_KD, 2)
            link(rope(C_QD, 5, [(0, 4, heads(T_QD, 4)), (4, 1, kd[:, :, 0:1]), (4, 1, kd[:, :, 1:2])]))
            for name in (("memkv", 0), ("memkv", 1)):
                low_unit(name)
            for b in range(NB):
                tile_copied(dve, ("p", N_PROJ - 1, b))
            ki = heads(T_KI, 2)
            rope(C_QI, 5, [(0, 4, heads(T_QI, 4)), (4, 1, ki[:, :, 0:1]), (4, 1, ki[:, :, 1:2])]).then_inc(roped_ready, 1)
            link(dve.tensor_scalar(wsc[:], proj[:, :, C_WI:C_WI + N_IDX], N_IDX ** -0.5 * HD ** -0.5, None, ALU.mult))

            def index():
                for h in range(N_IDX):
                    n = PAIRS[("I", h)]
                    dve.wait_ge(score_done, n + 1)
                    o = score_banks[n % 3]
                    for b in range(NB):
                        w = P * (b + 1)
                        s = isc[:, b, 0:w]
                        ins = dve.tensor_scalar(idx_tmp[:, 0:w] if h else s, o[:, b * S:b * S + w], 0.0,
                                                wsc[:, b, h:h + 1], ALU.max, ALU.mult)
                        if b == 1:
                            ins.then_inc(score_read[n % 3], 1)
                            dve.wait_ge(score_read[n % 3], n // 3 + 1)
                        else:
                            link(ins)
                        if h:
                            link(dve.tensor_tensor(s, s, idx_tmp[:, 0:w], ALU.add))
                for b in range(NB):
                    w = P * (b + 1)
                    link(dve.tensor_tensor(isc[:, b, 0:w], isc[:, b, 0:w], mask_causal[:, S - w:S], ALU.add))

            def select():
                for b in range(NB):
                    w = P * (b + 1)
                    s = isc[:, b, 0:w]
                    for _ in range(TOPK // 8):
                        link(dve.max(best[:], s))
                        link(dve.match_replace(s, best[:], s, GONE))
                    link(dve.tensor_scalar(maskD[:, b, 0:w], s, GONE / 2, NEG, ALU.is_ge, ALU.mult))
                    link(dve.tensor_tensor(maskD[:, b, 0:w], maskD[:, b, 0:w], mask_causal[:, S - w:S], ALU.add))

            def maxima(n):
                m = n % PROBS
                if n >= PROBS:
                    dve.wait_ge(tile_done, TILES[("T", n - PROBS, 3)][2] + 1)
                tiles = attention(n)
                for p in range(4):
                    pair = PAIRS[(n, p)]
                    dve.wait_ge(score_done, pair + 1)
                    o = score_banks[pair % 3]
                    for a in range(2):
                        k = 2 * p + a
                        _, _, w, addend, scale, first = tiles[k][:6]
                        ins = dve.tensor_tensor_reduce(prob[m][:, k, 0:w], o[:, a * S:a * S + w], addend, scale, first,
                                                       ALU.add, ALU.max, row_max[:, m, k:k + 1])
                    ins.then_inc(score_read[pair % 3], 1)
                dve.wait_ge(score_read[pair % 3], pair // 3 + 1)
                ins = dve.tensor_scalar(neg_max[:, m, :], row_max[:, m, :], -1.0, None, ALU.mult)
                if n < 2:
                    link(ins)
                    ins = dve.tensor_tensor(sink_in[:, m], sinks[:], neg_max[:, m, :], ALU.add)
                ins.then_inc(neg_ready, 1)

            def normalize(n):
                m = n % PROBS
                dve.wait_ge(exp_ready, n + 1)
                if n < 2:
                    link(dve.tensor_tensor(row_sum[:, m, :], row_sum[:, m, :], sink_exp[:, m], ALU.add))
                link(dve.reciprocal(row_rcp[:, m], row_sum[:, m, :]))
                if n >= 4:
                    h = 2 * (n - 4)
                    r = row_rcp[:, m].rearrange("p (h b r) -> p h b r", h=2, b=NB)
                    g = nsa_g[:, :, 3 * h:3 * h + 6].rearrange("p b (h r) -> p h b r", h=2)[:, :, :, 1:3]
                    for hh in range(2):
                        ins = dve.tensor_tensor(r[:, hh], r[:, hh], g[:, hh], ALU.mult)
                    link(ins)
                for k, tile in enumerate(attention(n)):
                    s = prob[m][:, k, 0:tile[2]]
                    ins = dve.tensor_scalar(s, s, row_rcp[:, m, k:k + 1], None, ALU.mult)
                    if k % 2:
                        ins.then_inc(prob_ready, 1)

            def low_out(n):
                dve.wait_ge(o_rounded, n + 1)
                hi, src = out_place(n, 0)
                lo, _ = out_place(n, 1)
                dve.tensor_tensor(lo, src, hi.bitcast(F32), ALU.subtract).then_inc(o_read, 1)

            dve.wait_ge(fills, 1)
            dve.wait_ge(sink_ld, 16)
            dve.wait_ge(unit_used, UNITS[("memkv", 1)] + 1)
            index()
            maxima(0)
            maxima(1)
            normalize(0)
            select()
            low_out(0)
            maxima(2)
            normalize(1)
            low_out(1)
            maxima(3)
            normalize(2)
            normalize(3)
            low_out(2)
            low_unit(("pswa", 0))
            low_unit(("pdm", 0))
            low_out(3)
            low_unit(("pswa", 1))

            tile_copied(dve, ("g", 23))

            for ft in range(KT):
                mt = merge_tmp[:, ft % 2]
                if ft >= 2:
                    dve.wait_ge(merged_ready, ft - 1)
                o = tile_ready(dve, ("mg", ft, 0))
                dve.tensor_tensor(mt[:, 0], o[:, 0:S], gate_tile(ft), ALU.mult)
                dve.tensor_tensor(mt[:, 1], o[:, S:2 * S], gate_tile(8 + ft), ALU.mult).then_inc(frees(("mg", ft, 0)), 1)
                tile_copied(dve, ("mg", ft, 0))
                o = tile_ready(dve, ("mg", ft, 1))
                link(dve.tensor_tensor(mt[:, 0], mt[:, 0], mt[:, 1], ALU.add))
                dve.tensor_tensor(mt[:, 2], o[:, 0:S], gate_tile(16 + ft), ALU.mult).then_inc(frees(("mg", ft, 1)), 1)
                tile_copied(dve, ("mg", ft, 1))
                dve.tensor_tensor(mt[:, 2], mt[:, 0], mt[:, 2], ALU.add).then_inc(merged_raw, 1)
                if ft in (2, 4):
                    low_unit({2: ("pdm", 1), 4: ("wout", 0)}[ft])
            for name in [("wout", i) for i in (1, 2, 3)] + [("mu", 0)]:
                low_unit(name)

            def split_hidden(tile, at_hid):
                raw, hi, lo = (x.rearrange("p f s -> p (f s)") if len(x.shape) == 3 else x for x in at_hid)
                dve.tensor_copy(hi, raw).then_inc(hid_rounded, 1)
                dve.wait_ge(hid_rounded, tile)
                return dve.tensor_tensor(lo, raw, hi.bitcast(F32), ALU.subtract)

            def mlp():
                first = ("mu", 1)

                def hidden(c, i=None):
                    t0, t6 = (0, 0) if i is None else (i * MLP_BODY, i * BODY)
                    b, held, _ = TILES[("m", c)]
                    x = c % MLP_BODY
                    dve.wait_ge(unit_used, t6 + (UNITS[first] - 2 * MLP_BODY + 2 + 2 * c))
                    dve.wait_ge(act_ready, t0 + (c + 1))
                    dve.tensor_tensor(hid[:, x, :], act_out[:, b, :], banks[b][:, :], ALU.mult).then_inc(tile_read[b], 1)
                    dve.wait_ge(tile_read[b], (0 if i is None else i) + (held + 1))
                    split_hidden(t0 + (c + 1), (hid[:, x, :], hid_hi[:, x], hid_lo[:, x])).then_inc(hid_ready, 1)

                with dve.Fori(0, (MLP_CHUNKS - 1) // MLP_BODY) as i:
                    for k in range(MLP_BODY):
                        low_unit(first, i, 2 * k)
                        hidden(k, i)
                        low_unit(first, i, 2 * k + 1)
                low_unit(("md", MLP_CHUNKS - 1))
                hidden(MLP_CHUNKS - 1)

            def ffn(f):
                first = ("w1", f, 1)
                base = MLP_CHUNKS + f * 2 * FFN_CHUNKS

                def hidden(c, ft, i=None):
                    t4, t6 = (0, 0) if i is None else (i * 2 * FFN_BODY, i * BODY)
                    b, held, _ = TILES[("f", f, c, ft)]
                    x = c % FFN_BODY
                    if ft == 0:
                        dve.wait_ge(unit_used, t6 + (UNITS[first] - 3 * FFN_BODY + 3 + 3 * c))
                    dve.wait_ge(act_ready, t4 + (base + 2 * c + ft + 1))
                    raw = hid[:, ft, 0:S]
                    dve.scalar_tensor_tensor(out=raw, in0=act_out[:, b, 0:S], scalar=0.5, in1=banks[b][:, S:2 * S],
                                             op0=ALU.mult, op1=ALU.mult).then_inc(tile_read[b], 1)
                    dve.wait_ge(tile_read[b], (0 if i is None else i) + (held + 1))
                    ins = split_hidden(t4 + (base + (16 if f else 0) + 2 * c + ft + 1),
                                       (raw, hid_hi[:, x, ft], hid_lo[:, x, ft]))
                    if ft == 1:
                        ins.then_inc(hid_ready, 1)

                with dve.Fori(0, (FFN_CHUNKS - 1) // FFN_BODY) as i:
                    for k in range(FFN_BODY):
                        low_unit(first, i, 3 * k)
                        hidden(k, 0, i)
                        hidden(k, 1, i)
                        low_unit(first, i, 3 * k + 1)
                        low_unit(first, i, 3 * k + 2)
                low_unit(("w2", f, FFN_CHUNKS - 1))
                hidden(FFN_CHUNKS - 1, 0)
                hidden(FFN_CHUNKS - 1, 1)

            norm(2)
            mlp()
            low_unit(("w1", 0, 0))
            norm(3)
            low_unit(("w3", 0, 0))
            ffn(0)
            mixer = [(x, i) for x in ("sv", "su", "so") for i in range(8)]
            low_unit(mixer[0])
            norm(4)
            low_unit(mixer[1])
            low_unit(mixer[2])
            for i in range(3, 11):
                low_unit(mixer[i])
            def v_stats(b):
                tile_copied(dve, ("sv", 7, b))
                for k in range(4):
                    ins = dve.bn_stats(stats[:, b, k, :], vtok[:, b, k * 512:(k + 1) * 512])
                link(ins)
                dve.bn_aggr(mv[:, b, :], stats[:, b, :, :]).then_inc(sgu_var, 1)

            v_stats(0)
            low_unit(mixer[11])
            v_stats(1)
            low_unit(mixer[12])
            dve.wait_ge(sgu_in, 16 * 4)
            rest_units = mixer[13:19]
            for b in range(NB):
                dve.wait_ge(sgu_sd, b + 1)
                link(dve.reciprocal(rstd[:, b:b + 1], sd[:, b:b + 1]))
                link(dve.tensor_scalar(vtok[:, b, :], vtok[:, b, :], mv[:, b, 0:1], rstd[:, b:b + 1],
                                       ALU.subtract, ALU.mult))
                if rest_units:
                    low_unit(rest_units.pop(0))
                link(dve.tensor_tensor(vtok[:, b, :], vtok[:, b, :], sgu_g, ALU.mult))
                if rest_units:
                    low_unit(rest_units.pop(0))
                dve.tensor_tensor(vtok[:, b, :], vtok[:, b, :], sgu_b, ALU.add).then_inc(v_ready, 1)
            for name in rest_units:
                low_unit(name)

            def gated(i):
                if i >= MLP_BODY:
                    dve.wait_ge(unit_used, UNITS[("so", i - MLP_BODY)] + 1)
                for ft in (2 * i, 2 * i + 1):
                    tile_copied(dve, ("su", ft))
                    o = tile_ready(dve, ("mix", ft))
                    raw = hid[:, ft % 2, 0:S]
                    bias = bs_bc[:, ft // 2 * P:(ft // 2 + 1) * P].unsqueeze(1).to_broadcast([P, NB, P])
                    dve.tensor_tensor(raw.rearrange("p (b s) -> p b s", s=P), o[:, 0:S].rearrange("p (b s) -> p b s", s=P),
                                      bias, ALU.add).then_inc(frees(("mix", ft)), 1)
                    tile_copied(dve, ("mix", ft))
                    link(dve.tensor_tensor(raw, raw, uT[:, ft, :], ALU.mult))
                    ins = split_hidden(MLP_CHUNKS + 2 * FFN_CHUNKS + ft + 1,
                                       (raw, hid_hi[:, i % MLP_BODY, ft % 2], hid_lo[:, i % MLP_BODY, ft % 2]))
                ins.then_inc(hid_ready, 1)

            for i in range(MLP_BODY):
                gated(i)
            for i in range(MLP_BODY, 8):
                gated(i)
                low_unit(("so", i))
            low_unit(("w1", 1, 0))
            norm(5)
            low_unit(("w3", 1, 0))
            ffn(1)
            low_unit(("kv", 0))
            norm(6)
            low_unit(("kv", 1))
            low_unit(("kv", 2))
            low_unit(("kv", 3))
            low_unit(("kv", 4))
            dve.wait_ge(fills, 3)
            for s in range(2):
                tile_copied(dve, ("kT", s, 1))
                dve.wait_ge(k_swapped[s], 32)
                for g in range(NG):
                    for odd in range(2):
                        part = slice(64 * odd, 64 * odd + 64)
                        src = (ka if g % 2 == odd else kb)[part, s, g // 2, :]
                        rows = src.rearrange("p (c j o) -> p o j c", o=2, j=8)[:, odd]
                        pe_col = colv[part, V_PE + 16 * s:V_PE + 16 * s + 16].unsqueeze(2).to_broadcast([64, 16, N_CMP])
                        for half in range(2):
                            ins = dve.tensor_tensor(cx[part, s, 8 * half:8 * half + 8, g, 0:N_CMP],
                                                    rows[:, :, half:half + N_CMP], pe_col[:, 8 * half:8 * half + 8, :],
                                                    ALU.add)
                ins.then_inc(cx_ready, 1)
                if s == 0:
                    low_unit(("kv", 5))
            low_unit(("w1", 2, 0))
            low_unit(("w3", 2, 0))
            ffn(2)
            low_unit(("qg", 0))
            norm(7)
            for i in range(4):
                low_unit(("q", i))

            dve.wait_ge(rel_back, 16)
            tile_copied(dve, ("qt",))
            dve.wait_ge(unit_used, UNITS[("q", 3)] + 1)
            dve.wait_ge(resid_ready, NB * 5)
            for b in range(NB):
                w = CMP_KEYS[b]
                first = (P if b == 0 else 0) + 31
                v = sc[:, b, :, 0:w]
                o = tile_ready(dve, ("cs", b))
                dve.tensor_tensor(v, o[:, 0:S].rearrange("p (h i) -> p h i", i=16)[:, :, 0:w],
                                  rel[:, :, first:first + 16 * (w - 1) + 1:16], ALU.add).then_inc(frees(("cs", b)), 1)
                tile_copied(dve, ("cs", b))
                link(dve.tensor_reduce(cmax[:], v, AX.X, ALU.max))
                dve.tensor_tensor(v, v, cmax[:].unsqueeze(2).to_broadcast([P, NH, w]),
                                  ALU.subtract).then_inc(cscore_ready, 1)
            maxima(4)
            for b in range(NB):
                w = CMP_KEYS[b]
                v = sc[:, b, :, 0:w]
                dve.wait_ge(cexp_ready, b + 1)
                link(dve.tensor_reduce(csum[:], v, AX.X, ALU.add))
                link(dve.reciprocal(crcp[:], csum[:]))
                link(dve.tensor_tensor(crcp[:], crcp[:], nsa_g[:, b, :].rearrange("p (h r) -> p h r", r=3)[:, :, 0], ALU.mult))
                if b == 0:
                    link(dve.tensor_scalar(crcp[:], crcp[:], row_valid, None, ALU.mult))
                dve.tensor_tensor(pc[:, b, :, 0:w], v, crcp[:].unsqueeze(2).to_broadcast([P, NH, w]),
                                  ALU.mult).then_inc(pc_ready, 1)
            maxima(5)
            normalize(4)
            for n in range(5, N_BATCH):
                if n + 1 < N_BATCH:
                    maxima(n + 1)
                normalize(n)
                if n >= 6 and n + 1 < N_BATCH:
                    low_out(n - 2)
            low_out(N_BATCH - 3)
            low_out(N_BATCH - 2)
            low_out(N_BATCH - 1)
            for i in range(WO_EARLY, 4):
                low_unit(("wo", i))
            low_unit(("w1", 3, 0))
            norm(8)
            low_unit(("w3", 3, 0))
            ffn(3)
            norm_rows(9)
            dve.wait_ge(gb_in, 16 * 13)
            dve.wait_ge(xn_ready, NB * 10)
            for h in range(2):
                half = slice(h * 512, (h + 1) * 512)
                link(dve.tensor_tensor(xn[:, 1, half], xn[:, 1, half], gain_bc[:, half], ALU.mult))
                dve.tensor_tensor(xn[:, 1, half], xn[:, 1, half], bias_bc[:, half], ALU.add).then_inc(out_ready[1], 1)

        @block.gpsimd
        def _(pool):
            link = chained(pool, pool_step)

            def low_unit(name):
                q, u, place = SPLITS[name], UNITS[name], split_slot(SPLITS[name])
                pool.wait_ge(hi_ready, q + 1)
                pool.wait_ge(split_ready, AHEAD + q)
                pool.tensor_tensor(split_lo[:, place, :], ring[:, u % SLOTS, :], split_hi[:, place, :].bitcast(F32),
                                   ALU.subtract).then_inc(split_ready, 1)

            pool.memset(zeros[:], 0.0)
            pool.memset(ones[:], 1.0)
            pool.memset(eps[:, 0:1], RMS_EPS)
            link(pool.memset(eps[:, 1:2], LN_EPS))
            pool.memset(rel_rows[32:33, :], NEG).then_inc(fills, 1)

            def load_rows(n):
                if n == 3:
                    pool.dma_start(gain_bc[:], t["g_final"].partition_broadcast(P)).then_inc(gb_in, 16)
                else:
                    l, j = (n - 4) // 3, (n - 4) % 3
                    pool.dma_start(gain_bc[:], t["ln_g_2"][l, j].partition_broadcast(P)).then_inc(gb_in, 16)
                    pool.dma_start(bias_bc[:], t["ln_b_2"][l, j].partition_broadcast(P)).then_inc(gb_in, 16)

            def residual(n):
                pool.wait_ge(gb_in, 16 * (1 + 2 * (n - 3)))
                for b in range(NB):
                    pool.wait_ge(xn_ready, NB * n + b + 1)
                    ins = pool.tensor_tensor(resid[:, b, :], xn[:, b, :], gain_bc[:], ALU.mult)
                    if n > 3:
                        link(ins)
                        ins = pool.tensor_tensor(resid[:, b, :], resid[:, b, :], bias_bc[:], ALU.add)
                    ins.then_inc(resid_ready, 1)
                pool.wait_ge(resid_ready, NB * (n - 2))
                load_rows(n + 1)

            pool.dma_start(pos_i[:], t["positions"].rearrange("a (b p) -> p (a b)", p=P),
                           allow_slow_non_contiguous=True).then_inc(pos_in, 16)
            pool.dma_start(onehot, t["onehot"]).then_inc(rel_in, 16)
            pool.dma_start(rel_rows[0:32, :], t["rel_table_2"]).then_inc(rel_in, 16)
            pool.dma_start(sinks[:], t["sinks"].partition_broadcast(P)).then_inc(sink_ld, 16)
            load_rows(3)
            tile_copied(pool, ("rel",))
            pool.dma_start(rel_dram.ap(), rel_out.unsqueeze(1).to_broadcast([NH, P, N_REL])).then_inc(rel_stored, 16)
            for i in range(GATES):
                low_unit(("gate", i))
            for ft in range(KT):
                pool.wait_ge(merged_rounded, ft + 1)
                pool.tensor_tensor(hT_lo[:, ft, :], merge_tmp[:, ft % 2, 2], hT_hi[:, ft, :].bitcast(F32),
                                   ALU.subtract).then_inc(merged_ready, 1)
            residual(3)
            pool.dma_start(ws, t["sgu_w_s_2"][0].rearrange("g p s -> p g s")).then_inc(sgu_in, 16)
            pool.dma_start(sgu_g, t["sgu_ln_g_2"][0].partition_broadcast(P)).then_inc(sgu_in, 16)
            pool.dma_start(sgu_b, t["sgu_ln_b_2"][0].partition_broadcast(P)).then_inc(sgu_in, 16)
            pool.dma_start(bs_bc, t["sgu_b_s_2"][0].rearrange("g p -> (g p)").partition_broadcast(P)).then_inc(sgu_in, 16)
            pool.wait_ge(sgu_in, 16 * 4)
            pool.affine_select(out=ws, in_=ws, compare_op=ALU.is_ge, fill=0.0, base=0,
                               pattern=[[0, GROUPS], [-1, P]], channel_multiplier=1).then_inc(ws_ready, 1)
            residual(4)
            residual(5)
            for s in range(2):
                pool.dma_start(cw2[:, s], t["cmp_w2_2"][s].rearrange("(m p) d -> p m d", p=P)).then_inc(cw2_in, 16)
            pool.memset(hidc, 0.0)
            pool.memset(kcT, 0.0)
            pool.memset(pc, 0.0).then_inc(fills, 1)
            pool.memset(cx, 0.0).then_inc(fills, 1)
            residual(6)
            residual(7)
            pool.wait_ge(rel_stored, 16)
            pool.dma_start(rel, bass.AP(rel_dram, P - 1, [[N_REL - 1, P], [P * N_REL, NH], [1, S]])).then_inc(rel_back, 16)
            for i in range(WO_EARLY):
                low_unit(("wo", i))
            residual(8)
            pool.wait_ge(gb_in, 16 * 13)
            pool.wait_ge(xn_ready, NB * 9 + 1)
            link(pool.tensor_tensor(xn[:, 0, :], xn[:, 0, :], gain_bc[:], ALU.mult))
            pool.tensor_tensor(xn[:, 0, :], xn[:, 0, :], bias_bc[:], ALU.add).then_inc(out_ready[0], 1)


NAMES = ["x", "mem", "positions", "g_mix", "w_in", "b_gate", "sinks", "g_mem", "w_mem_kv", "w_proj_swa",
         "w_proj_dsa", "w_proj_mem", "w_out", "g_mlp", "w_mlp_in", "w_mlp_out", "g_final", "rel_table_2",
         "ln_g_2", "ln_b_2", "ffn_w1_2", "ffn_w3_2", "ffn_w2_2", "sgu_w_in_2", "sgu_ln_g_2", "sgu_ln_b_2",
         "sgu_w_s_2", "sgu_b_s_2", "sgu_w_out_2", "kv_w_2", "cmp_pe_2", "cmp_w1_2", "cmp_b1_2", "cmp_w2_2",
         "nsa_w_qg_2", "nsa_w_o_2"]


def shape_constants():
    q, k = np.arange(P)[:, None], np.arange(P)[None, :]
    consts = np.zeros((P, N_CONST), np.float32)
    consts[:, K_ID:K_ID + P] = np.eye(P)
    diag = np.where(k <= q, 0.0, NEG)
    consts[:, K_SWA:K_SWA + P] = np.where(k > q, 0.0, NEG)
    consts[:, K_SWA + P:K_SWA + S] = diag
    consts[:, K_CAUSAL + P:K_CAUSAL + S] = diag
    half = np.arange(32, dtype=np.float32)
    consts[:, K_FREQ:K_FREQ + 32] = np.power(np.float32(10000.0), -half / np.float32(32))
    consts[:, K_ROW] = np.arange(P) >= 31
    dist = 2 * P - 1 - np.arange(N_REL)
    n = np.maximum(dist, 1).astype(np.float32)
    large = 16 + (np.log(n / np.float32(16)) / np.float32(np.log(128 / 16)) * np.float32(16)).astype(np.int32)
    bucket = np.where(dist < 16, np.maximum(dist, 0), np.minimum(large, 31))
    onehot = np.zeros((33, N_REL), np.float32)
    onehot[np.where(dist >= 0, bucket, 32), np.arange(N_REL)] = 1.0
    return consts, onehot


def kernel(**inputs):
    import concourse.bacc as bacc
    from concourse.bass_utils import run_bass_kernel_spmd

    nc = bacc.Bacc("TRN2", target_bir_lowering=False, num_devices=1)
    arrays, t = {}, {}
    consts, onehot = shape_constants()
    given = [(n, inputs[n]) for n in NAMES] + [("consts", consts), ("onehot", onehot)]
    for name, a in given:
        a = np.ascontiguousarray(a)
        arrays[f"in_{name}"] = a
        t[name] = nc.dram_tensor(f"in_{name}", a.shape, mybir.dt.from_np(a.dtype), kind="ExternalInput").ap()
    out = nc.dram_tensor("out_0", (1, S, D), F32, kind="ExternalOutput").ap()
    two_blocks(nc, t, out)
    r = run_bass_kernel_spmd(nc, [arrays], core_ids=[0])
    return r.results[0]["out_0"]
```
